# Optimizing a Trainium2 kernel written in Bass

```python
import math
import jax, jax.numpy as jnp
from jax import lax
import numpy as np

D_MODEL = 2048
BATCH = 1
SEQ = 256
DEPTH = 2

MEM_LEN = 256
N_HEADS_TOTAL = 16
HEAD_DIM = D_MODEL // N_HEADS_TOTAL
N_DIFF = 4
N_SB = 6
N_FOX = N_HEADS_TOTAL - N_DIFF - N_SB
MIX_WIDTH = N_HEADS_TOTAL * HEAD_DIM
DIFF_QK_DIM = HEAD_DIM // 2
A_W = N_DIFF * HEAD_DIM
SB_W = N_SB * HEAD_DIM
FOX_W = N_FOX * HEAD_DIM
IN_COLS = 3 * A_W + 3 * SB_W + 3 * FOX_W + N_FOX
N_CROSS_HEADS = 4
CROSS_HEAD_DIM = D_MODEL // 16
CROSS_W = N_CROSS_HEADS * CROSS_HEAD_DIM
D_FF = -(-8 * D_MODEL // (3 * 256)) * 256
BLOCK_Q = 128
ROPE_THETA = 10000.0
EPS = 1e-6
NEG_INF = -1e30

kernel_name = "hymba_diff_stickbreak_fox_trunk"

def rms_norm(x, g):
    xf = x.astype(jnp.float32)
    y = xf * lax.rsqrt(jnp.mean(xf * xf, axis=-1, keepdims=True) + EPS)
    return (y * g.astype(jnp.float32)).astype(x.dtype)

def rope(x, positions):
    d = x.shape[-1]
    half = d // 2
    inv_freq = ROPE_THETA ** (-jnp.arange(half, dtype=jnp.float32) / half)
    ang = positions.astype(jnp.float32)[..., None] * inv_freq
    cos = jnp.cos(ang)[:, :, None, :]
    sin = jnp.sin(ang)[:, :, None, :]
    x1 = x[..., :half].astype(jnp.float32)
    x2 = x[..., half:].astype(jnp.float32)
    out = jnp.concatenate([x1 * cos - x2 * sin, x2 * cos + x1 * sin], axis=-1)
    return out.astype(x.dtype)

def split_heads(t, n, d):
    b, s, _ = t.shape
    return t.reshape(b, s, n, d).transpose(0, 2, 1, 3)

def merge_heads(t):
    b, h, s, d = t.shape
    return t.transpose(0, 2, 1, 3).reshape(b, s, h * d)

def block_size(s):
    return math.gcd(s, BLOCK_Q)

def to_blocks(t, bq):
    b, h, s = t.shape[:3]
    rest = t.shape[3:]
    t = t.reshape((b, h, s // bq, bq) + rest)
    return jnp.moveaxis(t, 2, 0)

def from_blocks(t):
    nb, b, h, bq, d = t.shape
    return t.transpose(1, 2, 0, 3, 4).reshape(b, h, nb * bq, d)

def query_block_index(s, bq):
    return jnp.arange(s, dtype=jnp.int32).reshape(s // bq, bq)

def diff_attention(q1, q2, k1, k2, v, lam):
    s = q1.shape[2]
    bq = block_size(s)
    scale = DIFF_QK_DIM ** -0.5
    k_idx = jnp.arange(s, dtype=jnp.int32)

    def one_block(args):
        qa, qb, qi = args
        causal = qi[:, None] >= k_idx[None, :]
        s1 = jnp.einsum('bhqd,bhkd->bhqk', qa, k1).astype(jnp.float32) * scale
        s2 = jnp.einsum('bhqd,bhkd->bhqk', qb, k2).astype(jnp.float32) * scale
        p1 = jax.nn.softmax(jnp.where(causal, s1, NEG_INF), axis=-1)
        p2 = jax.nn.softmax(jnp.where(causal, s2, NEG_INF), axis=-1)
        w = p1 - lam * p2
        return jnp.einsum('bhqk,bhkd->bhqd', w.astype(v.dtype), v)

    out = lax.map(one_block, (to_blocks(q1, bq), to_blocks(q2, bq), query_block_index(s, bq)))
    return from_blocks(out)

def stick_breaking_attention(q, k, v):
    s = q.shape[2]
    bq = block_size(s)
    scale = HEAD_DIM ** -0.5
    k_idx = jnp.arange(s, dtype=jnp.int32)

    def one_block(args):
        qb, qi = args
        z = jnp.einsum('bhqd,bhkd->bhqk', qb, k).astype(jnp.float32) * scale
        strict = qi[:, None] > k_idx[None, :]
        log_remain = jnp.where(strict, jax.nn.log_sigmoid(-z), 0.0)
        after = lax.cumsum(log_remain, axis=3, reverse=True) - log_remain
        w = jnp.where(strict, jnp.exp(jax.nn.log_sigmoid(z) + after), 0.0)
        return jnp.einsum('bhqk,bhkd->bhqd', w.astype(v.dtype), v)

    out = lax.map(one_block, (to_blocks(q, bq), query_block_index(s, bq)))
    return from_blocks(out)

def forgetting_attention(q, k, v, log_f):
    s = q.shape[2]
    bq = block_size(s)
    scale = HEAD_DIM ** -0.5
    k_idx = jnp.arange(s, dtype=jnp.int32)
    cum = lax.cumsum(log_f, axis=2)

    def one_block(args):
        qb, cq, qi = args
        logits = jnp.einsum('bhqd,bhkd->bhqk', qb, k).astype(jnp.float32) * scale
        logits = logits + (cq[:, :, :, None] - cum[:, :, None, :])
        causal = qi[:, None] >= k_idx[None, :]
        p = jax.nn.softmax(jnp.where(causal, logits, NEG_INF), axis=-1)
        return jnp.einsum('bhqk,bhkd->bhqd', p.astype(v.dtype), v)

    out = lax.map(one_block, (to_blocks(q, bq), to_blocks(cum, bq), query_block_index(s, bq)))
    return from_blocks(out)

def hybrid_mixer(h, positions, layer_idx, w_in, b_f, lam_q1, lam_k1, lam_q2, lam_k2,
                 g_diff_sub, g_sb_out, g_fox_out, w_out):
    b, s, _ = h.shape
    proj = h @ w_in
    sizes = [A_W, A_W, A_W, SB_W, SB_W, SB_W, FOX_W, FOX_W, FOX_W]
    points = [int(p) for p in np.cumsum(sizes)]
    qa, ka, va, qb, kb, vb, qc, kc, vc, fc = jnp.split(proj, points, axis=-1)

    qa = rope(qa.reshape(b, s, 2 * N_DIFF, DIFF_QK_DIM), positions).reshape(b, s, N_DIFF, 2, DIFF_QK_DIM)
    ka = rope(ka.reshape(b, s, 2 * N_DIFF, DIFF_QK_DIM), positions).reshape(b, s, N_DIFF, 2, DIFF_QK_DIM)
    q1 = qa[:, :, :, 0, :].transpose(0, 2, 1, 3)
    q2 = qa[:, :, :, 1, :].transpose(0, 2, 1, 3)
    k1 = ka[:, :, :, 0, :].transpose(0, 2, 1, 3)
    k2 = ka[:, :, :, 1, :].transpose(0, 2, 1, 3)
    lam_init = 0.8 - 0.6 * math.exp(-0.3 * layer_idx)
    lam = (jnp.exp(jnp.sum(lam_q1.astype(jnp.float32) * lam_k1.astype(jnp.float32)))
           - jnp.exp(jnp.sum(lam_q2.astype(jnp.float32) * lam_k2.astype(jnp.float32)))) + lam_init
    oa = diff_attention(q1, q2, k1, k2, split_heads(va, N_DIFF, HEAD_DIM), lam)
    oa = merge_heads(rms_norm(oa, g_diff_sub) * (1.0 - lam_init))

    ob = stick_breaking_attention(split_heads(qb, N_SB, HEAD_DIM), split_heads(kb, N_SB, HEAD_DIM),
                                  split_heads(vb, N_SB, HEAD_DIM))
    ob = rms_norm(merge_heads(ob), g_sb_out)

    log_f = jax.nn.log_sigmoid((fc + b_f).astype(jnp.float32)).transpose(0, 2, 1)
    oc = forgetting_attention(split_heads(qc, N_FOX, HEAD_DIM), split_heads(kc, N_FOX, HEAD_DIM),
                              split_heads(vc, N_FOX, HEAD_DIM), log_f)
    oc = rms_norm(merge_heads(oc), g_fox_out)

    merged = jnp.concatenate([oa, ob, oc], axis=-1)
    return merged @ w_out

def memory_cross_attention(h, mem_n, w_cq, w_ckv, w_co):
    b, s, _ = h.shape
    m = mem_n.shape[1]
    q = (h @ w_cq).reshape(b, s, N_CROSS_HEADS, CROSS_HEAD_DIM)
    kv = mem_n @ w_ckv
    k = kv[:, :, :CROSS_W].reshape(b, m, N_CROSS_HEADS, CROSS_HEAD_DIM)
    v = kv[:, :, CROSS_W:].reshape(b, m, N_CROSS_HEADS, CROSS_HEAD_DIM)
    logits = jnp.einsum('bqhd,bmhd->bhqm', q, k).astype(jnp.float32) * CROSS_HEAD_DIM ** -0.5
    p = jax.nn.softmax(logits, axis=-1)
    o = jnp.einsum('bhqm,bmhd->bqhd', p.astype(v.dtype), v).reshape(b, s, CROSS_W)
    return o @ w_co

def swiglu(h, w_gate, w_up, w_down):
    return (jax.nn.silu(h @ w_gate) * (h @ w_up)) @ w_down

def setup_inputs(seed: int = 0) -> dict:
    key = jax.random.key(seed)
    ks = jax.random.split(key, 32)
    f32 = jnp.float32

    def dense(k, shape, fan_in):
        return jax.random.normal(k, shape, f32) * fan_in ** -0.5

    def gain(k, shape):
        return 1.0 + 0.05 * jax.random.normal(k, shape, f32)

    x = jax.random.normal(ks[0], (BATCH, SEQ, D_MODEL), f32)
    mem = jax.random.normal(ks[1], (BATCH, MEM_LEN, D_MODEL), f32)
    offsets = jax.random.randint(ks[2], (BATCH, 1), 0, SEQ, dtype=jnp.int32)
    positions = offsets + jnp.arange(SEQ, dtype=jnp.int32)[None, :]
    return {
        "x": x,
        "mem": mem,
        "positions": positions,
        "g_mix_pre": gain(ks[3], (DEPTH, D_MODEL)),
        "g_mix_post": gain(ks[4], (DEPTH, D_MODEL)),
        "w_in": dense(ks[5], (DEPTH, D_MODEL, IN_COLS), D_MODEL),
        "b_f": 2.0 + 0.5 * jax.random.normal(ks[6], (DEPTH, N_FOX), f32),
        "lam_q1": 0.1 * jax.random.normal(ks[7], (DEPTH, DIFF_QK_DIM), f32),
        "lam_k1": 0.1 * jax.random.normal(ks[8], (DEPTH, DIFF_QK_DIM), f32),
        "lam_q2": 0.1 * jax.random.normal(ks[9], (DEPTH, DIFF_QK_DIM), f32),
        "lam_k2": 0.1 * jax.random.normal(ks[10], (DEPTH, DIFF_QK_DIM), f32),
        "g_diff_sub": gain(ks[11], (DEPTH, HEAD_DIM)),
        "g_sb_out": gain(ks[12], (DEPTH, SB_W)),
        "g_fox_out": gain(ks[13], (DEPTH, FOX_W)),
        "w_out": dense(ks[14], (DEPTH, MIX_WIDTH, D_MODEL), MIX_WIDTH),
        "g_x_pre": gain(ks[15], (DEPTH, D_MODEL)),
        "g_x_post": gain(ks[16], (DEPTH, D_MODEL)),
        "g_mem": gain(ks[17], (DEPTH, D_MODEL)),
        "w_cq": dense(ks[18], (DEPTH, D_MODEL, CROSS_W), D_MODEL),
        "w_ckv": dense(ks[19], (DEPTH, D_MODEL, 2 * CROSS_W), D_MODEL),
        "w_co": dense(ks[20], (DEPTH, CROSS_W, D_MODEL), CROSS_W),
        "g_ffn_pre": gain(ks[21], (DEPTH, D_MODEL)),
        "g_ffn_post": gain(ks[22], (DEPTH, D_MODEL)),
        "w_gate": dense(ks[23], (DEPTH, D_MODEL, D_FF), D_MODEL),
        "w_up": dense(ks[24], (DEPTH, D_MODEL, D_FF), D_MODEL),
        "w_down": dense(ks[25], (DEPTH, D_FF, D_MODEL), D_FF),
    }

def reference(x, mem, positions, g_mix_pre, g_mix_post, w_in, b_f, lam_q1, lam_k1, lam_q2, lam_k2,
              g_diff_sub, g_sb_out, g_fox_out, w_out, g_x_pre, g_x_post, g_mem, w_cq, w_ckv, w_co,
              g_ffn_pre, g_ffn_post, w_gate, w_up, w_down):
    for l in range(DEPTH):
        h = rms_norm(x, g_mix_pre[l])
        y = hybrid_mixer(h, positions, l, w_in[l], b_f[l], lam_q1[l], lam_k1[l], lam_q2[l], lam_k2[l],
                         g_diff_sub[l], g_sb_out[l], g_fox_out[l], w_out[l])
        x = x + rms_norm(y, g_mix_post[l])
        h = rms_norm(x, g_x_pre[l])
        mem_n = rms_norm(mem, g_mem[l])
        y = memory_cross_attention(h, mem_n, w_cq[l], w_ckv[l], w_co[l])
        x = x + rms_norm(y, g_x_post[l])
        h = rms_norm(x, g_ffn_pre[l])
        y = swiglu(h, w_gate[l], w_up[l], w_down[l])
        x = x + rms_norm(y, g_ffn_post[l])
    return x


_drawn_inputs = setup_inputs


def setup_inputs(seed=0):
    import zlib

    import numpy as np

    out = dict(_drawn_inputs(seed))
    spreads = {}
    factors = {'lam_q2': 7.443, 'g_diff_sub': 2.683}
    for name, (base, spread) in spreads.items():
        noise = np.random.default_rng([zlib.crc32(name.encode()), seed]).standard_normal(out[name].shape)
        drawn = base * np.exp(spread * noise) if base else spread * noise
        out[name] = __import__('jax').numpy.asarray(drawn.astype(out[name].dtype))
    for name, factor in factors.items():
        out[name] = (out[name] * factor).astype(out[name].dtype)
    return out
```

```python
import math
from contextlib import ExitStack

import numpy as np

import concourse.bass as bass
from concourse import mybir

ALU = mybir.AluOpType
ACT = mybir.ActivationFunctionType
F32 = mybir.dt.float32
F32R = mybir.dt.float32r
BF16 = mybir.dt.bfloat16
I32 = mybir.dt.int32
AX_X = mybir.AxisListType.X

P = 128
NT = 2
EPS = 1e-6
NEG = -1e30
ROPE_THETA = 10000.0
N_DIFF, N_SB, N_FOX = 4, 6, 6
HD = 128
ROT = 32
PAIR_W = 3 * 2 * HD
WIDE = 1024
PAIRS_A, PAIRS_B, PAIRS_C = N_DIFF // 2, N_SB // 2, N_FOX // 2
PAIRS = PAIRS_A + PAIRS_B + PAIRS_C

RING = 4

C_ID, C_CAUSAL, C_STRICT, C_TRI, C_ONES, C_FREQ = 0, 128, 512, 896, 1024, 1152
C_W = C_FREQ + ROT


def trunk(nc, x, mem, positions, g_mix_pre, g_mix_post, w_in, b_f, lam_q1, lam_k1, lam_q2, lam_k2,
          g_diff_sub, g_sb_out, g_fox_out, w_out, g_x_pre, g_x_post, g_mem, w_cq, w_ckv, w_co,
          g_ffn_pre, g_ffn_post, w_gate, w_up, w_down, consts, out):
    DEPTH, D = g_mix_pre.shape
    DFF = w_gate.shape[2]
    KT = D // P
    FB = DFF // 512
    CW = w_cq.shape[2]
    NCH = CW // HD
    COK = CW // P
    lam_init = [0.8 - 0.6 * math.exp(-0.3 * n) for n in range(DEPTH)]
    G = 4 * (FB)
    assert D == 2048 and G == DFF // P and FB % 2 == 1 and CW == 512

    S_CKV, S_OUT = PAIRS, PAIRS + 1
    S_CQ, S_CO = S_OUT + 2, S_OUT + 3
    S_FFN, S_DOWN = S_CO + 2, S_CO + 2 + FB
    SETS = S_DOWN + 2
    K_CKV = PAIRS * KT
    K_OUT = K_CKV + KT
    K_CQ = K_OUT + 2 * KT
    K_CO = K_CQ + KT // 2
    K_FFN = K_CO + 2 * COK
    K_DOWN = K_FFN + FB * KT
    CHUNKS = K_DOWN + 2 * G
    T_X, T_MEM, T_MIX, T_CQ, T_CO, T_FFN, GROUPS = 0, 8, 16, 24, 32, 34, 42
    G_MIX, G_X, G_FFN, G_MEM, G_MERGED, GAINS = 0, KT, 2 * KT, 3 * KT, 4 * KT, 5 * KT
    Q_X, Q_MEM, Q_A, Q_B, Q_C, Q_OUT, Q_X2, Q_CO, Q_X3, Q_DOWN, SQUARES = \
        0, 2, 4, 12, 14, 16, 24, 26, 34, 36, 44

    with ExitStack() as ctx:
        def sb(name, shape, dt=F32):
            return ctx.enter_context(nc.sbuf_tensor(name, shape, dt))

        def sem(name):
            return ctx.enter_context(nc.semaphore(name))

        cst = sb("cst", [P, C_W])
        ident = cst[:, C_ID:C_ID + P]
        causal = cst[:, C_CAUSAL:C_CAUSAL + 3 * P]
        strict = cst[:, C_STRICT:C_STRICT + 3 * P]
        tri = cst[:, C_TRI:C_TRI + P]
        ones = cst[:, C_ONES:C_ONES + P]
        freq = cst[:, C_FREQ:C_FREQ + ROT]
        xs = sb("xs", [P, NT, D])
        raw = sb("raw", [P, RING, WIDE])
        wh = sb("wh", [P, RING, WIDE], F32R)
        wl = sb("wl", [P, RING, WIDE], F32R)
        xTh = sb("xTh", [P, KT, NT * P], F32R)
        xTl = sb("xTl", [P, KT, NT * P], F32R)
        pj = sb("pj", [P, NT, PAIR_W])
        mg = sb("mg", [P, NT, D])
        with ExitStack() as mixer:
            memTh = mixer.enter_context(nc.sbuf_tensor("memTh", [P, KT, NT * P], F32R))
            memTl = mixer.enter_context(nc.sbuf_tensor("memTl", [P, KT, NT * P], F32R))
            kv = mixer.enter_context(nc.sbuf_tensor("kv", [P, NT, WIDE], F32))
        hidT = sb("hidT", [P, G, NT * P])
        gbc = sb("gbc", [P, D])
        Z = sb("Z", [P, 2, 512])
        E = sb("E", [P, 2, 512])
        R = sb("R", [P, 2, 512])
        pT = sb("pT", [P, 2, 512])
        qkT = sb("qkT", [P, 2, 512])
        nlb = sb("nlb", [P, 2, NT, P])
        junk = qkT[:, :, :].rearrange("p a n -> p (a n)").bitcast(BF16)
        gT = sb("gT", [P, DEPTH, GAINS])
        grow = sb("grow", [P, DEPTH, P])
        wfr = sb("wfr", [P, DEPTH, KT, N_FOX])
        wfh = sb("wfh", [P, KT, N_FOX], F32R)
        wfl = sb("wfl", [P, KT, N_FOX], F32R)
        bfb = sb("bfb", [P, DEPTH, N_FOX])
        fz = sb("fz", [P, NT, N_FOX])
        fe = sb("fe", [P, NT, N_FOX])
        fs = sb("fs", [P, NT, N_FOX])
        nlf = sb("nlf", [P, N_FOX, NT])
        cum = sb("cum", [P, N_FOX, NT])
        cumq = sb("cumq", [P, 2, NT])
        posi = sb("posi", [P, NT], I32)
        posf = sb("posf", [P, NT])
        trig = sb("trig", [P, 4, NT, ROT])
        cosb = sb("cosb", [P, NT, ROT])
        sinb = sb("sinb", [P, NT, ROT])
        lamr = sb("lamr", [P, 4, DEPTH * 64])
        lamd = sb("lamd", [P, 2, DEPTH])
        nlam = sb("nlam", [P, DEPTH])
        mhalf = sb("mhalf", [P, 16])
        eps = sb("eps", [P, 16])
        inv_w = sb("inv_w", [P, 14])
        IW_D, IW_A, IW_C = 0, 2, 12
        ssy = sb("ssy", [P, NT, 4])
        ssy2 = sb("ssy2", [P, NT])
        ssx = sb("ssx", [P, NT])
        ssm = sb("ssm", [P, NT])
        ssh = sb("ssh", [P, 12])
        msx = sb("msx", [P, 9, 12])
        rx = sb("rx", [P, NT])
        rm = sb("rm", [P, NT])
        ry = sb("ry", [P, NT])
        rh = sb("rh", [P, 12])
        nmax = sb("nmax", [P, 4, NT])
        rsum = sb("rsum", [P, 4, NT])
        rinv = sb("rinv", [P, 4, NT])

        acc = ctx.enter_context(nc.psum_tensor("acc", [P, 4, 512], F32))
        aux = ctx.enter_context(nc.psum_tensor("aux", [P, 4, 512], F32))

        init_dma = sem("init_dma")
        raw_full = [sem(f"raw_full{s}") for s in range(RING)]
        wh_ready = sem("wh_ready")
        wl_ready = sem("wl_ready")
        w_free = sem("w_free")
        acc_done = sem("acc_done")
        acc_free = [sem(f"acc_free{b}") for b in range(4)]
        tp_done = sem("tp_done")
        tp_gain = sem("tp_gain")
        tp_high = sem("tp_high")
        xT_ready = sem("xT_ready")
        mem_full = sem("mem_full")
        gbc_full = sem("gbc_full")
        x_upd = sem("x_upd")
        sq_done = sem("sq_done")
        ssy_ready = sem("ssy_ready")
        ms = sem("ms")
        rx_ready = sem("rx_ready")
        rm_ready = sem("rm_ready")
        ry_ready = sem("ry_ready")
        rh_ready = sem("rh_ready")
        mg_ready = sem("mg_ready")
        f_done = sem("f_done")
        f_step = sem("f_step")
        f_act = sem("f_act")
        cum_done = sem("cum_done")
        cum_ready = sem("cum_ready")
        fox_ready = sem("fox_ready")
        rope_step = sem("rope_step")
        mem_low = sem("mem_low")
        qkT_done = sem("qkT_done")
        qkT_act = sem("qkT_act")
        qkT_dve = sem("qkT_dve")
        s_done = sem("s_done")
        dve_att = sem("dve_att")
        act_att = sem("act_att")
        pT_done = sem("pT_done")
        pT_act = sem("pT_act")
        pT_dve = sem("pT_dve")
        o_done = sem("o_done")
        o_read = sem("o_read")
        x_qT = sem("x_qT")
        x_kT = sem("x_kT")
        x_tp = sem("x_tp")
        x_s = sem("x_s")
        x_max = sem("x_max")
        x_exp = sem("x_exp")
        x_inv = sem("x_inv")
        x_pT = sem("x_pT")
        x_pTr = sem("x_pTr")
        x_o = sem("x_o")
        x_or = sem("x_or")
        silu_done = sem("silu_done")
        hT_done = sem("hT_done")
        hT_act = sem("hT_act")
        hT_dve = sem("hT_dve")
        st_high = sem("st_high")
        st_ready = sem("st_ready")
        boot = sem("boot")
        boot_dve = sem("boot_dve")
        boot_act = sem("boot_act")
        boot_pe = sem("boot_pe")
        boot_pool = sem("boot_pool")
        stored = sem("stored")

        DA, DB, DC = 24, 10, 10
        AA, AB, AC = 8, 8, 4
        DVE_ATT = PAIRS_A * DA + PAIRS_B * DB + PAIRS_C * DC
        ACT_ATT = PAIRS_A * AA + PAIRS_B * AB + PAIRS_C * AC
        MAPS = PAIRS_A * 4 + (PAIRS_B + PAIRS_C) * 2

        w_in_v = [
            w_in[:, :, 0:3 * N_DIFF * HD],
            w_in[:, :, 3 * N_DIFF * HD:3 * (N_DIFF + N_SB) * HD],
            w_in[:, :, 3 * (N_DIFF + N_SB) * HD:3 * (N_DIFF + N_SB + N_FOX) * HD],
        ]
        w_in_v = [v.rearrange("l (k p) (s c) -> l k p s c", p=P, s=3) for v in w_in_v]
        w_f_v = w_in[:, :, 3 * (N_DIFF + N_SB + N_FOX) * HD:].rearrange("l (k p) c -> p l k c", p=P)
        w_out_v = w_out.rearrange("l (k p) n -> l k p n", p=P)
        w_ckv_v = w_ckv.rearrange("l (k p) n -> l k p n", p=P)
        w_cq_v = w_cq.rearrange("l (k j p) n -> l k p j n", j=2, p=P)
        w_co_v = w_co.rearrange("l (k p) n -> l k p n", p=P)
        w_gate_v = w_gate.rearrange("l (k p) n -> l k p n", p=P)
        w_up_v = w_up.rearrange("l (k p) n -> l k p n", p=P)
        w_down_v = w_down.rearrange("l (k p) n -> l k p n", p=P)
        x_v = x.rearrange("b (t p) d -> p (b t) d", p=P)
        mem_v = mem.rearrange("b (t p) d -> p (b t) d", p=P)
        out_v = out.rearrange("b (t p) d -> p (b t) d", p=P)

        block = ctx.enter_context(nc.Block())

        def lows(l, n):
            return l * (GROUPS - 8) + ((n if n < T_MEM else n - 8) + 1)

        def last_chunk(s):
            if s < S_CQ:
                return KT * (s + 1) - 1
            if s < S_FFN:
                return (K_CO, K_CO + COK, K_FFN)[s - S_CQ] - 1
            if s < S_DOWN:
                return K_FFN + (s - S_FFN + 1) * KT - 1
            return K_DOWN + (s - S_DOWN + 1) * G - 1

        def wait_acc(eng, l, sets, s, b):
            if b < 3:
                eng.wait_ge(acc_done, l * (3 * SETS) + sets * 3 + (3 * s + b + 1))
            else:
                eng.wait_ge(w_free, l * CHUNKS + sets * KT + (last_chunk(s) + 1 + RING))

        def attention(group, l, i):
            pb = (0, PAIRS_A, PAIRS_A + PAIRS_B)[group]
            dve0 = (0, PAIRS_A * DA, PAIRS_A * DA + PAIRS_B * DB)[group]
            act0 = (0, PAIRS_A * AA, PAIRS_A * AA + PAIRS_B * AB)[group]
            map0 = (0, PAIRS_A * 4, PAIRS_A * 4 + PAIRS_B * 2)[group]
            d, a, m = ((DA, AA, 4), (DB, AB, 2), (DC, AC, 2))[group]

            def head(n):
                return l * (2 * PAIRS) + i * 2 + (2 * pb + n)

            def dve(n):
                return l * DVE_ATT + i * d + (dve0 + n)

            def act(n):
                return l * ACT_ATT + i * a + (act0 + n)

            def scores(n):
                return l * MAPS + i * m + (map0 + n)

            def one(n):
                return l * PAIRS + i + (pb + n)
            return head, dve, act, scores, one

        @block.sync
        def _(sp):
            def first(dst, src):
                sp.dma_start(dst, src).then_inc(init_dma, 16)
            first(cst[:, :], consts)
            first(xs[:, :, :], x_v)
            with nc.allow_non_contiguous_dma(reason="small parameters, once"):
                first(posi[:, :], positions.rearrange("b (t p) -> p (b t)", p=P))
                for at, g in ((G_MIX, g_mix_pre), (G_X, g_x_pre), (G_FFN, g_ffn_pre), (G_MEM, g_mem)):
                    first(grow[at:at + KT, :, :], g.rearrange("l (k p) -> k l p", p=P))
                for h in range(N_DIFF):
                    first(grow[G_MERGED + h:G_MERGED + h + 1, :, :], g_diff_sub.unsqueeze(0))
                first(grow[G_MERGED + N_DIFF:G_MERGED + N_DIFF + N_SB, :, :],
                      g_sb_out.rearrange("l (k p) -> k l p", p=P))
                first(grow[G_MERGED + N_DIFF + N_SB:GAINS, :, :],
                      g_fox_out.rearrange("l (k p) -> k l p", p=P))
                first(bfb[:, :, :], b_f.partition_broadcast(P))
                for n, v in enumerate((lam_q1, lam_k1, lam_q2, lam_k2)):
                    first(lamr[:, n, :], v.rearrange("l d -> (l d)").partition_broadcast(P))
                for n in range(DEPTH):
                    first(wfr[:, n, :, :], w_f_v[:, n, :, :])

            with sp.Fori(0, DEPTH) as l:
                def chunk(ahead, c, dsts, srcs):
                    sp.wait_ge(wl_ready, l * CHUNKS + ahead + (c + 1))
                    for d, v in zip(dsts, srcs):
                        sp.dma_start(d, v).then_inc(raw_full[c % RING], 32 // len(srcs))

                def slot(c):
                    return raw[:, c % RING, :]

                def pair_chunk(group, base, ahead, col, k):
                    chunk(ahead, base + k, [slot(k)[:, 0:PAIR_W].rearrange("p (s c) -> p s c", s=3)],
                          [w_in_v[group][l, k, :, :, bass.ds(col, 2 * HD)]])

                for k in range(KT):
                    if k == RING:
                        sp.wait_ge(x_upd, l * 24 + 1)
                        sp.dma_start(mg[:, :, :], mem_v).then_inc(mem_full, 16)
                        sp.dma_start(gbc[:, :], g_mix_post[l, :].partition_broadcast(P))\
                          .then_inc(gbc_full, 16)
                    pair_chunk(0, 0, 0, 0, k)
                for group, start, n in ((0, 1, PAIRS_A), (1, 0, PAIRS_B), (2, 0, PAIRS_C)):
                    pb = (0, PAIRS_A, PAIRS_A + PAIRS_B)[group]
                    with sp.Fori(start, n) as i:
                        for k in range(KT):
                            pair_chunk(group, pb * KT, i * KT, i * (2 * HD), k)
                for k in range(KT):
                    chunk(0, K_CKV + k, [slot(k)], [w_ckv_v[l, k]])
                with sp.Fori(0, 2) as s:
                    for k in range(KT):
                        chunk(s * KT, K_OUT + k, [slot(k)], [w_out_v[l, k, :, bass.ds(s * WIDE, WIDE)]])
                for k in range(KT // 2):
                    if k == KT // 2 - 2:
                        sp.wait_ge(x_upd, l * 24 + 9)
                        sp.dma_start(gbc[:, :], g_x_post[l, :].partition_broadcast(P))\
                          .then_inc(gbc_full, 16)
                    chunk(0, K_CQ + k, [slot(k).rearrange("p (j n) -> p j n", j=2)], [w_cq_v[l, k]])
                for s in range(2):
                    for k in range(COK):
                        chunk(0, K_CO + s * COK + k, [slot(k)], [w_co_v[l, k, :, s * WIDE:(s + 1) * WIDE]])
                with sp.Fori(0, FB) as j:
                    for k in range(KT):
                        chunk(j * KT, K_FFN + k, [slot(k)[:, 0:512], slot(k)[:, 512:1024]],
                              [w_gate_v[l, k, :, bass.ds(j * 512, 512)],
                               w_up_v[l, k, :, bass.ds(j * 512, 512)]])
                sp.wait_ge(x_upd, l * 24 + 17)
                sp.dma_start(gbc[:, :], g_ffn_post[l, :].partition_broadcast(P)).then_inc(gbc_full, 16)
                for s in range(2):
                    half = slice(s * WIDE, (s + 1) * WIDE)
                    for k in range(4):
                        chunk(0, K_DOWN + s * G + k, [slot(k)], [w_down_v[l, k, :, half]])
                    with sp.Fori(0, FB // 2) as g:
                        for k in range(8):
                            chunk(g * 8, K_DOWN + s * G + 4 + k, [slot(k)],
                                  [w_down_v[l, g * 8 + (4 + k), :, half]])
            sp.wait_ge(x_upd, DEPTH * 24 + 1)
            sp.dma_start(out_v, xs[:, :, :]).then_inc(stored, 16)
            sp.wait_ge(stored, 16)

        N_INIT = 3 + 4 + N_DIFF + 2 + 1 + 4 + DEPTH

        @block.tensor
        def _(pe):
            pe.wait_ge(init_dma, 16 * N_INIT)
            for n in range(DEPTH):
                pe.transpose(aux[:, n, 0:GAINS], grow[0:GAINS, n, :], ident[0:GAINS, 0:GAINS])\
                  .then_inc(boot_pe, 1)

            with pe.Fori(0, DEPTH) as l:
                def stream(ahead, c0, set_ahead, set0, n, width, lhs, hooks=None, start=True,
                           stop=True, subs=1, before=None):
                    for k in range(n):
                        if hooks and k in hooks:
                            hooks[k]()
                        if before:
                            before(k)
                        slot = (c0 + k) % RING
                        pe.wait_ge(wl_ready, l * CHUNKS + ahead + (c0 + k + 1 + RING))
                        for b in range(4):
                            if start and k == 0:
                                pe.wait_ge(acc_free[b], l * SETS + set_ahead + (set0 + 1))
                            a, t = b // 2, b % 2
                            for j in range(subs):
                                hi, lo = lhs(k * subs + j)
                                cols = slice(j * 512 + a * width, j * 512 + (a + 1) * width)
                                tok = slice(t * P, (t + 1) * P)
                                o = acc[:, b, 0:width]
                                pe.matmul(o, hi[:, tok], wh[:, slot, cols],
                                          start=start and k == 0 and j == 0, stop=False)
                                pe.matmul(o, hi[:, tok], wl[:, slot, cols], start=False, stop=False)
                                mm = pe.matmul(o, lo[:, tok], wh[:, slot, cols], start=False,
                                               stop=stop and k == n - 1 and j == subs - 1)
                            if stop and k == n - 1 and b < 3:
                                mm.then_inc(acc_done, 1)
                        mm.then_inc(w_free, 1)
                    if hooks and n in hooks:
                        hooks[n]()

                def x_lhs(k):
                    return xTh[:, k, :], xTl[:, k, :]

                def mem_lhs(k):
                    return memTh[:, k, :], memTl[:, k, :]

                def group(n, src, ready=None, back=4, bank=None):
                    if ready is not None:
                        pe.wait_ge(*ready)
                    if n >= back:
                        pe.wait_ge(tp_gain, l * GROUPS + (n - back + 1))
                    for j in range(4):
                        tr = pe.transpose(aux[:, n % 4 if bank is None else bank, j * P:(j + 1) * P],
                                          src[:, j * P:(j + 1) * P], ident)
                    tr.then_inc(tp_done, 1)

                def cols(g):
                    return g % 2, slice(g // 2 * 512, (g // 2 + 1) * 512)

                def wait_x(k, t0, per):
                    if k % (4 // per) == 0:
                        pe.wait_ge(xT_ready, lows(l, t0 + 2 * (k * per // 4) + 1))

                def x_groups(t0, lo, hi, upd):
                    for g in range(lo, hi):
                        t, c = cols(g)
                        group(t0 + g, xs[:, t, c], (x_upd, l * 24 + upd(g)))

                def att_transpose(group_, i):
                    head, dve, act, scores, one = attention(group_, l, i)
                    if group_ == 0:
                        pe.wait_ge(rope_step, l * (10 * PAIRS_A) + i * 10 + 10)
                    for b in range(4):
                        pe.wait_ge(acc_free[b], l * SETS + i + ((0, PAIRS_A, PAIRS_A + PAIRS_B)[group_] + 2))
                    for h in range(2):
                        for j, (t, at) in enumerate(((0, h), (1, h), (0, 2 + h), (1, 2 + h))):
                            tr = pe.transpose(aux[:, (0, 3)[h], j * P:(j + 1) * P],
                                              pj[:, t, at * HD:(at + 1) * HD], ident)
                        tr.then_inc(qkT_done, 1)

                def att_scores(group_, i, h):
                    head, dve, act, scores, one = attention(group_, l, i)
                    pe.wait_ge((qkT_act, qkT_dve)[h], one(1))
                    if group_ == 0 and h == 1:
                        pe.wait_ge(dve_att, dve(2))
                    if group_ == 2 and h == 0:
                        pe.wait_ge(fox_ready, l * PAIRS_C + i + 1)
                    maps = 2 if group_ == 0 else 1
                    for m in range(maps):
                        rows = slice(64 * m, 64 * m + 64) if group_ == 0 else slice(0, P)
                        s = aux[:, 1 + (m if group_ == 0 else h), :]
                        q, k = qkT[rows, h, 0:256], qkT[rows, h, 256:512]
                        last = group_ != 2
                        mm = pe.matmul(s[:, 0:P], q[:, 0:P], k[:, 0:P], start=True, stop=last)
                        if not last:
                            pe.matmul(s[:, 0:P], nlb[:, h, 0, :], tri, start=False, stop=True)
                        mm = pe.matmul(s[:, P:3 * P], q[:, P:2 * P], k[:, :], start=True, stop=last)
                        if not last:
                            pe.matmul(s[:, P:2 * P], nlb[:, h, 0, :], tri, start=False, stop=False)
                            pe.matmul(s[:, 2 * P:3 * P], nlb[:, h, 0, :], ones, start=False, stop=False)
                            mm = pe.matmul(s[:, 2 * P:3 * P], nlb[:, h, 1, :], tri, start=False, stop=True)
                        mm.then_inc(s_done, 1)

                def att_weights(group_, i, h):
                    head, dve, act, scores, one = attention(group_, l, i)
                    if group_ == 0:
                        pe.wait_ge(dve_att, dve(12 * (h + 1)))
                    else:
                        pe.wait_ge(act_att, act(7 + h if group_ == 1 else 2 * h + 2))
                    src = (R if group_ == 0 else E)[:, h, :]
                    for j in range(3):
                        tr = pe.transpose(aux[:, (0, 2)[h], j * P:(j + 1) * P], src[:, j * P:(j + 1) * P], ident)
                    tr.then_inc(pT_done, 1)

                def att_values(group_, i, h):
                    head, dve, act, scores, one = attention(group_, l, i)
                    pe.wait_ge((pT_act, pT_dve)[h], one(1))
                    v = [pj[:, t, (4 + h) * HD:(5 + h) * HD] for t in range(NT)]
                    o = aux[:, 3, h * 256:(h + 1) * 256]
                    pe.matmul(o[:, 0:P], pT[:, h, 0:P], v[0], start=True, stop=True)
                    pe.matmul(o[:, P:2 * P], pT[:, h, P:2 * P], v[0], start=True, stop=False)
                    pe.matmul(o[:, P:2 * P], pT[:, h, 2 * P:3 * P], v[1], start=False, stop=True)\
                      .then_inc(o_done, 1)

                def both(f, g_, i):
                    f(g_, i, 0)
                    f(g_, i, 1)

                def att_hooks(g_, i):
                    if g_ == 0:
                        return {4: lambda: att_transpose(0, i), 6: lambda: att_scores(0, i, 0),
                                8: lambda: att_scores(0, i, 1), 10: lambda: att_weights(0, i, 0),
                                11: lambda: att_values(0, i, 0), 12: lambda: att_weights(0, i, 1),
                                13: lambda: att_values(0, i, 1)}
                    return {1: lambda: att_transpose(g_, i), 3: lambda: both(att_scores, g_, i),
                            9: lambda: both(att_weights, g_, i), 11: lambda: both(att_values, g_, i)}

                x_groups(T_X, 0, 4, lambda g: 1)

                def gate():
                    pe.wait_ge(f_step, l * 5 + 1)
                    for t in range(NT):
                        o = aux[:, 3, t * 8:t * 8 + N_FOX]
                        tok = slice(t * P, (t + 1) * P)
                        for k in range(KT):
                            pe.matmul(o, xTh[:, k, tok], wfh[:, k, :], start=k == 0, stop=False)
                            pe.matmul(o, xTh[:, k, tok], wfl[:, k, :], start=False, stop=False)
                            mm = pe.matmul(o, xTl[:, k, tok], wfh[:, k, :], start=False, stop=k == KT - 1)
                    mm.then_inc(f_done, 1)

                def cumulate():
                    pe.wait_ge(f_step, l * 5 + 5)
                    o = aux[:, 2, :]
                    pe.matmul(o[:, 0:N_FOX], tri, nlf[:, :, 0], start=True, stop=True)
                    pe.matmul(o[:, 8:8 + N_FOX], ones, nlf[:, :, 0], start=True, stop=False)
                    pe.matmul(o[:, 8:8 + N_FOX], tri, nlf[:, :, 1], start=False, stop=True)\
                      .then_inc(cum_done, 1)

                def mem_groups(lo, hi):
                    for g in range(lo, hi):
                        t, c = cols(g)
                        group(T_MEM + g, mg[:, t, c], (mem_full, l * 16 + 16), back=2 if g > 1 else 1,
                              bank=g % 2)
                stream(0, 0, 0, 0, KT, 384, x_lhs, {
                    2: lambda: x_groups(T_X, 4, 6, lambda g: 1), 4: lambda: x_groups(T_X, 6, 8, lambda g: 1),
                    8: gate, 9: lambda: mem_groups(0, 2), 10: lambda: mem_groups(2, 4),
                    11: lambda: mem_groups(4, 6), 12: lambda: mem_groups(6, 8), 13: cumulate,
                }, before=lambda k: wait_x(k, T_X, 1) if k < 13 else None)

                for g_, n in ((0, PAIRS_A), (1, PAIRS_B), (2, PAIRS_C - 1)):
                    pb = (0, PAIRS_A, PAIRS_A + PAIRS_B)[g_]
                    with pe.Fori(0, n) as i:
                        stream(i * KT, (pb + 1) * KT, i, pb + 1, KT, 384, x_lhs, att_hooks(g_, i))

                def mix_groups(lo, hi):
                    for g in range(lo, hi):
                        t, c = cols(g)
                        group(T_MIX + g, mg[:, t, c],
                              (mg_ready, l * 5 + (1 if g < 2 else 3 if g < 4 else 5)),
                              back=4 if g else 1)
                pe.wait_ge(mem_low, l * 8 + 8)
                hooks = att_hooks(2, PAIRS_C - 1)
                stream(0, K_CKV, 0, S_CKV, KT, 512, mem_lhs, hooks)

                mix_groups(0, 4)
                stream(0, K_OUT, 0, S_OUT, KT, 512, x_lhs,
                       {3: lambda: mix_groups(4, 6), 5: lambda: mix_groups(6, 8)},
                       before=lambda k: wait_x(k, T_MIX, 1))
                stream(0, K_OUT + KT, 0, S_OUT + 1, KT, 512, x_lhs)

                x_groups(T_CQ, 0, 4, lambda g: g + 2)
                stream(0, K_CQ, 0, S_CQ, KT // 2, 256, x_lhs,
                       {1: lambda: x_groups(T_CQ, 4, 6, lambda g: g + 2),
                        3: lambda: x_groups(T_CQ, 6, 8, lambda g: g + 2)},
                       subs=2, before=lambda k: wait_x(k, T_CQ, 2))
                for b in range(4):
                    pe.wait_ge(acc_free[b], l * SETS + (S_CQ + 2))
                for i in range(NCH // 2):
                    def n_of(n):
                        return l * NCH + i * 2 + n
                    for h in range(2):
                        q = pj[:, :, bass.ds(i * (2 * HD) + h * HD, HD)]
                        k = kv[:, :, bass.ds(i * (2 * HD) + h * HD, HD)]
                        for j, v in enumerate((q[:, 0], q[:, 1], k[:, 0], k[:, 1])):
                            tr = pe.transpose(aux[:, (0, 3)[h], j * P:(j + 1) * P], v, ident)
                        tr.then_inc(x_tp, 1)
                    for h in range(2):
                        pe.wait_ge((x_qT, x_kT)[h], l * (NCH // 2) + (i + 1))
                        for t in range(NT):
                            mm = pe.matmul(aux[:, 1 + h, t * 256:(t + 1) * 256],
                                           qkT[:, h, t * P:(t + 1) * P], qkT[:, h, 256:512],
                                           start=True, stop=True)
                        mm.then_inc(x_s, 1)
                    for h in range(2):
                        pe.wait_ge(x_exp, n_of(h) * 2 + 2)
                        for j in range(4):
                            tr = pe.transpose(aux[:, (0, 2)[h], j * P:(j + 1) * P],
                                              E[:, h, j * P:(j + 1) * P], ident)
                        tr.then_inc(x_pT, 1)
                    for h in range(2):
                        pe.wait_ge(x_pTr, n_of(h + 1))
                        for t in range(NT):
                            for m in range(NT):
                                mm = pe.matmul(aux[:, 3, (2 * h + t) * P:(2 * h + t + 1) * P],
                                               pT[:, h, (2 * t + m) * P:(2 * t + m + 1) * P],
                                               kv[:, m, bass.ds(i * (2 * HD) + (CW + h * HD), HD)],
                                               start=m == 0, stop=m == 1)
                        mm.then_inc(x_o, 1)
                    pe.wait_ge(x_or, n_of(2))
                for t in range(NT):
                    group(T_CO + t, mg[:, t, 0:CW])

                def co_lhs(k):
                    return xTh[:, k, :], xTl[:, k, :]
                for s in range(2):
                    stream(0, K_CO + s * COK, 0, S_CO + s, COK, 512, co_lhs,
                           before=(lambda k: wait_x(k, T_CO, 1)) if s == 0 else None)

                def hidden_groups(n):
                    for t in range(NT):
                        pe.wait_ge(acc_free[2 + t], n)
                        for j in range(4):
                            tr = pe.transpose(aux[:, t, j * P:(j + 1) * P],
                                              E[:, t, j * P:(j + 1) * P], ident)
                        tr.then_inc(hT_done, 1)
                x_groups(T_FFN, 0, 4, lambda g: g + 10)
                stream(0, K_FFN, 0, S_FFN, KT, 512, x_lhs,
                       {2: lambda: x_groups(T_FFN, 4, 6, lambda g: g + 10),
                        4: lambda: x_groups(T_FFN, 6, 8, lambda g: g + 10)},
                       before=lambda k: wait_x(k, T_FFN, 1))
                with pe.Fori(0, FB - 1) as j:
                    stream(j * KT, K_FFN + KT, j, S_FFN + 1, KT, 512, x_lhs,
                           {3: lambda: hidden_groups(l * SETS + j + (S_FFN + 2))})

                def stage_lhs(slot):
                    return lambda k: (xTh[:, 4 * slot + k % 4, :], xTl[:, 4 * slot + k % 4, :])
                for s in range(2):
                    base, g0 = K_DOWN + s * G, s * FB
                    pe.wait_ge(st_ready, l * (2 * FB) + g0 + 1)
                    stream(0, base, 0, S_DOWN + s, 4, 512, stage_lhs(2),
                           {3: lambda: hidden_groups(l * SETS + (S_DOWN + 1))}
                           if s == 0 else None, stop=False)

                    def two(ahead, g, c, stop):
                        for n in range(2):
                            pe.wait_ge(st_ready, l * (2 * FB) + g + (g0 + n + 1))
                            stream(ahead, c + 4 * n, 0, S_DOWN + s, 4, 512, stage_lhs(1 - n),
                                   start=False, stop=stop and n == 1)
                    with pe.Fori(0, FB // 2 - 1) as g:
                        two(g * 8, g * 2 + 1, base + 4, False)
                    two(0, FB - 2, base + G - 8, True)

        @block.scalar
        def _(act):
            act.wait_ge(boot, 6)
            act.activation(sinb[:, :, :], trig[:, 2, :, :], ACT.Sin).then_inc(boot_act, 1)
            act.activation(cosb[:, :, :], trig[:, 3, :, :], ACT.Sin).then_inc(boot_act, 1)
            act.wait_ge(boot, 9)
            act.activation(lamd[:, :, :], lamd[:, :, :], ACT.Exp).then_inc(boot_act, 1)

            with act.Fori(0, DEPTH) as l:
                def split(ahead, c, width=WIDE):
                    s = c % RING
                    act.wait_ge(raw_full[s], l * (CHUNKS // RING * 32)
                                + ahead * (32 // RING)
                                + 32 * (c // RING + 1))
                    act.wait_ge(w_free, l * CHUNKS + ahead + (c + 1))
                    act.activation(wh[:, s, 0:width], raw[:, s, 0:width], ACT.Copy).then_inc(wh_ready, 1)

                def splits(ahead, c0, n, width=WIDE, hooks=None):
                    for k in range(n):
                        if hooks and k in hooks:
                            hooks[k]()
                        split(ahead, c0 + k, width)
                    if hooks and n in hooks:
                        hooks[n]()

                def square(n, src, total, wait=None):
                    if wait is not None:
                        act.wait_ge(*wait)
                    if n:
                        act.wait_ge(sq_done, l * SQUARES + n)
                    width = src.shape[-1]
                    act.activation(junk[:, 0:width], src, ACT.Square, accum_out=total).then_inc(sq_done, 1)

                def highs(t0, lo, hi, dst=None):
                    for g in range(lo, hi):
                        t, k = g % 2, g // 2 * 4
                        act.wait_ge(tp_gain, l * GROUPS + (t0 + g + 1))
                        act.activation((xTh if dst is None else dst)[:, k:k + 4, t * P:(t + 1) * P],
                                       R[:, g % 2, :].rearrange("p (k n) -> p k n", k=4), ACT.Copy)\
                           .then_inc(tp_high, 1)

                def drain_set(set_ahead, s, scale, dst, width):
                    for b in (0, 2):
                        wait_acc(act, l, set_ahead, s, b)
                        act.activation(dst(b // 2), acc[:, b, 0:width], ACT.Copy, scale=scale[:, 0:1])\
                           .then_inc(acc_free[b], 1)

                def drain_pair(i, pb):
                    act.wait_ge(rx_ready, l * 3 + 1)
                    drain_set(i, pb, rx, lambda a: pj[:, 0, a * 384:(a + 1) * 384], 384)

                def y_squares(s, q):
                    half = (s - S_OUT if s < S_CQ else s - S_CO if s < S_FFN else s - S_DOWN)
                    for b in range(4):
                        wait_acc(act, l, 0, s, b)
                        at = 2 * half + b // 2
                        square(q + b, acc[:, b, :], ssy[:, b % 2, at:at + 1])

                def att_qk(g_, i):
                    head, dve, actn, scores, one = attention(g_, l, i)
                    scale = 64 ** -0.5 if g_ == 0 else HD ** -0.5
                    act.wait_ge(qkT_done, head(1))
                    act.activation(qkT[:, 0, 0:256], aux[:, 0, 0:256], ACT.Copy, scale=scale)
                    act.activation(qkT[:, 0, 256:512], aux[:, 0, 256:512], ACT.Copy).then_inc(qkT_act, 1)

                def att_exps_a(i, h):
                    head, dve, actn, scores, one = attention(0, l, i)
                    if h == 1:
                        act.wait_ge(dve_att, dve(12))
                    for m in range(2):
                        act.wait_ge(dve_att, dve(12 * h + 4 + 2 * m))
                        for t, c in enumerate((slice(0, P), slice(P, 3 * P))):
                            act.activation(E[:, m, c], Z[:, m, c], ACT.Exp,
                                           bias=nmax[:, 2 * h + m, t:t + 1],
                                           accum_out=rsum[:, 2 * h + m, t:t + 1]).then_inc(act_att, 1)

                def att_exps_c(i):
                    head, dve, actn, scores, one = attention(2, l, i)
                    for h in range(2):
                        act.wait_ge(dve_att, dve(6 + 2 * h))
                        for t, c in enumerate((slice(0, P), slice(P, 3 * P))):
                            act.activation(E[:, h, c], Z[:, h, c], ACT.Exp, bias=nmax[:, h, t:t + 1],
                                           accum_out=rsum[:, h, t:t + 1]).then_inc(act_att, 1)

                def att_log(i):
                    head, dve, actn, scores, one = attention(1, l, i)
                    steps = ((ACT.Abs, Z, 1.0, 0.0), (ACT.Exp, E, -1.0, 0.0), (ACT.Ln, E, 1.0, 1.0))
                    for n, (f, src, scale, bias) in enumerate(steps):
                        for h in range(2):
                            if n == 0:
                                act.wait_ge(dve_att, dve(h + 1))
                            else:
                                act.wait_ge(act_att, actn(2 * n - 2 + h + 1))
                            act.activation(E[:, h, 0:3 * P], src[:, h, 0:3 * P], f, bias=bias, scale=scale)\
                               .then_inc(act_att, 1)

                def att_exps_b(i):
                    head, dve, actn, scores, one = attention(1, l, i)
                    for h in range(2):
                        act.wait_ge(dve_att, dve(9 + h))
                        act.activation(E[:, h, 0:3 * P], Z[:, h, 0:3 * P], ACT.Exp).then_inc(act_att, 1)

                def att_pT(g_, i):
                    head, dve, actn, scores, one = attention(g_, l, i)
                    act.wait_ge(pT_done, head(1))
                    act.activation(pT[:, 0, 0:3 * P], aux[:, 0, 0:3 * P], ACT.Copy).then_inc(pT_act, 1)

                def att_hooks(g_, i, pb):
                    hooks = {3: lambda: drain_pair(i, pb)}
                    if g_ == 0:
                        hooks.update({7: lambda: att_qk(0, i), 10: lambda: att_exps_a(i, 0),
                                      12: lambda: att_exps_a(i, 1), 13: lambda: att_pT(0, i)})
                    elif g_ == 1:
                        hooks.update({4: lambda: att_qk(1, i), 7: lambda: att_log(i),
                                      10: lambda: att_exps_b(i), 12: lambda: att_pT(1, i)})
                    else:
                        hooks.update({4: lambda: att_qk(2, i), 7: lambda: att_exps_c(i),
                                      12: lambda: att_pT(2, i)})
                    return hooks

                def gate_log():
                    act.wait_ge(f_step, l * 5 + 3)
                    act.activation(fe[:, :, :], fz[:, :, :], ACT.Abs).then_inc(f_act, 1)
                    act.wait_ge(f_act, l * 4 + 2)
                    act.activation(fe[:, :, :], fe[:, :, :], ACT.Exp, scale=-1.0).then_inc(f_act, 1)
                    act.wait_ge(f_act, l * 4 + 3)
                    act.activation(fe[:, :, :], fe[:, :, :], ACT.Ln, bias=1.0).then_inc(f_act, 1)

                def mem_squares():
                    for t in range(NT):
                        square(Q_MEM + t, mg[:, t, :], ssm[:, t:t + 1], (mem_full, l * 16 + 16))

                act.wait_ge(x_upd, l * 24 + 1)
                act.activation(wfh[:, :, :], wfr[:, bass.ds(l, 1), :, :].rearrange("p a k c -> p (a k) c"),
                               ACT.Copy).then_inc(f_act, 1)
                splits(0, 0, RING, PAIR_W)
                highs(T_X, 0, 4)
                splits(0, RING, KT - RING, PAIR_W, {
                    1: lambda: highs(T_X, 4, 6), 3: lambda: highs(T_X, 6, 8),
                    4: lambda: [square(Q_X + t, xs[:, t, :], ssx[:, t:t + 1]) for t in range(NT)],
                    6: mem_squares,
                    8: gate_log, 9: lambda: highs(T_MEM, 0, 2, memTh), 10: lambda: highs(T_MEM, 2, 4, memTh),
                    11: lambda: highs(T_MEM, 4, 6, memTh), 12: lambda: highs(T_MEM, 6, 8, memTh)})

                for g_, n in ((0, PAIRS_A), (1, PAIRS_B), (2, PAIRS_C - 1)):
                    pb = (0, PAIRS_A, PAIRS_A + PAIRS_B)[g_]
                    with act.Fori(0, n) as i:
                        splits(i * KT, (pb + 1) * KT, KT, PAIR_W, att_hooks(g_, i, pb))

                def head_squares():
                    act.wait_ge(o_read, l * (2 * PAIRS) + 2 * (PAIRS_A + PAIRS_B))
                    for t in range(NT):
                        for h in range(N_DIFF):
                            n = t * N_DIFF + h
                            square(Q_A + n, mg[:, t, h * HD:(h + 1) * HD], ssh[:, n:n + 1])
                    for t in range(NT):
                        square(Q_B + t, mg[:, t, 4 * HD:10 * HD], ssh[:, 8 + t:9 + t])

                def fox_squares():
                    act.wait_ge(o_read, (l + 1) * (2 * PAIRS))
                    for t in range(NT):
                        square(Q_C + t, mg[:, t, 10 * HD:D], ssh[:, 10 + t:11 + t])
                hooks = att_hooks(2, PAIRS_C - 1, PAIRS - 1)
                hooks[3] = lambda: drain_pair(0, PAIRS - 1)
                hooks[14] = head_squares
                hooks[16] = fox_squares
                splits(0, K_CKV, KT, WIDE, hooks)

                def drain_kv():
                    act.wait_ge(rm_ready, l + 1)
                    drain_set(0, S_CKV, rm, lambda a: kv[:, 0, a * 512:(a + 1) * 512], 512)
                splits(0, K_OUT, RING)
                drain_kv()
                highs(T_MIX, 0, 4)
                splits(0, K_OUT + RING, KT - RING, WIDE, {
                    2: lambda: highs(T_MIX, 4, 6), 4: lambda: highs(T_MIX, 6, 8)})
                splits(0, K_OUT + KT, KT, WIDE, {3: lambda: y_squares(S_OUT, Q_OUT)})
                splits(0, K_CQ, 3)
                y_squares(S_OUT + 1, Q_OUT + 4)
                splits(0, K_CQ + 3, 1)
                highs(T_CQ, 0, 4)
                splits(0, K_CQ + RING, KT // 2 - RING, WIDE, {
                    0: lambda: highs(T_CQ, 4, 6), 2: lambda: highs(T_CQ, 6, 8)})

                def x_squares(q, t_):
                    for t in range(NT):
                        square(q + t, xs[:, t, :], ssx[:, t:t + 1], (x_upd, l * 24 + t_))
                x_squares(Q_X2, 9)
                splits(0, K_CO, 3)
                act.wait_ge(rx_ready, l * 3 + 2)
                drain_set(0, S_CQ, rx, lambda a: pj[:, 0, a * 256:(a + 1) * 256], 256)
                splits(0, K_CO + 3, 1)
                with act.Fori(0, NCH // 2) as i:
                    def n_of(n):
                        return l * NCH + i * 2 + n
                    act.wait_ge(x_tp, n_of(1))
                    act.activation(qkT[:, 0, 0:256], aux[:, 0, 0:256], ACT.Copy, scale=HD ** -0.5)
                    act.activation(qkT[:, 0, 256:512], aux[:, 0, 256:512], ACT.Copy).then_inc(x_qT, 1)
                    for h in range(2):
                        act.wait_ge(x_max, n_of(h + 1))
                        for t in range(NT):
                            act.activation(E[:, h, t * 256:(t + 1) * 256],
                                           aux[:, 1 + h, t * 256:(t + 1) * 256], ACT.Exp,
                                           bias=nmax[:, h, t:t + 1],
                                           accum_out=rsum[:, h, t:t + 1]).then_inc(x_exp, 1)
                    for h in range(2):
                        act.wait_ge(x_pT, n_of(h + 1))
                        act.activation(pT[:, h, :], aux[:, (0, 2)[h], :], ACT.Copy).then_inc(x_pTr, 1)
                for t in range(NT):
                    act.wait_ge(tp_gain, l * GROUPS + (T_CO + t + 1))
                    act.activation(xTh[:, 0:4, t * P:(t + 1) * P],
                                   R[:, t, :].rearrange("p (k n) -> p k n", k=4), ACT.Copy)\
                       .then_inc(tp_high, 1)
                splits(0, K_CO + 4, 3)
                y_squares(S_CO, Q_CO)
                splits(0, K_CO + 7, 1)
                splits(0, K_FFN, 3)
                y_squares(S_CO + 1, Q_CO + 4)
                splits(0, K_FFN + 3, 1)
                highs(T_FFN, 0, 4)
                splits(0, K_FFN + RING, KT - RING, WIDE, {
                    1: lambda: highs(T_FFN, 4, 6), 3: lambda: highs(T_FFN, 6, 8),
                    6: lambda: x_squares(Q_X3, 17)})

                def silu(set_ahead, s):
                    act.wait_ge(rx_ready, l * 3 + 3)
                    for t in range(NT):
                        wait_acc(act, l, set_ahead, s, t)
                        act.activation(Z[:, t, :], acc[:, t, :], ACT.Silu, scale=rx[:, t:t + 1])\
                           .then_inc(acc_free[t], 1)

                def hidden(ahead, j):
                    act.wait_ge(hT_done, l * (2 * FB) + ahead * 2 + 2 * j + 1)
                    act.activation(hidT[:, bass.ds(ahead * 4 + 4 * j, 4), 0:P],
                                   aux[:, 0, :].rearrange("p (k n) -> p k n", k=4), ACT.Copy)\
                       .then_inc(hT_act, 1)
                with act.Fori(0, FB - 1) as j:
                    splits(j * KT, K_FFN + KT, KT, WIDE,
                           {3: lambda: silu(j, S_FFN), 7: lambda: hidden(j, 0)})

                def stage(ahead, s, g, slot):
                    act.wait_ge(w_free, l * CHUNKS + ahead * 4 + (K_DOWN + s * G + 4 * g))
                    act.activation(xTh[:, 4 * slot:4 * slot + 4, :],
                                   hidT[:, bass.ds(ahead * 4 + 4 * g, 4), :], ACT.Copy).then_inc(st_high, 1)
                for s in range(2):
                    base = K_DOWN + s * G
                    if s == 0:
                        act.wait_ge(hT_dve, l * FB + (FB - 1))
                    stage(0, s, 0, 2)
                    splits(0, base, 3)
                    if s == 0:
                        silu(0, S_FFN + FB - 1)
                    else:
                        y_squares(S_DOWN, Q_DOWN)
                    splits(0, base + 3, 1)
                    if s == 0:
                        stage(0, s, 1, 1)
                        splits(0, base + 4, 3)
                        hidden(0, FB - 1)
                        splits(0, base + 7, 1)
                        stage(0, s, 2, 0)
                        splits(0, base + 8, 4)
                        act.wait_ge(hT_dve, l * FB + FB)
                        act.wait_ge(hT_act, l * FB + FB)
                    lo = 3 if s == 0 else 1
                    with act.Fori(0, (FB - lo) // 2) as g:
                        stage(g * 2, s, lo, 1)
                        splits(g * 8, base + 4 * lo, 4)
                        stage(g * 2, s, lo + 1, 0)
                        splits(g * 8, base + 4 * lo + 4, 4)
                y_squares(S_DOWN + 1, Q_DOWN + 4)

        @block.vector
        def _(dve):
            dve.memset(mhalf[:, :], -0.5).then_inc(wl_ready, RING)
            dve.wait_ge(wl_ready, RING)
            dve.memset(fs[:, 0, 0:1], 0.0).then_inc(w_free, RING)
            for b in range(4):
                dve.memset(fe[:, 0, b:b + 1], 0.0).then_inc(acc_free[b], 1)
            dve.wait_ge(init_dma, 16 * N_INIT)

            two_pi = 2.0 * math.pi
            c1 = 6.28125
            c2 = float(np.float32(two_pi - c1))
            c3 = two_pi - c1 - c2
            big = 12582912.0
            dve.tensor_copy(posf[:, :], posi[:, :]).then_inc(boot, 1)
            dve.wait_ge(boot, 1)
            for t in range(NT):
                mm = dve.tensor_scalar(trig[:, 0, t, :], freq, posf[:, t:t + 1], None, ALU.mult)
            mm.then_inc(boot, 1)
            dve.wait_ge(boot, 2)
            step = 0
            for which, shift in ((2, 0.0), (3, 0.25)):
                r = trig[:, which, :, :]
                u = trig[:, 1, :, :]
                ops = [
                    lambda: dve.tensor_scalar(u, trig[:, 0, :, :], 1.0 / two_pi, shift, ALU.mult, ALU.add),
                    lambda: dve.tensor_scalar(u, u, big, None, ALU.add),
                    lambda: dve.tensor_scalar(u, u, -big, None, ALU.add),
                    lambda: dve.scalar_tensor_tensor(r, u, -c1, trig[:, 0, :, :], ALU.mult, ALU.add),
                    lambda: dve.scalar_tensor_tensor(r, u, -c2, r, ALU.mult, ALU.add),
                    lambda: dve.scalar_tensor_tensor(r, u, -c3, r, ALU.mult, ALU.add),
                    lambda: dve.tensor_scalar(r, r, two_pi * shift, None, ALU.add),
                    lambda: dve.tensor_scalar(r, r, 3.1415925, -3.1415925, ALU.min, ALU.max),
                ]
                for op in ops:
                    step += 1
                    op().then_inc(boot_dve, 1)
                    dve.wait_ge(boot_dve, step)
            dve.tensor_copy(lamd[:, 0, 0:1], posf[:, 0:1]).then_inc(boot, 4)
            dve.wait_ge(boot, 6)
            for n in range(2):
                dve.tensor_tensor(lamr[:, 2 * n, :], lamr[:, 2 * n, :], lamr[:, 2 * n + 1, :], ALU.mult)\
                   .then_inc(boot_dve, 1)
            dve.wait_ge(boot_dve, step + 2)
            for n in range(2):
                dve.tensor_reduce(lamd[:, n, :], lamr[:, 2 * n, :].rearrange("p (l d) -> p l d", l=DEPTH),
                                  AX_X, ALU.add).then_inc(boot, 1)
            dve.wait_ge(boot, 8)
            dve.tensor_copy(posf[:, 0:1], mhalf[:, 0:1]).then_inc(boot, 1)
            for n in range(DEPTH):
                dve.wait_ge(boot_pe, n + 1)
                dve.tensor_copy(gT[:, n, :], aux[:, n, 0:GAINS]).then_inc(boot_dve, 1)
            dve.wait_ge(boot_dve, step + 2 + DEPTH)
            dve.wait_ge(boot_act, 3)
            for n in range(DEPTH):
                v = gT[:, n, G_MERGED:G_MERGED + N_DIFF]
                dve.tensor_scalar(v, v, 1.0 - lam_init[n], None, ALU.mult).then_inc(boot_dve, 1)
            dve.tensor_tensor(nlam[:, :], lamd[:, 1, :], lamd[:, 0, :], ALU.subtract).then_inc(boot_dve, 1)
            dve.wait_ge(boot_dve, step + 3 + 2 * DEPTH)
            for n in range(DEPTH):
                dve.tensor_scalar(nlam[:, n:n + 1], nlam[:, n:n + 1], -lam_init[n], None, ALU.add)\
                   .then_inc(boot_dve, 1)
            dve.wait_ge(boot_dve, step + 3 + 3 * DEPTH)
            dve.memset(fz[:, 0, 0:1], 0.0).then_inc(x_upd, 1)

            with dve.Fori(0, DEPTH) as l:
                def splits(ahead, c0, n, width=WIDE, hooks=None):
                    for k in range(n):
                        if hooks and k in hooks:
                            hooks[k]()
                        s = (c0 + k) % RING
                        dve.wait_ge(wh_ready, l * CHUNKS + ahead + (c0 + k + 1))
                        dve.tensor_tensor(wl[:, s, 0:width], raw[:, s, 0:width],
                                          wh[:, s, 0:width].bitcast(F32), ALU.subtract)\
                           .then_inc(wl_ready, 1)
                    if hooks and n in hooks:
                        hooks[n]()

                def gain(n, t, k, goff, reused=False):
                    dve.wait_ge(tp_done, l * GROUPS + (n + 1))
                    src = aux[:, n % 4 if not T_MEM <= n < T_MIX else n % 2, :]
                    dst = R[:, t, :]
                    if reused:
                        dve.wait_ge(xT_ready, lows(l, n - 2))
                    if goff is None:
                        dve.tensor_copy(dst, src).then_inc(tp_gain, 1)
                    else:
                        g = gT[:, bass.ds(l, 1), goff + k:goff + k + 4].rearrange("p a k -> p (a k)")
                        dve.tensor_tensor(dst.rearrange("p (k n) -> p k n", k=4),
                                          src.rearrange("p (k n) -> p k n", k=4),
                                          g.unsqueeze(2).to_broadcast([P, 4, P]), ALU.mult)\
                           .then_inc(tp_gain, 1)

                def low(n, t, k):
                    dve.wait_ge(tp_high, l * GROUPS + (n + 1))
                    tok = slice(t * P, (t + 1) * P)
                    dve.tensor_tensor(xTl[:, k:k + 4, tok], R[:, t, :].rearrange("p (k n) -> p k n", k=4),
                                      xTh[:, k:k + 4, tok].bitcast(F32), ALU.subtract)\
                       .then_inc(xT_ready, 1)

                def groups(t0, lo, hi, goff, upd=None):
                    for g in range(lo, hi):
                        if upd is not None:
                            for b in ((0, 1, 2) if g == 0 else (g + 2,)):
                                if b < 8:
                                    update(b, upd)
                        gain(t0 + g, g % 2, g // 2 * 4, goff, g > 1)
                        if g > lo:
                            low(t0 + g - 1, (g - 1) % 2, (g - 1) // 2 * 4)
                    low(t0 + hi - 1, (hi - 1) % 2, (hi - 1) // 2 * 4)

                def update(b, n):
                    if b == 0:
                        dve.wait_ge(ry_ready, l * 3 + n + 1)
                    t, c = b % 2, slice(b // 2 * 512, (b // 2 + 1) * 512)
                    dve.scalar_tensor_tensor(xs[:, t, c], mg[:, t, c], ry[:, t:t + 1], xs[:, t, c],
                                             ALU.mult, ALU.add).then_inc(x_upd, 1)

                def drain_set(set_ahead, s, scale, dst, width):
                    for b in (1, 3):
                        wait_acc(dve, l, set_ahead, s, b)
                        dve.tensor_scalar(dst(b // 2), acc[:, b, 0:width], scale[:, 1:2], None, ALU.mult)\
                           .then_inc(acc_free[b], 1)

                def drain_pair(i, pb):
                    dve.wait_ge(rx_ready, l * 3 + 1)
                    drain_set(i, pb, rx, lambda a: pj[:, 1, a * 384:(a + 1) * 384], 384)

                def drain_y(half, q, n):
                    dve.wait_ge(gbc_full, l * 48 + 16 * (n + 1))
                    for b in range(4):
                        dve.wait_ge(sq_done, l * SQUARES + (q + b + 1))
                        c = slice((2 * half + b // 2) * 512, (2 * half + b // 2 + 1) * 512)
                        dve.tensor_tensor(mg[:, b % 2, c], acc[:, b, :], gbc[:, c], ALU.mult)\
                           .then_inc(acc_free[b], 1)

                def sum_y():
                    dve.tensor_reduce(ssy2[:, :], ssy[:, :, :], AX_X, ALU.add).then_inc(ssy_ready, 1)

                def att_qk(g_, i):
                    head, dven, actn, scores, one = attention(g_, l, i)
                    scale = 64 ** -0.5 if g_ == 0 else HD ** -0.5
                    dve.wait_ge(qkT_done, head(2))
                    dve.tensor_scalar(qkT[:, 1, 0:256], aux[:, 3, 0:256], scale, None, ALU.mult)
                    dve.tensor_copy(qkT[:, 1, 256:512], aux[:, 3, 256:512]).then_inc(qkT_dve, 1)

                def neg_max(m, src):
                    dve.tensor_reduce(nmax[:, m, 0:1], src[:, 0:P], AX_X, ALU.max, negate=True)\
                       .then_inc(dve_att, 1)
                    dve.tensor_reduce(nmax[:, m, 1:2], src[:, P:3 * P], AX_X, ALU.max, negate=True)\
                       .then_inc(dve_att, 1)

                def att_max_a(i, h):
                    head, dven, actn, scores, one = attention(0, l, i)
                    for m in range(2):
                        dve.wait_ge(s_done, scores(2 * h + m + 1))
                        dve.tensor_tensor(Z[:, m, 0:3 * P], aux[:, 1 + m, 0:3 * P], causal, ALU.add)\
                           .then_inc(dve_att, 1)
                    for m in range(2):
                        dve.wait_ge(dve_att, dven(12 * h + m + 1))
                        neg_max(2 * h + m, Z[:, m, :])

                def att_mix_a(i, h):
                    head, dven, actn, scores, one = attention(0, l, i)
                    dve.wait_ge(act_att, actn(4 * h + 4))
                    dve.reciprocal(rinv[:, 2 * h:2 * h + 2, :], rsum[:, 2 * h:2 * h + 2, :])\
                       .then_inc(dve_att, 1)
                    dve.wait_ge(dve_att, dven(12 * h + 7))
                    dve.tensor_scalar(rinv[:, 2 * h + 1, :], rinv[:, 2 * h + 1, :], nlam[:, bass.ds(l, 1)],
                                      None, ALU.mult).then_inc(dve_att, 1)
                    parts = (slice(0, P), slice(P, 3 * P))
                    for t, c in enumerate(parts):
                        dve.tensor_scalar(R[:, h, c], E[:, 0, c], rinv[:, 2 * h, t:t + 1], None, ALU.mult)\
                           .then_inc(dve_att, 1)
                    dve.wait_ge(dve_att, dven(12 * h + 10))
                    for t, c in enumerate(parts):
                        dve.scalar_tensor_tensor(R[:, h, c], E[:, 1, c], rinv[:, 2 * h + 1, t:t + 1],
                                                 R[:, h, c], ALU.mult, ALU.add).then_inc(dve_att, 1)

                def att_mask_b(i):
                    head, dven, actn, scores, one = attention(1, l, i)
                    for h in range(2):
                        dve.wait_ge(s_done, scores(h + 1))
                        dve.tensor_tensor(Z[:, h, 0:3 * P], aux[:, 1 + h, 0:3 * P], strict, ALU.add)\
                           .then_inc(dve_att, 1)

                def att_sums_b(i):
                    head, dven, actn, scores, one = attention(1, l, i)
                    for h in range(2):
                        dve.wait_ge(act_att, actn(5 + h))
                        dve.scalar_tensor_tensor(E[:, h, 0:3 * P], Z[:, h, 0:3 * P], 0.0, E[:, h, 0:3 * P],
                                                 ALU.max, ALU.add).then_inc(dve_att, 1)
                    for h in range(2):
                        dve.wait_ge(dve_att, dven(3 + h))
                        for lo, hi in ((0, P), (P, 3 * P)):
                            back = E[:, h, lo:hi][:, ::-1]
                            dve.tensor_tensor_scan(R[:, h, lo:hi][:, ::-1], back, back, 0.0,
                                                   ALU.add, ALU.max).then_inc(dve_att, 1)
                    for h in range(2):
                        dve.wait_ge(dve_att, dven(6 + 2 * h))
                        dve.tensor_tensor(Z[:, h, 0:3 * P], Z[:, h, 0:3 * P], R[:, h, 0:3 * P],
                                          ALU.subtract).then_inc(dve_att, 1)

                def att_max_c(i):
                    head, dven, actn, scores, one = attention(2, l, i)
                    for h in range(2):
                        dve.wait_ge(s_done, scores(h + 1))
                        for t, c in enumerate((slice(0, P), slice(P, 3 * P))):
                            dve.scalar_tensor_tensor(Z[:, h, c], aux[:, 1 + h, c], cumq[:, h, t:t + 1],
                                                     causal[:, c], ALU.add, ALU.add).then_inc(dve_att, 1)
                    for h in range(2):
                        dve.wait_ge(dve_att, dven(2 * h + 2))
                        neg_max(h, Z[:, h, :])

                def att_inv_c(i):
                    head, dven, actn, scores, one = attention(2, l, i)
                    for h in range(2):
                        dve.wait_ge(act_att, actn(2 * h + 2))
                        dve.reciprocal(rinv[:, h, :], rsum[:, h, :]).then_inc(dve_att, 1)

                def att_pT(g_, i):
                    head, dven, actn, scores, one = attention(g_, l, i)
                    dve.wait_ge(pT_done, head(2))
                    dve.tensor_copy(pT[:, 1, 0:3 * P], aux[:, 2, 0:3 * P]).then_inc(pT_dve, 1)

                def att_out(g_, i):
                    head, dven, actn, scores, one = attention(g_, l, i)
                    col = (0, N_DIFF * HD, (N_DIFF + N_SB) * HD)[g_]
                    if g_ == 2:
                        dve.wait_ge(dve_att, dven(10))
                    dve.wait_ge(o_done, head(2))
                    for h in range(2):
                        at = bass.ds(i * (2 * HD) + (col + h * HD), HD)
                        o = aux[:, 3, h * 256:(h + 1) * 256].rearrange("p (t n) -> p t n", t=NT)
                        if g_ < 2:
                            dve.tensor_copy(mg[:, :, at], o).then_inc(o_read, 1)
                        else:
                            dve.tensor_tensor(mg[:, :, at], o, rinv[:, h, :].unsqueeze(2)
                                              .to_broadcast([P, NT, HD]), ALU.mult).then_inc(o_read, 1)

                def att_hooks(g_, i, pb):
                    hooks = {3: lambda: drain_pair(i, pb)}
                    if g_ == 0:
                        hooks.update({7: lambda: att_qk(0, i), 9: lambda: att_max_a(i, 0),
                                      10: lambda: att_mix_a(i, 0), 11: lambda: att_max_a(i, 1),
                                      13: lambda: att_mix_a(i, 1), 15: lambda: att_pT(0, i),
                                      16: lambda: att_out(0, i)})
                    elif g_ == 1:
                        hooks.update({4: lambda: att_qk(1, i), 6: lambda: att_mask_b(i),
                                      9: lambda: att_sums_b(i), 12: lambda: att_pT(1, i),
                                      14: lambda: att_out(1, i)})
                    else:
                        hooks.update({4: lambda: att_qk(2, i), 6: lambda: att_max_c(i),
                                      9: lambda: att_inv_c(i), 12: lambda: att_pT(2, i),
                                      14: lambda: att_out(2, i)})
                    return hooks

                def gate_logits():
                    dve.wait_ge(f_done, l + 1)
                    dve.wait_ge(rx_ready, l * 3 + 1)
                    for t in range(NT):
                        dve.scalar_tensor_tensor(
                            fz[:, t, :], aux[:, 3, t * 8:t * 8 + N_FOX], rx[:, t:t + 1],
                            bfb[:, bass.ds(l, 1), :].rearrange("p a c -> p (a c)"),
                            ALU.mult, ALU.add).then_inc(f_step, 1)
                    dve.wait_ge(f_step, l * 5 + 3)
                    dve.tensor_scalar(fs[:, :, :], fz[:, :, :], -1.0, 0.0, ALU.mult, ALU.max)\
                       .then_inc(f_step, 1)

                def gate_sum():
                    dve.wait_ge(f_step, l * 5 + 4)
                    dve.wait_ge(f_act, l * 4 + 4)
                    dve.tensor_tensor(nlf[:, :, :].rearrange("p c t -> p t c"), fs[:, :, :], fe[:, :, :],
                                      ALU.add).then_inc(f_step, 1)

                def gate_cum():
                    dve.wait_ge(cum_done, l + 1)
                    for t in range(NT):
                        m = dve.tensor_scalar(cum[:, :, t], aux[:, 2, t * 8:t * 8 + N_FOX], -1.0, None,
                                              ALU.mult)
                    m.then_inc(cum_ready, 1)

                def mem_gains(lo, hi):
                    for g in range(lo, hi):
                        if g > 1:
                            dve.wait_ge(mem_low, l * 8 + g - 1)
                        gain(T_MEM + g, g % 2, g // 2 * 4, G_MEM)
                dve.wait_ge(f_act, l * 4 + 1)
                dve.tensor_tensor(wfl[:, :, :], wfr[:, bass.ds(l, 1), :, :].rearrange("p a k c -> p (a k) c"),
                                  wfh[:, :, :].bitcast(F32), ALU.subtract).then_inc(f_step, 1)
                splits(0, 0, RING, PAIR_W)
                groups(T_X, 0, 4, G_MIX)
                splits(0, RING, KT - RING, PAIR_W, {
                    1: lambda: groups(T_X, 4, 6, G_MIX), 3: lambda: groups(T_X, 6, 8, G_MIX),
                    7: gate_logits, 8: lambda: (mem_gains(0, 2), gate_sum()),
                    9: lambda: mem_gains(2, 4), 10: lambda: mem_gains(4, 6), 11: lambda: mem_gains(6, 8),
                    12: gate_cum})

                for g_, n in ((0, PAIRS_A), (1, PAIRS_B), (2, PAIRS_C - 1)):
                    pb = (0, PAIRS_A, PAIRS_A + PAIRS_B)[g_]
                    with dve.Fori(0, n) as i:
                        splits(i * KT, (pb + 1) * KT, KT, PAIR_W, att_hooks(g_, i, pb))

                def norm_ab():
                    dve.wait_ge(rh_ready, l * 2 + 1)
                    for t in range(NT):
                        v = mg[:, t, 0:N_DIFF * HD].rearrange("p (h n) -> p h n", n=HD)
                        r = rh[:, t * N_DIFF:(t + 1) * N_DIFF].unsqueeze(2).to_broadcast([P, N_DIFF, HD])
                        m = dve.tensor_tensor(v, v, r, ALU.mult)
                    m.then_inc(mg_ready, 1)
                    for t in range(NT):
                        v = mg[:, t, 4 * HD:10 * HD]
                        dve.tensor_scalar(v, v, rh[:, 8 + t:9 + t], None, ALU.mult).then_inc(mg_ready, 1)

                def norm_c():
                    dve.wait_ge(rh_ready, l * 2 + 2)
                    for t in range(NT):
                        v = mg[:, t, 10 * HD:D]
                        dve.tensor_scalar(v, v, rh[:, 10 + t:11 + t], None, ALU.mult).then_inc(mg_ready, 1)
                hooks = att_hooks(2, PAIRS_C - 1, PAIRS - 1)
                hooks[3] = lambda: drain_pair(0, PAIRS - 1)
                hooks[16] = norm_ab
                splits(0, K_CKV, KT, WIDE, hooks)

                splits(0, K_OUT, RING)
                norm_c()
                dve.wait_ge(rm_ready, l + 1)
                drain_set(0, S_CKV, rm, lambda a: kv[:, 1, a * 512:(a + 1) * 512], 512)
                groups(T_MIX, 0, 4, G_MERGED)
                splits(0, K_OUT + RING, KT - RING, WIDE, {
                    2: lambda: groups(T_MIX, 4, 6, G_MERGED), 4: lambda: groups(T_MIX, 6, 8, G_MERGED)})
                splits(0, K_OUT + KT, KT, WIDE, {3: lambda: drain_y(0, Q_OUT, 0)})
                splits(0, K_CQ, 3)
                drain_y(1, Q_OUT + 4, 0)
                sum_y()
                splits(0, K_CQ + 3, 1)
                groups(T_CQ, 0, 4, G_X, 0)
                splits(0, K_CQ + RING, KT // 2 - RING, WIDE, {
                    0: lambda: groups(T_CQ, 4, 6, G_X, 0), 2: lambda: groups(T_CQ, 6, 8, G_X, 0)})

                splits(0, K_CO, 3)
                dve.wait_ge(rx_ready, l * 3 + 2)
                drain_set(0, S_CQ, rx, lambda a: pj[:, 1, a * 256:(a + 1) * 256], 256)
                splits(0, K_CO + 3, 1)
                with dve.Fori(0, NCH // 2) as i:
                    def n_of(n):
                        return l * NCH + i * 2 + n
                    dve.wait_ge(x_tp, n_of(2))
                    dve.tensor_scalar(qkT[:, 1, 0:256], aux[:, 3, 0:256], HD ** -0.5, None, ALU.mult)
                    dve.tensor_copy(qkT[:, 1, 256:512], aux[:, 3, 256:512]).then_inc(x_kT, 1)
                    for h in range(2):
                        dve.wait_ge(x_s, n_of(h + 1))
                        dve.tensor_reduce(nmax[:, h, :], aux[:, 1 + h, :].rearrange("p (t n) -> p t n", t=NT),
                                          AX_X, ALU.max, negate=True).then_inc(x_max, 1)
                    for h in range(2):
                        dve.wait_ge(x_exp, n_of(h) * 2 + 2)
                        dve.reciprocal(rinv[:, h, :], rsum[:, h, :]).then_inc(x_inv, 1)
                    dve.wait_ge(x_o, n_of(2))
                    dve.wait_ge(x_inv, n_of(2))
                    for h in range(2):
                        dve.tensor_tensor(mg[:, :, bass.ds(i * (2 * HD) + h * HD, HD)],
                                          aux[:, 3, h * 256:(h + 1) * 256].rearrange("p (t n) -> p t n", t=NT),
                                          rinv[:, h, :].unsqueeze(2).to_broadcast([P, NT, HD]), ALU.mult)\
                           .then_inc(x_or, 1)
                for t in range(NT):
                    gain(T_CO + t, t, 0, None)
                for t in range(NT):
                    low(T_CO + t, t, 0)
                splits(0, K_CO + 4, 3)
                drain_y(0, Q_CO, 1)
                splits(0, K_CO + 7, 1)
                splits(0, K_FFN, 3)
                drain_y(1, Q_CO + 4, 1)
                sum_y()
                splits(0, K_FFN + 3, 1)
                groups(T_FFN, 0, 4, G_FFN, 1)
                splits(0, K_FFN + RING, KT - RING, WIDE, {
                    1: lambda: groups(T_FFN, 4, 6, G_FFN, 1), 3: lambda: groups(T_FFN, 6, 8, G_FFN, 1)})

                def product(set_ahead, s):
                    dve.wait_ge(rx_ready, l * 3 + 3)
                    for t in range(NT):
                        wait_acc(dve, l, set_ahead, s, 2 + t)
                        dve.wait_ge(acc_free[t], l * SETS + set_ahead + (s + 2))
                        dve.scalar_tensor_tensor(E[:, t, :], acc[:, 2 + t, :], rx[:, t:t + 1], Z[:, t, :],
                                                 ALU.mult, ALU.mult).then_inc(acc_free[2 + t], 1)

                def hidden(ahead, j):
                    dve.wait_ge(hT_done, l * (2 * FB) + ahead * 2 + 2 * j + 2)
                    dve.tensor_copy(hidT[:, bass.ds(ahead * 4 + 4 * j, 4), P:2 * P],
                                    aux[:, 1, :].rearrange("p (k n) -> p k n", k=4)).then_inc(hT_dve, 1)
                with dve.Fori(0, FB - 1) as j:
                    splits(j * KT, K_FFN + KT, KT, WIDE,
                           {3: lambda: product(j, S_FFN), 7: lambda: hidden(j, 0)})

                def stage(ahead, s, g, slot):
                    dve.wait_ge(st_high, l * (2 * FB) + ahead + (s * FB + g + 1))
                    dve.tensor_tensor(xTl[:, 4 * slot:4 * slot + 4, :],
                                      hidT[:, bass.ds(ahead * 4 + 4 * g, 4), :],
                                      xTh[:, 4 * slot:4 * slot + 4, :].bitcast(F32), ALU.subtract)\
                       .then_inc(st_ready, 1)
                for s in range(2):
                    base = K_DOWN + s * G
                    stage(0, s, 0, 2)
                    splits(0, base, 3)
                    if s == 0:
                        product(0, S_FFN + FB - 1)
                    else:
                        drain_y(0, Q_DOWN, 2)
                    splits(0, base + 3, 1)
                    if s == 0:
                        stage(0, s, 1, 1)
                        splits(0, base + 4, 3)
                        hidden(0, FB - 1)
                        splits(0, base + 7, 1)
                        stage(0, s, 2, 0)
                        splits(0, base + 8, 4)
                    lo = 3 if s == 0 else 1
                    with dve.Fori(0, (FB - lo) // 2) as g:
                        stage(g * 2, s, lo, 1)
                        splits(g * 8, base + 4 * lo, 4)
                        stage(g * 2, s, lo + 1, 0)
                        splits(g * 8, base + 4 * lo + 4, 4)
                drain_y(1, Q_DOWN + 4, 2)
                sum_y()
                for b in range(8):
                    update(b, 2)

        @block.gpsimd
        def _(pool):
            pool.memset(eps[:, :], EPS).then_inc(boot_pool, 1)
            pool.memset(inv_w[:, IW_D:IW_A], 1.0 / D).then_inc(boot_pool, 1)
            pool.memset(inv_w[:, IW_A:IW_A + NT * N_DIFF], 1.0 / HD).then_inc(boot_pool, 1)
            pool.memset(inv_w[:, IW_A + NT * N_DIFF:IW_C], 1.0 / (N_SB * HD)).then_inc(boot_pool, 1)
            pool.memset(inv_w[:, IW_C:IW_C + NT], 1.0 / (N_FOX * HD)).then_inc(boot_pool, 1)
            pool.wait_ge(boot_pool, 5)
            pool.wait_ge(boot_act, 2)
            pool.wait_ge(wl_ready, RING)
            with pool.Fori(0, DEPTH) as l:
                def rms(n, dst, src, at, done):
                    w = src.shape[-1]
                    pool.tensor_tensor(msx[:, n, 0:w], src, inv_w[:, at:at + w], ALU.mult).then_inc(ms, 1)
                    pool.wait_ge(ms, l * 18 + 2 * n + 1)
                    pool.tensor_tensor(msx[:, n, 0:w], msx[:, n, 0:w], eps[:, 0:w], ALU.add).then_inc(ms, 1)
                    pool.wait_ge(ms, l * 18 + 2 * n + 2)
                    pool.tensor_tensor(dst, msx[:, n, 0:w], mhalf[:, 0:w], ALU.pow).then_inc(done, 1)

                def rms_x(n, q):
                    pool.wait_ge(sq_done, l * SQUARES + q + NT)
                    rms(n, rx[:, :], ssx[:, :], IW_D, rx_ready)

                def rms_y(n, k):
                    pool.wait_ge(ssy_ready, l * 3 + k + 1)
                    rms(n, ry[:, :], ssy2[:, :], IW_D, ry_ready)
                rms_x(0, Q_X)
                pool.wait_ge(sq_done, l * SQUARES + Q_MEM + NT)
                rms(1, rm[:, :], ssm[:, :], IW_D, rm_ready)
                for g in range(8):
                    t, k = g % 2, g // 2 * 4
                    tok = slice(t * P, (t + 1) * P)
                    pool.wait_ge(tp_high, l * GROUPS + (T_MEM + g + 1))
                    pool.tensor_tensor(memTl[:, k:k + 4, tok], R[:, t, :].rearrange("p (k n) -> p k n", k=4),
                                       memTh[:, k:k + 4, tok].bitcast(F32), ALU.subtract)\
                        .then_inc(mem_low, 1)

                with pool.Fori(0, PAIRS_A) as i:
                    pool.wait_ge(mem_low, l * 8 + 8)
                    for b in range(4):
                        pool.wait_ge(acc_free[b], l * SETS + i + 2)
                    for t in range(NT):
                        v = pj[:, t, 0:512].rearrange("p (b n) -> p b n", n=ROT)
                        v4 = pj[:, t, 0:512].rearrange("p (b s n) -> p b s n", s=2, n=ROT)
                        a = R[:, 0, :].rearrange("p (b n) -> p b n", n=ROT)
                        a4 = R[:, 0, :].rearrange("p (b s n) -> p b s n", s=2, n=ROT)
                        b4 = R[:, 1, :].rearrange("p (b s n) -> p b s n", s=2, n=ROT)
                        cosv = cosb[:, t, :].unsqueeze(1)
                        sinv = sinb[:, t, :].unsqueeze(1).to_broadcast([P, 8, ROT])
                        n0 = l * (10 * PAIRS_A) + i * 10 + 5 * t
                        if t:
                            pool.wait_ge(rope_step, n0)
                        pool.tensor_tensor(a, v, cosv.to_broadcast([P, 16, ROT]), ALU.mult)\
                            .then_inc(rope_step, 1)
                        for s in range(2):
                            pool.tensor_tensor(b4[:, :, s, :], v4[:, :, 1 - s, :], sinv, ALU.mult)\
                                .then_inc(rope_step, 1)
                        pool.wait_ge(rope_step, n0 + 3)
                        for s, op in ((0, ALU.subtract), (1, ALU.add)):
                            pool.tensor_tensor(v4[:, :, s, :], a4[:, :, s, :], b4[:, :, s, :], op)\
                                .then_inc(rope_step, 1)

                def spread(i):
                    head, dven, actn, scores, one = attention(2, l, i)
                    pool.wait_ge(cum_ready, l + 1)
                    pool.wait_ge(dve_att, dven(0))
                    h2 = bass.ds(i * 2, 2)
                    pool.tensor_copy(cumq[:, :, :], cum[:, h2, :])
                    pool.tensor_copy(nlb[:, :, :, :].rearrange("p h t n -> p (h t) n"),
                                     nlf[:, h2, :].rearrange("p h t -> p (h t)").unsqueeze(2)
                                     .to_broadcast([P, 2 * NT, P])).then_inc(fox_ready, 1)
                with pool.Fori(0, PAIRS_C) as i:
                    spread(i)
                pool.wait_ge(sq_done, l * SQUARES + Q_C)
                rms(2, rh[:, 0:10], ssh[:, 0:10], IW_A, rh_ready)
                pool.wait_ge(sq_done, l * SQUARES + Q_C + NT)
                rms(3, rh[:, 10:12], ssh[:, 10:12], IW_C, rh_ready)
                rms_y(4, 0)
                rms_x(5, Q_X2)
                rms_y(6, 1)
                rms_x(7, Q_X3)
                rms_y(8, 2)


_INS = ["x", "mem", "positions", "g_mix_pre", "g_mix_post", "w_in", "b_f", "lam_q1", "lam_k1", "lam_q2",
        "lam_k2", "g_diff_sub", "g_sb_out", "g_fox_out", "w_out", "g_x_pre", "g_x_post", "g_mem", "w_cq",
        "w_ckv", "w_co", "g_ffn_pre", "g_ffn_post", "w_gate", "w_up", "w_down"]


def _constants():
    q, k = np.arange(P)[:, None], np.arange(P)[None, :]
    zero = np.zeros((P, P))
    causal = np.where(q >= k, 0.0, NEG)
    strict = np.where(q > k, 0.0, NEG)
    c = np.zeros((P, C_W), np.float32)
    c[:, C_ID:C_ID + P] = np.eye(P)
    c[:, C_CAUSAL:C_CAUSAL + 3 * P] = np.concatenate([causal, zero, causal], 1)
    c[:, C_STRICT:C_STRICT + 3 * P] = np.concatenate([strict, zero, strict], 1)
    c[:, C_TRI:C_TRI + P] = q <= k
    c[:, C_ONES:C_ONES + P] = 1.0
    c[:, C_FREQ:C_FREQ + ROT] = np.float32(ROPE_THETA) ** (-np.arange(ROT, dtype=np.float32) / ROT)
    return c


def kernel(**inputs):
    import concourse.bacc as bacc
    from concourse.bass_utils import run_bass_kernel_spmd

    nc = bacc.Bacc("TRN2", target_bir_lowering=False, num_devices=1, dynamic_dma_scratch_size=1024)
    arrays, args = {}, []
    for name in _INS:
        a = np.ascontiguousarray(inputs[name])
        arrays[f"in_{name}"] = a
        args.append(nc.dram_tensor(f"in_{name}", a.shape, mybir.dt.from_np(a.dtype), kind="ExternalInput").ap())
    arrays["in_consts"] = _constants()
    args.append(nc.dram_tensor("in_consts", (P, C_W), F32, kind="ExternalInput").ap())
    args.append(nc.dram_tensor("out_x", inputs["x"].shape, F32, kind="ExternalOutput").ap())
    trunk(nc, *args)
    r = run_bass_kernel_spmd(nc, [arrays], core_ids=[0])
    return r.results[0]["out_x"]
```

```python
import math
from contextlib import ExitStack

import numpy as np

import concourse.bass as bass
from concourse import mybir

ALU = mybir.AluOpType
ACT = mybir.ActivationFunctionType
F32 = mybir.dt.float32
F32R = mybir.dt.float32r
BF16 = mybir.dt.bfloat16
I32 = mybir.dt.int32
AX_X = mybir.AxisListType.X

P = 128
NT = 2
EPS = 1e-6
NEG = -1e30
ROPE_THETA = 10000.0
N_DIFF, N_SB, N_FOX = 4, 6, 6
HD = 128
ROT = 32
PAIR_W = 3 * 2 * HD
WIDE = 1024
PAIRS_A, PAIRS_B, PAIRS_C = N_DIFF // 2, N_SB // 2, N_FOX // 2
PAIRS = PAIRS_A + PAIRS_B + PAIRS_C

ORDER = (0, 2, 1, 3)
RING = 4

C_ID, C_CAUSAL, C_STRICT, C_TRI, C_ONES, C_FREQ = 0, 128, 512, 896, 1024, 1152
C_W = C_FREQ + ROT


def trunk(nc, x, mem, positions, g_mix_pre, g_mix_post, w_in, b_f, lam_q1, lam_k1, lam_q2, lam_k2,
          g_diff_sub, g_sb_out, g_fox_out, w_out, g_x_pre, g_x_post, g_mem, w_cq, w_ckv, w_co,
          g_ffn_pre, g_ffn_post, w_gate, w_up, w_down, consts, out):
    DEPTH, D = g_mix_pre.shape
    DFF = w_gate.shape[2]
    KT = D // P
    FB = DFF // 512
    CW = w_cq.shape[2]
    NCH = CW // HD
    COK = CW // P
    lam_init = [0.8 - 0.6 * math.exp(-0.3 * n) for n in range(DEPTH)]
    G = 4 * (FB)
    assert D == 2048 and G == DFF // P and FB % 2 == 1 and CW == 512

    S_OUT = PAIRS
    S_MK, S_CQ, S_MV, S_CO = S_OUT + 2, S_OUT + 3, S_OUT + 4, S_OUT + 5
    S_FFN, S_DOWN = S_CO + 2, S_CO + 2 + FB
    SETS = S_DOWN + 2
    K_OUT = PAIRS * KT
    K_MK = K_OUT + 2 * KT
    K_CQ = K_MK + KT // 2
    K_MV = K_CQ + KT // 2
    K_CO = K_MV + KT // 2
    K_FFN = K_CO + 2 * COK
    K_DOWN = K_FFN + FB * KT
    CHUNKS = K_DOWN + 2 * G
    T_X, T_MIX, T_MEM, T_CQ, T_CO, T_FFN, GROUPS = 0, 8, 16, 24, 32, 34, 42
    G_MIX, G_X, G_FFN, G_MEM, G_MERGED, GAINS = 0, KT, 2 * KT, 3 * KT, 4 * KT, 5 * KT
    Q_X, Q_A, Q_B, Q_C, Q_OUT, Q_MEM, Q_OUT2, Q_X2, Q_CO, Q_X3, Q_DOWN, SQUARES = \
        0, 2, 10, 12, 14, 18, 20, 24, 26, 34, 36, 44

    NORMS = 12

    with ExitStack() as ctx:
        def sb(name, shape, dt=F32):
            return ctx.enter_context(nc.sbuf_tensor(name, shape, dt))

        def sem(name):
            return ctx.enter_context(nc.semaphore(name))

        cst = sb("cst", [P, C_W])
        ident = cst[:, C_ID:C_ID + P]
        causal = cst[:, C_CAUSAL:C_CAUSAL + 3 * P]
        strict = cst[:, C_STRICT:C_STRICT + 3 * P]
        tri = cst[:, C_TRI:C_TRI + P]
        ones = cst[:, C_ONES:C_ONES + P]
        freq = cst[:, C_FREQ:C_FREQ + ROT]
        xs = sb("xs", [P, NT, D])
        raw = sb("raw", [P, RING, WIDE])
        wh = sb("wh", [P, RING, WIDE], F32R)
        wl = sb("wl", [P, RING, WIDE], F32R)
        xTh = sb("xTh", [P, KT, NT * P], F32R)
        xTl = sb("xTl", [P, KT, NT * P], F32R)
        pj = sb("pj", [P, NT, PAIR_W])
        mg = sb("mg", [P, NT, D])
        mst = sb("mst", [P, NT, D])
        with ExitStack() as mixer:
            memTh = mixer.enter_context(nc.sbuf_tensor("memTh", [P, KT, NT * P], F32R))
            memTl = mixer.enter_context(nc.sbuf_tensor("memTl", [P, KT, NT * P], F32R))
            kv = mixer.enter_context(nc.sbuf_tensor("kv", [P, NT, 2 * CW], F32))
        hidT = sb("hidT", [P, G, NT * P])
        gbc = sb("gbc", [P, D])
        Z = sb("Z", [P, 2, 512])
        E = sb("E", [P, 2, 512])
        R = sb("R", [P, 2, 512])
        pT = sb("pT", [P, 2, 512])
        qkT = sb("qkT", [P, 2, 512])
        nlb = sb("nlb", [P, 2, NT, P])
        fT = Z[0:N_FOX, 0, 0:NT * P]
        junk = qkT[:, :, :].rearrange("p a n -> p (a n)").bitcast(BF16)
        gT = sb("gT", [P, DEPTH, GAINS])
        grow = sb("grow", [P, DEPTH, P])
        wfr = sb("wfr", [P, DEPTH, KT, N_FOX])
        wfh = sb("wfh", [P, KT, N_FOX], F32R)
        wfl = sb("wfl", [P, KT, N_FOX], F32R)
        bfb = sb("bfb", [P, DEPTH, N_FOX])
        fz = sb("fz", [P, NT, N_FOX])
        fe = sb("fe", [P, NT, N_FOX])
        fs = sb("fs", [P, NT, N_FOX])
        nlf = sb("nlf", [P, N_FOX, NT])
        cum = sb("cum", [P, N_FOX, NT])
        cumq = sb("cumq", [P, 2, NT])
        posi = sb("posi", [P, NT], I32)
        posf = sb("posf", [P, NT])
        trig = sb("trig", [P, 5, NT, ROT])
        cosb = sb("cosb", [P, NT, ROT])
        sinb = sb("sinb", [P, NT, ROT])
        lamr = sb("lamr", [P, 4, DEPTH * 64])
        lamp = sb("lamp", [P, 2, DEPTH * 64])
        lamd = sb("lamd", [P, 2, DEPTH])
        lame = sb("lame", [P, 2, DEPTH])
        lamn = sb("lamn", [P, DEPTH])
        nlam = sb("nlam", [P, DEPTH])
        mhalf = sb("mhalf", [P, 16])
        eps = sb("eps", [P, 16])
        inv_w = sb("inv_w", [P, 14])
        IW_D, IW_A, IW_C = 0, 2, 12
        ssy = sb("ssy", [P, NT, 4])
        ssy2 = sb("ssy2", [P, NT])
        ssx = sb("ssx", [P, NT])
        ssm = sb("ssm", [P, NT])
        ssh = sb("ssh", [P, 12])
        msx = sb("msx", [P, 9, 12])
        rx = sb("rx", [P, NT])
        rm = sb("rm", [P, NT])
        ry = sb("ry", [P, NT])
        rh = sb("rh", [P, 12])
        nmax = sb("nmax", [P, 4, NT])
        rsum = sb("rsum", [P, 4, NT])
        rinv = sb("rinv", [P, 4, NT])

        acc = ctx.enter_context(nc.psum_tensor("acc", [P, 4, 512], F32))
        aux = ctx.enter_context(nc.psum_tensor("aux", [P, 4, 512], F32))

        cst_full = sem("cst_full")
        x_full = [sem(f"x_full{n}") for n in range(4)]
        gains_full = sem("gains_full")
        wf_full = sem("wf_full")
        par_full = sem("par_full")
        raw_full = [sem(f"raw_full{s}") for s in range(RING)]
        wh_ready = sem("wh_ready")
        wl_ready = sem("wl_ready")
        w_free = sem("w_free")
        acc_done = sem("acc_done")
        acc_free = [sem(f"acc_free{b}") for b in range(4)]
        tp_done = sem("tp_done")
        tp_gain = sem("tp_gain")
        tp_high = sem("tp_high")
        xT_ready = sem("xT_ready")
        mem_full = sem("mem_full")
        gbc_full = sem("gbc_full")
        x_upd = [sem(f"x_upd{t}") for t in range(NT)]
        sq_done = sem("sq_done")
        ssy_ready = [sem(f"ssy_ready{t}") for t in range(NT)]
        ms = sem("ms")
        rx_ready = sem("rx_ready")
        rm_ready = sem("rm_ready")
        ry_ready = [sem(f"ry_ready{t}") for t in range(NT)]
        rh_ready = sem("rh_ready")
        mg_ready = sem("mg_ready")
        f_done = sem("f_done")
        f_step = sem("f_step")
        f_act = sem("f_act")
        cum_done = sem("cum_done")
        cum_ready = sem("cum_ready")
        fox_ready = sem("fox_ready")
        rope_step = sem("rope_step")
        mem_low = sem("mem_low")
        qkT_done = sem("qkT_done")
        qkT_act = sem("qkT_act")
        qkT_dve = sem("qkT_dve")
        s_done = sem("s_done")
        dve_att = sem("dve_att")
        act_att = sem("act_att")
        pT_done = sem("pT_done")
        pT_act = sem("pT_act")
        pT_dve = sem("pT_dve")
        o_done = sem("o_done")
        o_read = sem("o_read")
        x_act = sem("x_act")
        x_dve = sem("x_dve")
        x_tp = sem("x_tp")
        x_s = sem("x_s")
        x_max = sem("x_max")
        x_exp = sem("x_exp")
        x_inv = sem("x_inv")
        x_pT = sem("x_pT")
        x_pTa = sem("x_pTa")
        x_pTd = sem("x_pTd")
        x_o = sem("x_o")
        x_or = sem("x_or")
        silu_done = sem("silu_done")
        hT_done = sem("hT_done")
        hT_act = sem("hT_act")
        hT_dve = sem("hT_dve")
        st_high = sem("st_high")
        st_ready = sem("st_ready")
        boot = sem("boot")
        boot_pe = sem("boot_pe")
        boot_pool = sem("boot_pool")
        boot_trig = sem("boot_trig")
        trig_ready = sem("trig_ready")
        sin_ready = sem("sin_ready")
        lam_step = sem("lam_step")
        lam_exp = sem("lam_exp")
        stored = sem("stored")

        DA, DB, DC = 24, 10, 10
        AA, AB, AC = 8, 8, 4
        DVE_ATT = PAIRS_A * DA + PAIRS_B * DB + PAIRS_C * DC
        ACT_ATT = PAIRS_A * AA + PAIRS_B * AB + PAIRS_C * AC
        MAPS = PAIRS_A * 4 + (PAIRS_B + PAIRS_C) * 2

        w_in_v = [
            w_in[:, :, 0:3 * N_DIFF * HD],
            w_in[:, :, 3 * N_DIFF * HD:3 * (N_DIFF + N_SB) * HD],
            w_in[:, :, 3 * (N_DIFF + N_SB) * HD:3 * (N_DIFF + N_SB + N_FOX) * HD],
        ]
        w_in_v = [v.rearrange("l (k p) (s c) -> l k p s c", p=P, s=3) for v in w_in_v]
        w_f_v = w_in[:, :, 3 * (N_DIFF + N_SB + N_FOX) * HD:].rearrange("l (k p) c -> p l k c", p=P)
        w_out_v = w_out.rearrange("l (k p) n -> l k p n", p=P)
        w_ckv_v = w_ckv.rearrange("l (k j p) n -> l k p j n", j=2, p=P)
        w_cq_v = w_cq.rearrange("l (k j p) n -> l k p j n", j=2, p=P)
        w_co_v = w_co.rearrange("l (k p) n -> l k p n", p=P)
        w_gate_v = w_gate.rearrange("l (k p) n -> l k p n", p=P)
        w_up_v = w_up.rearrange("l (k p) n -> l k p n", p=P)
        w_down_v = w_down.rearrange("l (k p) n -> l k p n", p=P)
        x_v = x.rearrange("b (t p) d -> p (b t) d", p=P)
        mem_v = mem.rearrange("b (t p) d -> p (b t) d", p=P)
        out_v = out.rearrange("b (t p) d -> p (b t) d", p=P)

        block = ctx.enter_context(nc.Block())

        def lows(l, n):
            return l * (GROUPS - 8) + ((n if n < T_MEM else n - 8) + 1)

        def last_chunk(s):
            if s < S_MK:
                return KT * (s + 1) - 1
            if s < S_FFN:
                return (K_CQ, K_MV, K_CO, K_CO + COK, K_FFN)[s - S_MK] - 1
            if s < S_DOWN:
                return K_FFN + (s - S_FFN + 1) * KT - 1
            return K_DOWN + (s - S_DOWN + 1) * G - 1

        def wait_acc(eng, l, sets, s, b):
            if b < 3:
                eng.wait_ge(acc_done, l * (3 * SETS) + sets * 3 + (3 * s + ORDER.index(b) + 1))
            else:
                eng.wait_ge(w_free, l * CHUNKS + sets * KT + (last_chunk(s) + 1 + RING))

        def attention(group, l, i):
            pb = (0, PAIRS_A, PAIRS_A + PAIRS_B)[group]
            dve0 = (0, PAIRS_A * DA, PAIRS_A * DA + PAIRS_B * DB)[group]
            act0 = (0, PAIRS_A * AA, PAIRS_A * AA + PAIRS_B * AB)[group]
            map0 = (0, PAIRS_A * 4, PAIRS_A * 4 + PAIRS_B * 2)[group]
            d, a, m = ((DA, AA, 4), (DB, AB, 2), (DC, AC, 2))[group]

            def head(n):
                return l * (2 * PAIRS) + i * 2 + (2 * pb + n)

            def dve(n):
                return l * DVE_ATT + i * d + (dve0 + n)

            def act(n):
                return l * ACT_ATT + i * a + (act0 + n)

            def scores(n):
                return l * MAPS + i * m + (map0 + n)

            def one(n):
                return l * PAIRS + i + (pb + n)
            return head, dve, act, scores, one

        @block.sync
        def _(sp):
            sp.dma_start(cst[:, :], consts).then_inc(cst_full, 16)
            sp.dma_start(xs[:, :, 0:512], x_v[:, :, 0:512]).then_inc(x_full[0], 16)

            with sp.Fori(0, DEPTH) as l:
                def chunk(ahead, c, dsts, srcs):
                    sp.wait_ge(wl_ready, l * CHUNKS + ahead + (c + 1))
                    for d, v in zip(dsts, srcs):
                        sp.dma_start(d, v).then_inc(raw_full[c % RING], 32 // len(srcs))

                def slot(c):
                    return raw[:, c % RING, :]

                def pair_chunk(group, base, ahead, col, k):
                    chunk(ahead, base + k, [slot(k)[:, 0:PAIR_W].rearrange("p (s c) -> p s c", s=3)],
                          [w_in_v[group][l, k, :, :, bass.ds(col, 2 * HD)]])

                for k in range(KT):
                    if k == KT // 2:
                        sp.wait_ge(x_upd[1], l * 12 + 4)
                        sp.dma_start(gbc[:, :], g_mix_post[l, :].partition_broadcast(P))\
                          .then_inc(gbc_full, 16)
                    pair_chunk(0, 0, 0, 0, k)
                for group, start, n in ((0, 1, PAIRS_A), (1, 0, PAIRS_B), (2, 0, PAIRS_C)):
                    pb = (0, PAIRS_A, PAIRS_A + PAIRS_B)[group]
                    with sp.Fori(start, n) as i:
                        for k in range(KT):
                            pair_chunk(group, pb * KT, i * KT, i * (2 * HD), k)
                with sp.Fori(0, 2) as s:
                    for k in range(KT):
                        chunk(s * KT, K_OUT + k, [slot(k)], [w_out_v[l, k, :, bass.ds(s * WIDE, WIDE)]])
                for base, w, col in ((K_MK, w_ckv_v, 0), (K_CQ, w_cq_v, 0), (K_MV, w_ckv_v, CW)):
                    for k in range(KT // 2):
                        if base == K_MV and k == 0:
                            sp.wait_ge(x_upd[1], l * 12 + 8)
                            sp.dma_start(gbc[:, :], g_x_post[l, :].partition_broadcast(P))\
                              .then_inc(gbc_full, 16)
                        chunk(0, base + k, [slot(k).rearrange("p (j n) -> p j n", j=2)],
                              [w[l, k, :, :, col:col + CW]])
                for s in range(2):
                    for k in range(COK):
                        chunk(0, K_CO + s * COK + k, [slot(k)], [w_co_v[l, k, :, s * WIDE:(s + 1) * WIDE]])
                with sp.Fori(0, FB) as j:
                    for k in range(KT):
                        chunk(j * KT, K_FFN + k, [slot(k)[:, 0:512], slot(k)[:, 512:1024]],
                              [w_gate_v[l, k, :, bass.ds(j * 512, 512)],
                               w_up_v[l, k, :, bass.ds(j * 512, 512)]])
                sp.wait_ge(x_upd[1], l * 12 + 12)
                sp.dma_start(gbc[:, :], g_ffn_post[l, :].partition_broadcast(P)).then_inc(gbc_full, 16)
                for s in range(2):
                    half = slice(s * WIDE, (s + 1) * WIDE)
                    for k in range(4):
                        chunk(0, K_DOWN + s * G + k, [slot(k)], [w_down_v[l, k, :, half]])
                    with sp.Fori(0, FB // 2) as g:
                        for k in range(8):
                            chunk(g * 8, K_DOWN + s * G + 4 + k, [slot(k)],
                                  [w_down_v[l, g * 8 + (4 + k), :, half]])
            sp.wait_ge(x_upd[1], DEPTH * 12 + 4)
            sp.dma_start(out_v, xs[:, :, :]).then_inc(stored, 16)
            sp.wait_ge(stored, 16)

        N_GAINS, N_PAR = 7, 1 + 1 + 4

        @block.tensor
        def _(pe):
            pe.wait_ge(cst_full, 16)
            pe.wait_ge(gains_full, 16 * N_GAINS)
            for n in range(DEPTH):
                pe.transpose(aux[:, 4 - DEPTH + n, 0:GAINS], grow[0:GAINS, n, :], ident[0:GAINS, 0:GAINS])\
                  .then_inc(boot_pe, 1)

            with pe.Fori(0, DEPTH) as l:
                def stream(ahead, c0, set_ahead, set0, n, width, lhs, hooks=None, start=True,
                           stop=True, subs=1, before=None, early=False, late=False):
                    def products(k, t):
                        slot = (c0 + k) % RING
                        for a in range(2):
                            b = 2 * a + t
                            if start and k == 0:
                                pe.wait_ge(acc_free[b], l * SETS + set_ahead + (set0 + 1))
                            for j in range(subs):
                                hi, lo = lhs(k * subs + j)
                                cols = slice(j * 512 + a * width, j * 512 + (a + 1) * width)
                                tok = slice(t * P, (t + 1) * P)
                                o = acc[:, b, 0:width]
                                pe.matmul(o, hi[:, tok], wh[:, slot, cols],
                                          start=start and k == 0 and j == 0, stop=False)
                                pe.matmul(o, hi[:, tok], wl[:, slot, cols], start=False, stop=False)
                                mm = pe.matmul(o, lo[:, tok], wh[:, slot, cols], start=False,
                                               stop=stop and k == n - 1 and j == subs - 1)
                            if stop and k == n - 1 and b < 3:
                                mm.then_inc(acc_done, 1)
                        if t == 1:
                            mm.then_inc(w_free, 1)

                    def enter(k, t):
                        if hooks and (k, t) in hooks:
                            hooks[(k, t)]()
                        if t == 0:
                            if hooks and k in hooks:
                                hooks[k]()
                            pe.wait_ge(wl_ready, l * CHUNKS + ahead + (c0 + k + 1 + RING))
                        if before:
                            before(k, t)
                    apart = [range(0, RING)] if early else []
                    apart += [range(n - RING, n)] if late else []
                    k = 0
                    while k < n:
                        ks = next((list(a) for a in apart if k in a), [k])
                        for t in range(NT):
                            for k in ks:
                                enter(k, t)
                                products(k, t)
                        k = ks[-1] + 1
                    if hooks and n in hooks:
                        hooks[n]()

                def x_lhs(k):
                    return xTh[:, k, :], xTl[:, k, :]

                def mem_lhs(k):
                    return memTh[:, k, :], memTl[:, k, :]

                def group(n, src, ready=None, back=4):
                    if ready is not None:
                        pe.wait_ge(*ready)
                    if n >= back:
                        pe.wait_ge(tp_gain, l * GROUPS + (n - back + 1))
                    for j in range(4):
                        tr = pe.transpose(aux[:, n % 4, j * P:(j + 1) * P],
                                          src[:, j * P:(j + 1) * P], ident)
                    tr.then_inc(tp_done, 1)

                def cols(g):
                    return g % 2, slice(g // 2 * 512, (g // 2 + 1) * 512)

                def wait_x(k, t, t0, per):
                    if k % (4 // per) == 0:
                        pe.wait_ge(xT_ready, lows(l, t0 + 2 * (k * per // 4) + t))

                def x_groups(t0, lo, hi, n):
                    for g in range(lo, hi):
                        t, c = cols(g)
                        if t0 == T_X and t == 0:
                            pe.wait_ge(x_full[g // 2], 16)
                        group(t0 + g, xs[:, t, c], (x_upd[t], l * 12 + 4 * n + (g // 2 + 1)))

                def att_transpose(group_, i):
                    head, dve, act, scores, one = attention(group_, l, i)
                    if group_ == 0:
                        pe.wait_ge(rope_step, l * (10 * PAIRS_A) + i * 10 + 10)
                    for b in range(4):
                        pe.wait_ge(acc_free[b], l * SETS + i + ((0, PAIRS_A, PAIRS_A + PAIRS_B)[group_] + 2))
                    for h in range(2):
                        for j, (t, at) in enumerate(((0, h), (1, h), (0, 2 + h), (1, 2 + h))):
                            tr = pe.transpose(aux[:, (0, 3)[h], j * P:(j + 1) * P],
                                              pj[:, t, at * HD:(at + 1) * HD], ident)
                        tr.then_inc(qkT_done, 1)

                def att_scores(group_, i, h):
                    head, dve, act, scores, one = attention(group_, l, i)
                    pe.wait_ge((qkT_act, qkT_dve)[h], one(1))
                    if group_ == 0 and h == 1:
                        pe.wait_ge(dve_att, dve(2))
                    if group_ == 2 and h == 0:
                        pe.wait_ge(fox_ready, l * PAIRS_C + i + 1)
                    maps = 2 if group_ == 0 else 1
                    for m in range(maps):
                        rows = slice(64 * m, 64 * m + 64) if group_ == 0 else slice(0, P)
                        s = aux[:, 1 + (m if group_ == 0 else h), :]
                        q, k = qkT[rows, h, 0:256], qkT[rows, h, 256:512]
                        last = group_ != 2
                        mm = pe.matmul(s[:, 0:P], q[:, 0:P], k[:, 0:P], start=True, stop=last)
                        if not last:
                            pe.matmul(s[:, 0:P], nlb[:, h, 0, :], tri, start=False, stop=True)
                        mm = pe.matmul(s[:, P:3 * P], q[:, P:2 * P], k[:, :], start=True, stop=last)
                        if not last:
                            pe.matmul(s[:, P:2 * P], nlb[:, h, 0, :], tri, start=False, stop=False)
                            pe.matmul(s[:, 2 * P:3 * P], nlb[:, h, 0, :], ones, start=False, stop=False)
                            mm = pe.matmul(s[:, 2 * P:3 * P], nlb[:, h, 1, :], tri, start=False, stop=True)
                        mm.then_inc(s_done, 1)

                def att_weights(group_, i, h):
                    head, dve, act, scores, one = attention(group_, l, i)
                    if group_ == 0:
                        pe.wait_ge(dve_att, dve(12 * (h + 1)))
                    else:
                        pe.wait_ge(act_att, act(7 + h if group_ == 1 else 2 * h + 2))
                    src = (R if group_ == 0 else E)[:, h, :]
                    for j in range(3):
                        tr = pe.transpose(aux[:, (0, 2)[h], j * P:(j + 1) * P], src[:, j * P:(j + 1) * P], ident)
                    tr.then_inc(pT_done, 1)

                def att_values(group_, i, h):
                    head, dve, act, scores, one = attention(group_, l, i)
                    pe.wait_ge((pT_act, pT_dve)[h], one(1))
                    v = [pj[:, t, (4 + h) * HD:(5 + h) * HD] for t in range(NT)]
                    o = aux[:, 3, h * 256:(h + 1) * 256]
                    pe.matmul(o[:, 0:P], pT[:, h, 0:P], v[0], start=True, stop=True)
                    pe.matmul(o[:, P:2 * P], pT[:, h, P:2 * P], v[0], start=True, stop=False)
                    pe.matmul(o[:, P:2 * P], pT[:, h, 2 * P:3 * P], v[1], start=False, stop=True)\
                      .then_inc(o_done, 1)

                def both(f, g_, i):
                    f(g_, i, 0)
                    f(g_, i, 1)

                def att_hooks(g_, i):
                    if g_ == 0:
                        return {4: lambda: att_transpose(0, i), 6: lambda: att_scores(0, i, 0),
                                8: lambda: att_scores(0, i, 1), 10: lambda: att_weights(0, i, 0),
                                11: lambda: att_values(0, i, 0), 12: lambda: att_weights(0, i, 1),
                                13: lambda: att_values(0, i, 1)}
                    return {1: lambda: att_transpose(g_, i), 3: lambda: both(att_scores, g_, i),
                            9: lambda: both(att_weights, g_, i), 11: lambda: both(att_values, g_, i)}

                x_groups(T_X, 0, 1, 0)

                def gate():
                    pe.wait_ge(f_step, l * 6 + 1)
                    o = aux[0:N_FOX, 3, 0:NT * P]
                    for k in range(KT):
                        pe.matmul(o, wfh[:, k, :], xTh[:, k, :], start=k == 0, stop=False)
                        pe.matmul(o, wfl[:, k, :], xTh[:, k, :], start=False, stop=False)
                        mm = pe.matmul(o, wfh[:, k, :], xTl[:, k, :], start=False, stop=k == KT - 1)
                    mm.then_inc(f_done, 1)

                def gate_wait():
                    pe.wait_ge(f_step, l * 6 + 2)

                def gate_transpose():
                    for t in range(NT):
                        tr = pe.transpose(aux[:, 3, t * P:t * P + N_FOX], fT[:, t * P:(t + 1) * P],
                                          ident[0:N_FOX, 0:N_FOX])
                    tr.then_inc(f_done, 1)

                def cumulate():
                    pe.wait_ge(f_step, l * 6 + 6)
                    o = aux[:, 2, :]
                    pe.matmul(o[:, 0:N_FOX], tri, nlf[:, :, 0], start=True, stop=True)
                    pe.matmul(o[:, 8:8 + N_FOX], ones, nlf[:, :, 0], start=True, stop=False)
                    pe.matmul(o[:, 8:8 + N_FOX], tri, nlf[:, :, 1], start=False, stop=True)\
                      .then_inc(cum_done, 1)

                stream(0, 0, 0, 0, KT, 384, x_lhs, {
                    1: lambda: x_groups(T_X, 1, 2, 0), 3: lambda: x_groups(T_X, 2, 3, 0),
                    (1, 1): lambda: x_groups(T_X, 3, 4, 0), (3, 1): lambda: x_groups(T_X, 4, 6, 0),
                    5: lambda: x_groups(T_X, 6, 8, 0), 8: gate, 10: gate_wait, 11: gate_transpose, 14: cumulate,
                }, before=lambda k, t: wait_x(k, t, T_X, 1), early=True)

                for g_, n in ((0, PAIRS_A), (1, PAIRS_B), (2, PAIRS_C - 2)):
                    pb = (0, PAIRS_A, PAIRS_A + PAIRS_B)[g_]
                    with pe.Fori(0, n) as i:
                        stream(i * KT, (pb + 1) * KT, i, pb + 1, KT, 384, x_lhs, att_hooks(g_, i))

                def mix_groups(lo, hi):
                    for g in range(lo, hi):
                        t, c = cols(g)
                        group(T_MIX + g, mg[:, t, c],
                              (mg_ready, l * 5 + (1 if g < 2 else 3 if g < 4 else 5)))

                def mem_groups(lo, hi):
                    for g in range(lo, hi):
                        t, c = cols(g)
                        group(T_MEM + g, mst[:, t, c])
                hooks = att_hooks(2, PAIRS_C - 2)
                hooks[16] = lambda: mix_groups(0, 2)
                stream(0, K_OUT - KT, 0, PAIRS - 1, KT, 384, x_lhs, hooks)

                mix_groups(2, 4)

                def last_transpose():
                    pe.wait_ge(tp_gain, l * GROUPS + (T_MIX + 4))
                    att_transpose(2, PAIRS_C - 1)
                stream(0, K_OUT, 0, S_OUT, KT, 512, x_lhs, {
                    2: last_transpose, 3: lambda: both(att_scores, 2, PAIRS_C - 1),
                    4: lambda: both(att_weights, 2, PAIRS_C - 1),
                    6: lambda: both(att_values, 2, PAIRS_C - 1), 8: lambda: mix_groups(4, 8)},
                       before=lambda k, t: wait_x(k, t, T_MIX, 1))
                pe.wait_ge(mem_full, 16)
                stream(0, K_OUT + KT, 0, S_OUT + 1, KT, 512, x_lhs,
                       {2 + n: (lambda g: lambda: mem_groups(g, g + 1))(n) for n in range(8)})

                pe.wait_ge(mem_low, l * 8 + 8)
                stream(0, K_MK, 0, S_MK, KT // 2, 256, mem_lhs,
                       {2: lambda: x_groups(T_CQ, 0, 2, 1),
                        3: lambda: x_groups(T_CQ, 2, 4, 1),
                        5: lambda: x_groups(T_CQ, 4, 6, 1),
                        7: lambda: x_groups(T_CQ, 6, 8, 1)}, subs=2)
                stream(0, K_CQ, 0, S_CQ, KT // 2, 256, x_lhs, subs=2,
                       before=lambda k, t: wait_x(k, t, T_CQ, 2))

                def x_transpose(p):
                    for b in range(4):
                        pe.wait_ge(acc_free[b], l * SETS + (S_CQ + 2))
                    for h in range(2):
                        at = slice((2 * p + h) * HD, (2 * p + h + 1) * HD)
                        for j, v in enumerate((pj[:, 0, at], pj[:, 1, at], kv[:, 0, at], kv[:, 1, at])):
                            tr = pe.transpose(aux[:, (0, 3)[h], j * P:(j + 1) * P], v, ident)
                        tr.then_inc(x_tp, 1)

                def x_scores(p):
                    for h in range(2):
                        pe.wait_ge((x_act, x_dve)[h], l * 2 + (p + 1))
                        if p:
                            pe.wait_ge(x_exp, l * (2 * NCH) + (2 * h + 2))
                        for t in range(NT):
                            mm = pe.matmul(aux[:, 1 + h, t * 256:(t + 1) * 256],
                                           qkT[:, h, t * P:(t + 1) * P], qkT[:, h, 256:512],
                                           start=True, stop=True)
                        mm.then_inc(x_s, 1)

                def x_weights(p):
                    for h in range(2):
                        pe.wait_ge(x_exp, l * (2 * NCH) + (4 * p + 2 * h + 2))
                        for j in range(4):
                            tr = pe.transpose(aux[:, ((0, 3) if p == 0 else (1, 2))[h], j * P:(j + 1) * P],
                                              (E if p == 0 else Z)[:, h, j * P:(j + 1) * P], ident)
                        tr.then_inc(x_pT, 1)

                def x_values(p):
                    for h in range(2):
                        pe.wait_ge((x_pTa, x_pTd)[h], l * 2 + (p + 1))
                        at = CW + (2 * p + h) * HD
                        for t in range(NT):
                            for m in range(NT):
                                mm = pe.matmul(aux[:, (0, 3)[p], (2 * h + t) * P:(2 * h + t + 1) * P],
                                               (pT if p == 0 else R)[:, h, (2 * t + m) * P:(2 * t + m + 1) * P],
                                               kv[:, m, at:at + HD], start=m == 0, stop=m == 1)
                    mm.then_inc(x_o, 1)
                stream(0, K_MV, 0, S_MV, KT // 2, 256, mem_lhs,
                       {1: lambda: x_transpose(0), 2: lambda: x_scores(0), 3: lambda: x_transpose(1),
                        4: lambda: x_scores(1), 5: lambda: x_weights(0), 7: lambda: x_weights(1)}, subs=2)
                for b in range(4):
                    pe.wait_ge(acc_free[b], l * SETS + (S_MV + 2))
                for p in range(2):
                    x_values(p)
                pe.wait_ge(x_or, l * 2 + 2)
                for t in range(NT):
                    group(T_CO + t, mg[:, t, 0:CW])

                def co_lhs(k):
                    return xTh[:, k, :], xTl[:, k, :]
                for s in range(2):
                    stream(0, K_CO + s * COK, 0, S_CO + s, COK, 512, co_lhs,
                           before=(lambda k, t: wait_x(k, t, T_CO, 1)) if s == 0 else None,
                           early=s == 0, late=s == 1)

                def hidden_groups(n):
                    for t in range(NT):
                        pe.wait_ge(acc_free[2 + t], n)
                        for j in range(4):
                            tr = pe.transpose(aux[:, t, j * P:(j + 1) * P],
                                              E[:, t, j * P:(j + 1) * P], ident)
                        tr.then_inc(hT_done, 1)
                x_groups(T_FFN, 0, 1, 2)
                stream(0, K_FFN, 0, S_FFN, KT, 512, x_lhs,
                       {1: lambda: x_groups(T_FFN, 1, 2, 2), 3: lambda: x_groups(T_FFN, 2, 3, 2),
                        (1, 1): lambda: x_groups(T_FFN, 3, 4, 2), (3, 1): lambda: x_groups(T_FFN, 4, 6, 2),
                        5: lambda: x_groups(T_FFN, 6, 8, 2)},
                       before=lambda k, t: wait_x(k, t, T_FFN, 1), early=True)
                with pe.Fori(0, (FB - 1) // 2) as j:
                    for n in range(2):
                        stream(j * (2 * KT), K_FFN + KT + n * KT, j * 2, S_FFN + 1 + n, KT, 512, x_lhs,
                               {3: lambda: hidden_groups(l * SETS + j * 2 + (S_FFN + 2 + n))})

                def stage_lhs(slot):
                    return lambda k: (xTh[:, 4 * slot + k % 4, :], xTl[:, 4 * slot + k % 4, :])
                for s in range(2):
                    base, g0 = K_DOWN + s * G, s * FB
                    pe.wait_ge(st_ready, l * (2 * FB) + g0 + 1)
                    stream(0, base, 0, S_DOWN + s, 4, 512, stage_lhs(2),
                           {3: lambda: hidden_groups(l * SETS + (S_DOWN + 1))}
                           if s == 0 else None, stop=False)

                    def two(ahead, g, c, stop):
                        for n in range(2):
                            pe.wait_ge(st_ready, l * (2 * FB) + g + (g0 + n + 1))
                            stream(ahead, c + 4 * n, 0, S_DOWN + s, 4, 512, stage_lhs(1 - n),
                                   start=False, stop=stop and n == 1, late=stop and s == 1 and n == 1)
                    with pe.Fori(0, FB // 2 - 1) as g:
                        two(g * 8, g * 2 + 1, base + 4, False)
                    two(0, FB - 2, base + G - 8, True)

        @block.scalar
        def _(act):
            def par(dst, src, full):
                act.dma_start(dst, src).then_inc(full, 16)
            par(grow[G_MERGED:G_MERGED + N_DIFF, :, :], g_diff_sub.partition_broadcast(N_DIFF), gains_full)
            for at, g in ((G_MIX, g_mix_pre), (G_X, g_x_pre), (G_FFN, g_ffn_pre), (G_MEM, g_mem),
                          (G_MERGED + N_DIFF, g_sb_out), (G_MERGED + N_DIFF + N_SB, g_fox_out)):
                k = g.shape[1] // P
                par(grow[at:at + k, :, :], g.rearrange("l (k p) -> k l p", p=P), gains_full)
            for n in range(1, 4):
                par(xs[:, :, n * 512:(n + 1) * 512], x_v[:, :, n * 512:(n + 1) * 512], x_full[n])
            with nc.allow_non_contiguous_dma(reason="the forget gate's weights, once"):
                for n in range(DEPTH):
                    par(wfr[:, n, :, :], w_f_v[:, n, :, :], wf_full)
            act.wait_ge(raw_full[0], 32)
            par(mst[:, :, :], mem_v, mem_full)

            with act.Fori(0, DEPTH) as l:
                def split(ahead, c, width=WIDE):
                    s = c % RING
                    act.wait_ge(raw_full[s], l * (CHUNKS // RING * 32)
                                + ahead * (32 // RING)
                                + 32 * (c // RING + 1))
                    act.wait_ge(w_free, l * CHUNKS + ahead + (c + 1))
                    act.activation(wh[:, s, 0:width], raw[:, s, 0:width], ACT.Copy).then_inc(wh_ready, 1)

                def splits(ahead, c0, n, width=WIDE, hooks=None):
                    for k in range(n):
                        if hooks and k in hooks:
                            hooks[k]()
                        split(ahead, c0 + k, width)
                    if hooks and n in hooks:
                        hooks[n]()

                def square(n, src, total, wait=None):
                    if wait is not None:
                        act.wait_ge(*wait)
                    if n:
                        act.wait_ge(sq_done, l * SQUARES + n)
                    width = src.shape[-1]
                    act.activation(junk[:, 0:width], src, ACT.Square, accum_out=total).then_inc(sq_done, 1)

                def highs(t0, lo, hi, dst=None):
                    for g in range(lo, hi):
                        t, k = g % 2, g // 2 * 4
                        act.wait_ge(tp_gain, l * GROUPS + (t0 + g + 1))
                        act.activation((xTh if dst is None else dst)[:, k:k + 4, t * P:(t + 1) * P],
                                       R[:, g % 2, :].rearrange("p (k n) -> p k n", k=4), ACT.Copy)\
                           .then_inc(tp_high, 1)

                def drain_set(set_ahead, s, scale, dst, width):
                    for b in (0, 2):
                        wait_acc(act, l, set_ahead, s, b)
                        act.activation(dst(b // 2), acc[:, b, 0:width], ACT.Copy, scale=scale[:, 0:1])\
                           .then_inc(acc_free[b], 1)

                def drain_pair(i, pb):
                    act.wait_ge(rx_ready, l * 3 + 1)
                    drain_set(i, pb, rx, lambda a: pj[:, 0, a * 384:(a + 1) * 384], 384)

                def y_squares(s, q):
                    half = (s - S_OUT if s < S_MK else s - S_CO if s < S_FFN else s - S_DOWN)
                    for n, b in enumerate(ORDER):
                        wait_acc(act, l, 0, s, b)
                        at = 2 * half + b // 2
                        square(q + n, acc[:, b, :], ssy[:, b % 2, at:at + 1])

                def att_qk(g_, i):
                    head, dve, actn, scores, one = attention(g_, l, i)
                    scale = 64 ** -0.5 if g_ == 0 else HD ** -0.5
                    act.wait_ge(qkT_done, head(1))
                    act.activation(qkT[:, 0, 0:256], aux[:, 0, 0:256], ACT.Copy, scale=scale)
                    act.activation(qkT[:, 0, 256:512], aux[:, 0, 256:512], ACT.Copy).then_inc(qkT_act, 1)

                def att_exps_a(i, h):
                    head, dve, actn, scores, one = attention(0, l, i)
                    if h == 1:
                        act.wait_ge(dve_att, dve(12))
                    for m in range(2):
                        act.wait_ge(dve_att, dve(12 * h + 4 + 2 * m))
                        for t, c in enumerate((slice(0, P), slice(P, 3 * P))):
                            act.activation(E[:, m, c], Z[:, m, c], ACT.Exp,
                                           bias=nmax[:, 2 * h + m, t:t + 1],
                                           accum_out=rsum[:, 2 * h + m, t:t + 1]).then_inc(act_att, 1)

                def att_exps_c(i):
                    head, dve, actn, scores, one = attention(2, l, i)
                    for h in range(2):
                        act.wait_ge(dve_att, dve(6 + 2 * h))
                        for t, c in enumerate((slice(0, P), slice(P, 3 * P))):
                            act.activation(E[:, h, c], Z[:, h, c], ACT.Exp, bias=nmax[:, h, t:t + 1],
                                           accum_out=rsum[:, h, t:t + 1]).then_inc(act_att, 1)

                def att_log(i):
                    head, dve, actn, scores, one = attention(1, l, i)
                    steps = ((ACT.Abs, Z, 1.0, 0.0), (ACT.Exp, E, -1.0, 0.0), (ACT.Ln, E, 1.0, 1.0))
                    for n, (f, src, scale, bias) in enumerate(steps):
                        for h in range(2):
                            if n == 0:
                                act.wait_ge(dve_att, dve(h + 1))
                            else:
                                act.wait_ge(act_att, actn(2 * n - 2 + h + 1))
                            act.activation(E[:, h, 0:3 * P], src[:, h, 0:3 * P], f, bias=bias, scale=scale)\
                               .then_inc(act_att, 1)

                def att_exps_b(i):
                    head, dve, actn, scores, one = attention(1, l, i)
                    for h in range(2):
                        act.wait_ge(dve_att, dve(9 + h))
                        act.activation(E[:, h, 0:3 * P], Z[:, h, 0:3 * P], ACT.Exp).then_inc(act_att, 1)

                def att_pT(g_, i):
                    head, dve, actn, scores, one = attention(g_, l, i)
                    act.wait_ge(pT_done, head(1))
                    act.activation(pT[:, 0, 0:3 * P], aux[:, 0, 0:3 * P], ACT.Copy).then_inc(pT_act, 1)

                def att_hooks(g_, i, pb):
                    hooks = {3: lambda: drain_pair(i, pb)}
                    if g_ == 0:
                        hooks.update({7: lambda: att_qk(0, i), 10: lambda: att_exps_a(i, 0),
                                      12: lambda: att_exps_a(i, 1), 13: lambda: att_pT(0, i)})
                    elif g_ == 1:
                        hooks.update({4: lambda: att_qk(1, i), 7: lambda: att_log(i),
                                      10: lambda: att_exps_b(i), 12: lambda: att_pT(1, i)})
                    else:
                        hooks.update({4: lambda: att_qk(2, i), 7: lambda: att_exps_c(i),
                                      12: lambda: att_pT(2, i)})
                    return hooks

                def gate_log():
                    act.wait_ge(f_step, l * 6 + 4)
                    act.activation(fe[:, :, :], fz[:, :, :], ACT.Abs).then_inc(f_act, 1)
                    act.wait_ge(f_act, l * 4 + 2)
                    act.activation(fe[:, :, :], fe[:, :, :], ACT.Exp, scale=-1.0).then_inc(f_act, 1)
                    act.wait_ge(f_act, l * 4 + 3)
                    act.activation(fe[:, :, :], fe[:, :, :], ACT.Ln, bias=1.0).then_inc(f_act, 1)

                def mem_squares():
                    for t in range(NT):
                        square(Q_MEM + t, mst[:, t, :], ssm[:, t:t + 1], (mem_full, 16))

                def sines():
                    act.wait_ge(trig_ready, 2)
                    act.activation(sinb[:, :, :], trig[:, 2, :, :], ACT.Sin)
                    act.activation(cosb[:, :, :], trig[:, 3, :, :], ACT.Sin).then_inc(sin_ready, 1)
                    act.wait_ge(lam_step, l * 5 + 3)
                    act.activation(lame[:, :, :], lamd[:, :, :], ACT.Exp).then_inc(lam_exp, 1)

                def gate_weights():
                    act.wait_ge(wf_full, 16 * DEPTH)
                    act.activation(wfh[:, :, :], wfr[:, bass.ds(l, 1), :, :].rearrange("p a k c -> p (a k) c"),
                                   ACT.Copy).then_inc(f_act, 1)
                splits(0, 0, 1, PAIR_W)
                highs(T_X, 0, 1)
                splits(0, 1, 2, PAIR_W)
                highs(T_X, 1, 2)
                splits(0, 3, 1, PAIR_W)
                highs(T_X, 2, 4)
                splits(0, RING, KT - RING, PAIR_W, {
                    1: lambda: highs(T_X, 4, 6), 3: lambda: highs(T_X, 6, 8),
                    4: lambda: [square(Q_X + t, xs[:, t, :], ssx[:, t:t + 1]) for t in range(NT)],
                    5: gate_weights, 6: sines, 9: gate_log})

                for g_, n in ((0, PAIRS_A), (1, PAIRS_B), (2, PAIRS_C - 2)):
                    pb = (0, PAIRS_A, PAIRS_A + PAIRS_B)[g_]
                    with act.Fori(0, n) as i:
                        splits(i * KT, (pb + 1) * KT, KT, PAIR_W, att_hooks(g_, i, pb))

                def head_squares():
                    act.wait_ge(o_read, l * (2 * PAIRS) + 2 * (PAIRS_A + PAIRS_B))
                    for t in range(NT):
                        for h in range(N_DIFF):
                            n = t * N_DIFF + h
                            square(Q_A + n, mg[:, t, h * HD:(h + 1) * HD], ssh[:, n:n + 1])
                    for t in range(NT):
                        square(Q_B + t, mg[:, t, 4 * HD:10 * HD], ssh[:, 8 + t:9 + t])

                def fox_squares():
                    act.wait_ge(o_read, (l + 1) * (2 * PAIRS))
                    for t in range(NT):
                        square(Q_C + t, mg[:, t, 10 * HD:D], ssh[:, 10 + t:11 + t])
                hooks = att_hooks(2, PAIRS_C - 2, 0)
                hooks[3] = lambda: drain_pair(0, PAIRS - 2)
                hooks[9] = head_squares
                splits(0, K_OUT - KT, KT, PAIR_W, hooks)

                def mix_highs():
                    wait_acc(act, l, 0, PAIRS - 1, 3)
                    highs(T_MIX, 0, 2)
                    drain_pair(0, PAIRS - 1)
                    highs(T_MIX, 2, 4)
                splits(0, K_OUT, KT, WIDE, {
                    3: mix_highs, 5: lambda: att_qk(2, PAIRS_C - 1), 6: lambda: att_exps_c(PAIRS_C - 1),
                    8: lambda: att_pT(2, PAIRS_C - 1), 10: fox_squares,
                    11: lambda: highs(T_MIX, 4, 6), 12: lambda: highs(T_MIX, 6, 8)})
                splits(0, K_OUT + KT, KT, WIDE, {
                    3: lambda: y_squares(S_OUT, Q_OUT), 4: mem_squares,
                    **{5 + n: (lambda g: lambda: highs(T_MEM, g, g + 1, memTh))(n) for n in range(8)}})

                def x_squares(q, n):
                    act.wait_ge(x_upd[1], l * 12 + n)
                    for t in range(NT):
                        square(q + t, xs[:, t, :], ssx[:, t:t + 1])
                splits(0, K_MK, KT // 2, WIDE, {
                    3: lambda: y_squares(S_OUT + 1, Q_OUT2), 4: lambda: highs(T_CQ, 0, 2),
                    6: lambda: highs(T_CQ, 2, 4), 7: lambda: highs(T_CQ, 4, 6), 8: lambda: highs(T_CQ, 6, 8)})

                def drain_keys():
                    act.wait_ge(rm_ready, l + 1)
                    drain_set(0, S_MK, rm, lambda a: kv[:, 0, a * 256:(a + 1) * 256], 256)

                def drain_queries():
                    act.wait_ge(rx_ready, l * 3 + 2)
                    drain_set(0, S_CQ, rx, lambda a: pj[:, 0, a * 256:(a + 1) * 256], 256)

                def drain_values():
                    drain_set(0, S_MV, rm, lambda a: kv[:, 0, CW + a * 256:CW + (a + 1) * 256], 256)

                def x_qk(p):
                    act.wait_ge(x_tp, l * NCH + (2 * p + 1))
                    act.activation(qkT[:, 0, 0:256], aux[:, 0, 0:256], ACT.Copy, scale=HD ** -0.5)
                    act.activation(qkT[:, 0, 256:512], aux[:, 0, 256:512], ACT.Copy).then_inc(x_act, 1)

                def x_exps(p):
                    for h in range(2):
                        act.wait_ge(x_max, l * NCH + (2 * p + h + 1))
                        for t in range(NT):
                            act.activation((E if p == 0 else Z)[:, h, t * 256:(t + 1) * 256],
                                           aux[:, 1 + h, t * 256:(t + 1) * 256], ACT.Exp,
                                           bias=nmax[:, 2 * p + h, t:t + 1],
                                           accum_out=rsum[:, 2 * p + h, t:t + 1]).then_inc(x_exp, 1)

                def x_pTs(p):
                    act.wait_ge(x_pT, l * NCH + (2 * p + 1))
                    act.activation((pT if p == 0 else R)[:, 0, :], aux[:, 0 if p == 0 else 1, :], ACT.Copy)\
                       .then_inc(x_pTa, 1)
                splits(0, K_CQ, KT // 2, WIDE, {3: drain_keys, 4: lambda: x_squares(Q_X2, 8)})
                splits(0, K_MV, KT // 2, WIDE, {
                    3: drain_queries, 4: lambda: x_qk(0), 5: lambda: x_exps(0), 6: lambda: x_qk(1),
                    7: lambda: x_exps(1), 8: lambda: x_pTs(0)})
                splits(0, K_CO, 3)
                drain_values()
                x_pTs(1)
                splits(0, K_CO + 3, 1)
                for t in range(NT):
                    act.wait_ge(tp_gain, l * GROUPS + (T_CO + t + 1))
                    act.activation(xTh[:, 0:4, t * P:(t + 1) * P],
                                   R[:, t, :].rearrange("p (k n) -> p k n", k=4), ACT.Copy)\
                       .then_inc(tp_high, 1)
                splits(0, K_CO + 4, 3)
                y_squares(S_CO, Q_CO)
                splits(0, K_CO + 7, 1)
                y_squares(S_CO + 1, Q_CO + 4)
                splits(0, K_FFN, 1)
                highs(T_FFN, 0, 1)
                splits(0, K_FFN + 1, 2)
                highs(T_FFN, 1, 2)
                splits(0, K_FFN + 3, 1)
                highs(T_FFN, 2, 4)
                splits(0, K_FFN + RING, KT - RING, WIDE, {
                    1: lambda: highs(T_FFN, 4, 6), 3: lambda: highs(T_FFN, 6, 8),
                    6: lambda: x_squares(Q_X3, 12)})

                def silu(set_ahead, s):
                    act.wait_ge(rx_ready, l * 3 + 3)
                    for t in range(NT):
                        wait_acc(act, l, set_ahead, s, t)
                        act.activation(Z[:, t, :], acc[:, t, :], ACT.Silu, scale=rx[:, t:t + 1])\
                           .then_inc(acc_free[t], 1)

                def hidden(ahead, j):
                    act.wait_ge(hT_done, l * (2 * FB) + ahead * 2 + 2 * j + 1)
                    act.activation(hidT[:, bass.ds(ahead * 4 + 4 * j, 4), 0:P],
                                   aux[:, 0, :].rearrange("p (k n) -> p k n", k=4), ACT.Copy)\
                       .then_inc(hT_act, 1)
                with act.Fori(0, FB - 1) as j:
                    splits(j * KT, K_FFN + KT, KT, WIDE,
                           {3: lambda: silu(j, S_FFN), 7: lambda: hidden(j, 0)})

                def stage(ahead, s, g, slot):
                    act.wait_ge(w_free, l * CHUNKS + ahead * 4 + (K_DOWN + s * G + 4 * g))
                    act.activation(xTh[:, 4 * slot:4 * slot + 4, :],
                                   hidT[:, bass.ds(ahead * 4 + 4 * g, 4), :], ACT.Copy).then_inc(st_high, 1)
                for s in range(2):
                    base = K_DOWN + s * G
                    if s == 0:
                        act.wait_ge(hT_dve, l * FB + (FB - 1))
                    stage(0, s, 0, 2)
                    splits(0, base, 3)
                    if s == 0:
                        silu(0, S_FFN + FB - 1)
                    else:
                        y_squares(S_DOWN, Q_DOWN)
                    splits(0, base + 3, 1)
                    if s == 0:
                        stage(0, s, 1, 1)
                        splits(0, base + 4, 3)
                        hidden(0, FB - 1)
                        splits(0, base + 7, 1)
                        stage(0, s, 2, 0)
                        splits(0, base + 8, 4)
                        act.wait_ge(hT_dve, l * FB + FB)
                        act.wait_ge(hT_act, l * FB + FB)
                    lo = 3 if s == 0 else 1
                    with act.Fori(0, (FB - lo) // 2) as g:
                        stage(g * 2, s, lo, 1)
                        splits(g * 8, base + 4 * lo, 4)
                        stage(g * 2, s, lo + 1, 0)
                        splits(g * 8, base + 4 * lo + 4, 4)
                y_squares(S_DOWN + 1, Q_DOWN + 4)

        @block.vector
        def _(dve):
            dve.memset(fs[:, 0, 1:2], 0.0).then_inc(x_upd[0], 4)
            dve.memset(mhalf[:, :], -0.5).then_inc(wl_ready, RING)
            dve.memset(fs[:, 0, 0:1], 0.0).then_inc(w_free, RING)
            for b in range(4):
                dve.memset(fe[:, 0, b:b + 1], 0.0).then_inc(acc_free[b], 1)
            for n in range(DEPTH):
                dve.wait_ge(boot_pe, n + 1)
                dve.tensor_copy(gT[:, n, :], aux[:, 4 - DEPTH + n, 0:GAINS]).then_inc(boot, 1)
            dve.wait_ge(boot, DEPTH)
            for n in range(DEPTH):
                v = gT[:, n, G_MERGED:G_MERGED + N_DIFF]
                dve.tensor_scalar(v, v, 1.0 - lam_init[n], None, ALU.mult).then_inc(boot, 1)
            dve.wait_ge(boot, 2 * DEPTH)

            with dve.Fori(0, DEPTH) as l:
                def splits(ahead, c0, n, width=WIDE, hooks=None):
                    for k in range(n):
                        if hooks and k in hooks:
                            hooks[k]()
                        s = (c0 + k) % RING
                        dve.wait_ge(wh_ready, l * CHUNKS + ahead + (c0 + k + 1))
                        dve.tensor_tensor(wl[:, s, 0:width], raw[:, s, 0:width],
                                          wh[:, s, 0:width].bitcast(F32), ALU.subtract)\
                           .then_inc(wl_ready, 1)
                    if hooks and n in hooks:
                        hooks[n]()

                def gain(n, t, k, goff, reused=False):
                    dve.wait_ge(tp_done, l * GROUPS + (n + 1))
                    src = aux[:, n % 4, :]
                    dst = R[:, t, :]
                    if reused:
                        dve.wait_ge(xT_ready, lows(l, n - 2))
                    if goff is None:
                        dve.tensor_copy(dst, src).then_inc(tp_gain, 1)
                    else:
                        g = gT[:, bass.ds(l, 1), goff + k:goff + k + 4].rearrange("p a k -> p (a k)")
                        dve.tensor_tensor(dst.rearrange("p (k n) -> p k n", k=4),
                                          src.rearrange("p (k n) -> p k n", k=4),
                                          g.unsqueeze(2).to_broadcast([P, 4, P]), ALU.mult)\
                           .then_inc(tp_gain, 1)

                def low(n, t, k):
                    dve.wait_ge(tp_high, l * GROUPS + (n + 1))
                    tok = slice(t * P, (t + 1) * P)
                    dve.tensor_tensor(xTl[:, k:k + 4, tok], R[:, t, :].rearrange("p (k n) -> p k n", k=4),
                                      xTh[:, k:k + 4, tok].bitcast(F32), ALU.subtract)\
                       .then_inc(xT_ready, 1)

                def groups(t0, lo, hi, goff):
                    for g in range(lo, hi):
                        gain(t0 + g, g % 2, g // 2 * 4, goff, g > 1)
                        if g > lo:
                            low(t0 + g - 1, (g - 1) % 2, (g - 1) // 2 * 4)
                    low(t0 + hi - 1, (hi - 1) % 2, (hi - 1) // 2 * 4)

                def update(n, t, *blocks):
                    dve.wait_ge(ry_ready[t], l * 3 + (n + t))
                    for b in blocks:
                        if n == 0:
                            dve.wait_ge(x_full[b], 16)
                        c = slice(b * 512, (b + 1) * 512)
                        dve.scalar_tensor_tensor(xs[:, t, c], mg[:, t, c], ry[:, t:t + 1], xs[:, t, c],
                                                 ALU.mult, ALU.add).then_inc(x_upd[t], 1)

                def drain_set(set_ahead, s, scale, dst, width):
                    for b in (1, 3):
                        wait_acc(dve, l, set_ahead, s, b)
                        dve.tensor_scalar(dst(b // 2), acc[:, b, 0:width], scale[:, 1:2], None, ALU.mult)\
                           .then_inc(acc_free[b], 1)

                def drain_pair(i, pb):
                    dve.wait_ge(rx_ready, l * 3 + 1)
                    drain_set(i, pb, rx, lambda a: pj[:, 1, a * 384:(a + 1) * 384], 384)

                def drain_y(half, q, n, tiles=(0, 1)):
                    dve.wait_ge(gbc_full, l * 48 + 16 * (n + 1))
                    for at, b in enumerate(ORDER):
                        if b % 2 not in tiles:
                            continue
                        dve.wait_ge(sq_done, l * SQUARES + (q + at + 1))
                        c = slice((2 * half + b // 2) * 512, (2 * half + b // 2 + 1) * 512)
                        dve.tensor_tensor(mg[:, b % 2, c], acc[:, b, :], gbc[:, c], ALU.mult)\
                           .then_inc(acc_free[b], 1)

                def sum_y(t):
                    dve.tensor_reduce(ssy2[:, t:t + 1], ssy[:, t, :], AX_X, ALU.add).then_inc(ssy_ready[t], 1)

                def turn(t0, goff, n, c0, width):
                    gain(t0, 0, 0, goff)
                    splits(0, c0, 1, width)
                    low(t0, 0, 0)
                    update(n, 1, 0)
                    splits(0, c0 + 1, 1, width)
                    if n:
                        update(n, 0, 1)
                    splits(0, c0 + 2, 1, width)
                    gain(t0 + 1, 1, 0, goff)
                    splits(0, c0 + 3, 1, width)
                    low(t0 + 1, 1, 0)
                    update(n, 1, 1)
                    groups(t0, 2, 4, goff)
                    if n:
                        update(n, 0, 2, 3)
                    update(n, 1, 2, 3)

                def att_qk(g_, i):
                    head, dven, actn, scores, one = attention(g_, l, i)
                    scale = 64 ** -0.5 if g_ == 0 else HD ** -0.5
                    dve.wait_ge(qkT_done, head(2))
                    dve.tensor_scalar(qkT[:, 1, 0:256], aux[:, 3, 0:256], scale, None, ALU.mult)
                    dve.tensor_copy(qkT[:, 1, 256:512], aux[:, 3, 256:512]).then_inc(qkT_dve, 1)

                def neg_max(m, src):
                    dve.tensor_reduce(nmax[:, m, 0:1], src[:, 0:P], AX_X, ALU.max, negate=True)\
                       .then_inc(dve_att, 1)
                    dve.tensor_reduce(nmax[:, m, 1:2], src[:, P:3 * P], AX_X, ALU.max, negate=True)\
                       .then_inc(dve_att, 1)

                def att_max_a(i, h):
                    head, dven, actn, scores, one = attention(0, l, i)
                    for m in range(2):
                        dve.wait_ge(s_done, scores(2 * h + m + 1))
                        dve.tensor_tensor(Z[:, m, 0:3 * P], aux[:, 1 + m, 0:3 * P], causal, ALU.add)\
                           .then_inc(dve_att, 1)
                    for m in range(2):
                        dve.wait_ge(dve_att, dven(12 * h + m + 1))
                        neg_max(2 * h + m, Z[:, m, :])

                def att_mix_a(i, h):
                    head, dven, actn, scores, one = attention(0, l, i)
                    dve.wait_ge(act_att, actn(4 * h + 4))
                    dve.reciprocal(rinv[:, 2 * h:2 * h + 2, :], rsum[:, 2 * h:2 * h + 2, :])\
                       .then_inc(dve_att, 1)
                    dve.wait_ge(dve_att, dven(12 * h + 7))
                    dve.tensor_scalar(rinv[:, 2 * h + 1, :], rinv[:, 2 * h + 1, :], nlam[:, bass.ds(l, 1)],
                                      None, ALU.mult).then_inc(dve_att, 1)
                    parts = (slice(0, P), slice(P, 3 * P))
                    for t, c in enumerate(parts):
                        dve.tensor_scalar(R[:, h, c], E[:, 0, c], rinv[:, 2 * h, t:t + 1], None, ALU.mult)\
                           .then_inc(dve_att, 1)
                    dve.wait_ge(dve_att, dven(12 * h + 10))
                    for t, c in enumerate(parts):
                        dve.scalar_tensor_tensor(R[:, h, c], E[:, 1, c], rinv[:, 2 * h + 1, t:t + 1],
                                                 R[:, h, c], ALU.mult, ALU.add).then_inc(dve_att, 1)

                def att_mask_b(i):
                    head, dven, actn, scores, one = attention(1, l, i)
                    for h in range(2):
                        dve.wait_ge(s_done, scores(h + 1))
                        dve.tensor_tensor(Z[:, h, 0:3 * P], aux[:, 1 + h, 0:3 * P], strict, ALU.add)\
                           .then_inc(dve_att, 1)

                def att_sums_b(i):
                    head, dven, actn, scores, one = attention(1, l, i)
                    for h in range(2):
                        dve.wait_ge(act_att, actn(5 + h))
                        dve.scalar_tensor_tensor(E[:, h, 0:3 * P], Z[:, h, 0:3 * P], 0.0, E[:, h, 0:3 * P],
                                                 ALU.max, ALU.add).then_inc(dve_att, 1)
                    for h in range(2):
                        dve.wait_ge(dve_att, dven(3 + h))
                        for lo, hi in ((0, P), (P, 3 * P)):
                            back = E[:, h, lo:hi][:, ::-1]
                            dve.tensor_tensor_scan(R[:, h, lo:hi][:, ::-1], back, back, 0.0,
                                                   ALU.add, ALU.max).then_inc(dve_att, 1)
                    for h in range(2):
                        dve.wait_ge(dve_att, dven(6 + 2 * h))
                        dve.tensor_tensor(Z[:, h, 0:3 * P], Z[:, h, 0:3 * P], R[:, h, 0:3 * P],
                                          ALU.subtract).then_inc(dve_att, 1)

                def att_max_c(i):
                    head, dven, actn, scores, one = attention(2, l, i)
                    for h in range(2):
                        dve.wait_ge(s_done, scores(h + 1))
                        for t, c in enumerate((slice(0, P), slice(P, 3 * P))):
                            dve.scalar_tensor_tensor(Z[:, h, c], aux[:, 1 + h, c], cumq[:, h, t:t + 1],
                                                     causal[:, c], ALU.add, ALU.add).then_inc(dve_att, 1)
                    for h in range(2):
                        dve.wait_ge(dve_att, dven(2 * h + 2))
                        neg_max(h, Z[:, h, :])

                def att_inv_c(i):
                    head, dven, actn, scores, one = attention(2, l, i)
                    for h in range(2):
                        dve.wait_ge(act_att, actn(2 * h + 2))
                        dve.reciprocal(rinv[:, h, :], rsum[:, h, :]).then_inc(dve_att, 1)

                def att_pT(g_, i):
                    head, dven, actn, scores, one = attention(g_, l, i)
                    dve.wait_ge(pT_done, head(2))
                    dve.tensor_copy(pT[:, 1, 0:3 * P], aux[:, 2, 0:3 * P]).then_inc(pT_dve, 1)

                def att_out(g_, i):
                    head, dven, actn, scores, one = attention(g_, l, i)
                    col = (0, N_DIFF * HD, (N_DIFF + N_SB) * HD)[g_]
                    if g_ == 2:
                        dve.wait_ge(dve_att, dven(10))
                    dve.wait_ge(o_done, head(2))
                    for h in range(2):
                        at = bass.ds(i * (2 * HD) + (col + h * HD), HD)
                        o = aux[:, 3, h * 256:(h + 1) * 256].rearrange("p (t n) -> p t n", t=NT)
                        if g_ < 2:
                            dve.tensor_copy(mg[:, :, at], o).then_inc(o_read, 1)
                        else:
                            dve.tensor_tensor(mg[:, :, at], o, rinv[:, h, :].unsqueeze(2)
                                              .to_broadcast([P, NT, HD]), ALU.mult).then_inc(o_read, 1)

                def att_hooks(g_, i, pb):
                    hooks = {3: lambda: drain_pair(i, pb)}
                    if g_ == 0:
                        hooks.update({7: lambda: att_qk(0, i), 9: lambda: att_max_a(i, 0),
                                      10: lambda: att_mix_a(i, 0), 11: lambda: att_max_a(i, 1),
                                      13: lambda: att_mix_a(i, 1), 15: lambda: att_pT(0, i),
                                      16: lambda: att_out(0, i)})
                    elif g_ == 1:
                        hooks.update({4: lambda: att_qk(1, i), 6: lambda: att_mask_b(i),
                                      9: lambda: att_sums_b(i), 12: lambda: att_pT(1, i),
                                      14: lambda: att_out(1, i)})
                    else:
                        hooks.update({4: lambda: att_qk(2, i), 6: lambda: att_max_c(i),
                                      9: lambda: att_inv_c(i), 12: lambda: att_pT(2, i),
                                      14: lambda: att_out(2, i)})
                    return hooks

                def gate_logits():
                    dve.wait_ge(f_done, l * 2 + 2)
                    dve.wait_ge(rx_ready, l * 3 + 1)
                    for t in range(NT):
                        dve.scalar_tensor_tensor(
                            fz[:, t, :], aux[:, 3, t * P:t * P + N_FOX], rx[:, t:t + 1],
                            bfb[:, bass.ds(l, 1), :].rearrange("p a c -> p (a c)"),
                            ALU.mult, ALU.add).then_inc(f_step, 1)
                    dve.wait_ge(f_step, l * 6 + 4)
                    dve.tensor_scalar(fs[:, :, :], fz[:, :, :], -1.0, 0.0, ALU.mult, ALU.max)\
                       .then_inc(f_step, 1)

                def gate_sum():
                    dve.wait_ge(f_step, l * 6 + 5)
                    dve.wait_ge(f_act, l * 4 + 4)
                    dve.tensor_tensor(nlf[:, :, :].rearrange("p c t -> p t c"), fs[:, :, :], fe[:, :, :],
                                      ALU.add).then_inc(f_step, 1)

                def gate_cum():
                    dve.wait_ge(cum_done, l + 1)
                    for t in range(NT):
                        m = dve.tensor_scalar(cum[:, :, t], aux[:, 2, t * 8:t * 8 + N_FOX], -1.0, None,
                                              ALU.mult)
                    m.then_inc(cum_ready, 1)

                def lambdas():
                    dve.wait_ge(par_full, 16 * N_PAR)
                    for n in range(2):
                        dve.tensor_tensor(lamp[:, n, :], lamr[:, 2 * n, :], lamr[:, 2 * n + 1, :], ALU.mult)\
                           .then_inc(lam_step, 1)
                    dve.wait_ge(lam_step, l * 5 + 2)
                    dve.tensor_reduce(lamd[:, :, :], lamp[:, :, :].rearrange("p n (l d) -> p (n l) d", l=DEPTH),
                                      AX_X, ALU.add).then_inc(lam_step, 1)

                def lambdas_end():
                    dve.wait_ge(lam_exp, l + 1)
                    dve.tensor_tensor(lamn[:, :], lame[:, 1, :], lame[:, 0, :], ALU.subtract)\
                       .then_inc(lam_step, 1)
                    dve.wait_ge(lam_step, l * 5 + 4)
                    for n in range(DEPTH):
                        m = dve.tensor_scalar(nlam[:, n:n + 1], lamn[:, n:n + 1], -lam_init[n], None, ALU.add)
                    m.then_inc(lam_step, 1)

                def gate_low():
                    dve.wait_ge(f_act, l * 4 + 1)
                    dve.tensor_tensor(wfl[:, :, :], wfr[:, bass.ds(l, 1), :, :].rearrange("p a k c -> p (a k) c"),
                                      wfh[:, :, :].bitcast(F32), ALU.subtract).then_inc(f_step, 1)

                def gate_out():
                    dve.wait_ge(f_done, l * 2 + 1)
                    dve.tensor_copy(fT, aux[0:N_FOX, 3, 0:NT * P]).then_inc(f_step, 1)
                turn(T_X, G_MIX, 0, 0, PAIR_W)
                splits(0, RING, KT - RING, PAIR_W, {
                    1: lambda: groups(T_X, 4, 6, G_MIX), 3: lambda: groups(T_X, 6, 8, G_MIX),
                    4: lambdas, 5: gate_low, 6: lambdas_end, 7: gate_out, 8: gate_logits, 9: gate_sum,
                    12: gate_cum})

                for g_, n in ((0, PAIRS_A), (1, PAIRS_B), (2, PAIRS_C - 2)):
                    pb = (0, PAIRS_A, PAIRS_A + PAIRS_B)[g_]
                    with dve.Fori(0, n) as i:
                        splits(i * KT, (pb + 1) * KT, KT, PAIR_W, att_hooks(g_, i, pb))

                def norm_ab():
                    dve.wait_ge(rh_ready, l * 2 + 1)
                    for t in range(NT):
                        v = mg[:, t, 0:N_DIFF * HD].rearrange("p (h n) -> p h n", n=HD)
                        r = rh[:, t * N_DIFF:(t + 1) * N_DIFF].unsqueeze(2).to_broadcast([P, N_DIFF, HD])
                        m = dve.tensor_tensor(v, v, r, ALU.mult)
                    m.then_inc(mg_ready, 1)
                    for t in range(NT):
                        v = mg[:, t, 4 * HD:10 * HD]
                        dve.tensor_scalar(v, v, rh[:, 8 + t:9 + t], None, ALU.mult).then_inc(mg_ready, 1)

                def norm_c():
                    dve.wait_ge(rh_ready, l * 2 + 2)
                    for t in range(NT):
                        v = mg[:, t, 10 * HD:D]
                        dve.tensor_scalar(v, v, rh[:, 10 + t:11 + t], None, ALU.mult).then_inc(mg_ready, 1)
                hooks = att_hooks(2, PAIRS_C - 2, 0)
                hooks[3] = lambda: drain_pair(0, PAIRS - 2)
                hooks[16] = norm_ab
                splits(0, K_OUT - KT, KT, PAIR_W, hooks)

                def mix_first():
                    groups(T_MIX, 0, 2, G_MERGED)
                    drain_pair(0, PAIRS - 1)
                    groups(T_MIX, 2, 4, G_MERGED)

                def mem_gain(g):
                    if g > 1:
                        dve.wait_ge(mem_low, l * 8 + g - 1)
                    gain(T_MEM + g, g % 2, g // 2 * 4, G_MEM)
                last = PAIRS_C - 1
                splits(0, K_OUT, KT, WIDE, {
                    3: mix_first, 5: lambda: (att_qk(2, last), att_max_c(last)), 7: lambda: att_inv_c(last),
                    8: lambda: att_pT(2, last), 9: lambda: att_out(2, last), 10: norm_c,
                    11: lambda: groups(T_MIX, 4, 8, G_MERGED)})
                splits(0, K_OUT + KT, KT, WIDE, {
                    3: lambda: drain_y(0, Q_OUT, 0),
                    **{5 + n: (lambda g: lambda: mem_gain(g))(n) for n in range(8)}})

                def drain_keys():
                    dve.wait_ge(rm_ready, l + 1)
                    drain_set(0, S_MK, rm, lambda a: kv[:, 1, a * 256:(a + 1) * 256], 256)

                def drain_queries():
                    dve.wait_ge(rx_ready, l * 3 + 2)
                    drain_set(0, S_CQ, rx, lambda a: pj[:, 1, a * 256:(a + 1) * 256], 256)

                def drain_values():
                    drain_set(0, S_MV, rm, lambda a: kv[:, 1, CW + a * 256:CW + (a + 1) * 256], 256)

                def x_qk(p):
                    dve.wait_ge(x_tp, l * NCH + (2 * p + 2))
                    dve.tensor_scalar(qkT[:, 1, 0:256], aux[:, 3, 0:256], HD ** -0.5, None, ALU.mult)
                    dve.tensor_copy(qkT[:, 1, 256:512], aux[:, 3, 256:512]).then_inc(x_dve, 1)

                def x_maxs(p):
                    for h in range(2):
                        dve.wait_ge(x_s, l * NCH + (2 * p + h + 1))
                        dve.tensor_reduce(nmax[:, 2 * p + h, :],
                                          aux[:, 1 + h, :].rearrange("p (t n) -> p t n", t=NT),
                                          AX_X, ALU.max, negate=True).then_inc(x_max, 1)

                def x_pTs(p):
                    dve.wait_ge(x_pT, l * NCH + (2 * p + 2))
                    dve.tensor_copy((pT if p == 0 else R)[:, 1, :], aux[:, 3 if p == 0 else 2, :])\
                       .then_inc(x_pTd, 1)

                def x_inverse():
                    dve.wait_ge(x_exp, l * (2 * NCH) + 2 * NCH)
                    dve.reciprocal(rinv[:, :, :], rsum[:, :, :]).then_inc(x_inv, 1)

                def keys_y():
                    for t in range(NT):
                        drain_y(1, Q_OUT2, 0, (t,))
                        sum_y(t)

                def x2_groups(*which):
                    for g in which:
                        if g == 0:
                            update(1, 0, 0)
                            update(1, 1, 0)
                        groups(T_CQ, g, g + 2, G_X)
                        if g < 6:
                            update(1, 0, g // 2 + 1)
                            update(1, 1, g // 2 + 1)
                splits(0, K_MK, KT // 2, WIDE, {
                    3: keys_y, 4: lambda: x2_groups(0), 5: lambda: x2_groups(2),
                    6: lambda: x2_groups(4), 8: lambda: x2_groups(6)})
                splits(0, K_CQ, KT // 2, WIDE, {3: drain_keys})
                splits(0, K_MV, KT // 2, WIDE, {
                    3: drain_queries, 4: lambda: x_qk(0), 5: lambda: x_maxs(0), 6: lambda: x_qk(1),
                    7: lambda: x_maxs(1), 8: lambda: x_pTs(0)})
                splits(0, K_CO, 3)
                drain_values()
                x_pTs(1)
                x_inverse()
                splits(0, K_CO + 3, 1)
                dve.wait_ge(x_inv, l + 1)
                for p in range(2):
                    dve.wait_ge(x_o, l * 2 + (p + 1))
                    for h in range(2):
                        m = dve.tensor_tensor(
                            mg[:, :, (2 * p + h) * HD:(2 * p + h + 1) * HD],
                            aux[:, (0, 3)[p], h * 256:(h + 1) * 256].rearrange("p (t n) -> p t n", t=NT),
                            rinv[:, 2 * p + h, :].unsqueeze(2).to_broadcast([P, NT, HD]), ALU.mult)
                    m.then_inc(x_or, 1)
                for t in range(NT):
                    gain(T_CO + t, t, 0, None)
                for t in range(NT):
                    low(T_CO + t, t, 0)
                splits(0, K_CO + 4, 3)
                drain_y(0, Q_CO, 1)
                splits(0, K_CO + 7, 1)
                drain_y(1, Q_CO + 4, 1, (0,))
                sum_y(0)
                update(2, 0, 0)
                drain_y(1, Q_CO + 4, 1, (1,))
                sum_y(1)
                turn(T_FFN, G_FFN, 2, K_FFN, WIDE)
                splits(0, K_FFN + RING, KT - RING, WIDE, {
                    1: lambda: groups(T_FFN, 4, 6, G_FFN), 3: lambda: groups(T_FFN, 6, 8, G_FFN)})

                def product(set_ahead, s):
                    dve.wait_ge(rx_ready, l * 3 + 3)
                    for t in range(NT):
                        wait_acc(dve, l, set_ahead, s, 2 + t)
                        dve.wait_ge(acc_free[t], l * SETS + set_ahead + (s + 2))
                        dve.scalar_tensor_tensor(E[:, t, :], acc[:, 2 + t, :], rx[:, t:t + 1], Z[:, t, :],
                                                 ALU.mult, ALU.mult).then_inc(acc_free[2 + t], 1)

                def hidden(ahead, j):
                    dve.wait_ge(hT_done, l * (2 * FB) + ahead * 2 + 2 * j + 2)
                    dve.tensor_copy(hidT[:, bass.ds(ahead * 4 + 4 * j, 4), P:2 * P],
                                    aux[:, 1, :].rearrange("p (k n) -> p k n", k=4)).then_inc(hT_dve, 1)
                with dve.Fori(0, FB - 1) as j:
                    splits(j * KT, K_FFN + KT, KT, WIDE,
                           {3: lambda: product(j, S_FFN), 7: lambda: hidden(j, 0)})

                def stage(ahead, s, g, slot):
                    dve.wait_ge(st_high, l * (2 * FB) + ahead + (s * FB + g + 1))
                    dve.tensor_tensor(xTl[:, 4 * slot:4 * slot + 4, :],
                                      hidT[:, bass.ds(ahead * 4 + 4 * g, 4), :],
                                      xTh[:, 4 * slot:4 * slot + 4, :].bitcast(F32), ALU.subtract)\
                       .then_inc(st_ready, 1)
                for s in range(2):
                    base = K_DOWN + s * G
                    stage(0, s, 0, 2)
                    splits(0, base, 3)
                    if s == 0:
                        product(0, S_FFN + FB - 1)
                    else:
                        drain_y(0, Q_DOWN, 2)
                    splits(0, base + 3, 1)
                    if s == 0:
                        stage(0, s, 1, 1)
                        splits(0, base + 4, 3)
                        hidden(0, FB - 1)
                        splits(0, base + 7, 1)
                        stage(0, s, 2, 0)
                        splits(0, base + 8, 4)
                    lo = 3 if s == 0 else 1
                    with dve.Fori(0, (FB - lo) // 2) as g:
                        stage(g * 2, s, lo, 1)
                        splits(g * 8, base + 4 * lo, 4)
                        stage(g * 2, s, lo + 1, 0)
                        splits(g * 8, base + 4 * lo + 4, 4)
                drain_y(1, Q_DOWN + 4, 2, (0,))
                sum_y(0)
                update(3, 0, 0, 1, 2, 3)
                drain_y(1, Q_DOWN + 4, 2, (1,))
                sum_y(1)
            dve.wait_ge(ry_ready[1], DEPTH * 3 + 1)
            for b in range(4):
                c = slice(b * 512, (b + 1) * 512)
                dve.scalar_tensor_tensor(xs[:, 1, c], mg[:, 1, c], ry[:, 1:2], xs[:, 1, c],
                                         ALU.mult, ALU.add).then_inc(x_upd[1], 1)

        @block.gpsimd
        def _(pool):
            pool.memset(eps[:, :], EPS).then_inc(boot_pool, 1)
            pool.memset(inv_w[:, IW_D:IW_A], 1.0 / D).then_inc(boot_pool, 1)
            pool.memset(inv_w[:, IW_A:IW_A + NT * N_DIFF], 1.0 / HD).then_inc(boot_pool, 1)
            pool.memset(inv_w[:, IW_A + NT * N_DIFF:IW_C], 1.0 / (N_SB * HD)).then_inc(boot_pool, 1)
            pool.memset(inv_w[:, IW_C:IW_C + NT], 1.0 / (N_FOX * HD)).then_inc(boot_pool, 1)
            pool.memset(mg[:, 1, :], 0.0).then_inc(boot_pool, 1)
            pool.wait_ge(boot_pool, 6)
            pool.memset(ry[:, 1:2], 0.0).then_inc(ry_ready[1], 1)
            def load(dst, src, full):
                pool.dma_start(dst, src).then_inc(full, 16)
            with nc.allow_non_contiguous_dma(reason="small parameters, once"):
                load(posi[:, :], positions.rearrange("b (t p) -> p (b t)", p=P), par_full)
                load(bfb[:, :, :], b_f.partition_broadcast(P), par_full)
                for n, v in enumerate((lam_q1, lam_k1, lam_q2, lam_k2)):
                    load(lamr[:, n, :], v.rearrange("l d -> (l d)").partition_broadcast(P), par_full)
            pool.wait_ge(wl_ready, RING)
            pool.wait_ge(cst_full, 16)
            pool.wait_ge(par_full, 16 * N_PAR)
            two_pi = 2.0 * math.pi
            c1 = 6.28125
            c2 = float(np.float32(two_pi - c1))
            c3 = two_pi - c1 - c2
            big = 12582912.0
            angle, u, w = trig[:, 0, :, :], trig[:, 1, :, :], trig[:, 4, :, :]
            steps = [lambda: pool.tensor_copy(posf[:, :], posi[:, :])]
            steps += [lambda t=t: pool.tensor_scalar(trig[:, 0, t, :], freq, posf[:, t:t + 1], None, ALU.mult)
                      for t in range(NT)]
            for which, shift in ((2, 0.0), (3, 0.25)):
                r = trig[:, which, :, :]
                steps += [
                    lambda shift=shift: pool.tensor_scalar(u, angle, 1.0 / two_pi, shift, ALU.mult, ALU.add),
                    lambda: pool.tensor_scalar(u, u, big, None, ALU.add),
                    lambda: pool.tensor_scalar(u, u, -big, None, ALU.add)]
                for n, part in enumerate((c1, c2, c3)):
                    steps += [lambda part=part: pool.tensor_scalar(w, u, -part, None, ALU.mult),
                              lambda r=r, n=n: pool.tensor_tensor(r, r if n else angle, w, ALU.add)]
                steps += [lambda r=r, shift=shift: pool.tensor_scalar(r, r, two_pi * shift, None, ALU.add),
                          lambda r=r: pool.tensor_scalar(r, r, 3.1415925, -3.1415925, ALU.min, ALU.max)]
            for n, step in enumerate(steps):
                step().then_inc(boot_trig, 1)
                pool.wait_ge(boot_trig, n + 1)
            pool.memset(posf[:, :], 0.0).then_inc(trig_ready, 2)

            with pool.Fori(0, DEPTH) as l:
                def rms(n, row, dst, src, at, done, col=0):
                    w = src.shape[-1]
                    m = msx[:, row, col:col + w]
                    pool.tensor_tensor(m, src, inv_w[:, at:at + w], ALU.mult).then_inc(ms, 1)
                    pool.wait_ge(ms, l * (2 * NORMS) + 2 * n + 1)
                    pool.tensor_tensor(m, m, eps[:, 0:w], ALU.add).then_inc(ms, 1)
                    pool.wait_ge(ms, l * (2 * NORMS) + 2 * n + 2)
                    pool.tensor_tensor(dst, m, mhalf[:, 0:w], ALU.pow).then_inc(done, 1)

                def rms_x(n, row, q):
                    pool.wait_ge(sq_done, l * SQUARES + q + NT)
                    rms(n, row, rx[:, :], ssx[:, :], IW_D, rx_ready)

                def rms_y(n, row, k):
                    for t in range(NT):
                        pool.wait_ge(ssy_ready[t], l * 3 + k + 1)
                        rms(n + t, row, ry[:, t:t + 1], ssy2[:, t:t + 1], IW_D, ry_ready[t], t)
                rms_x(0, 0, Q_X)
                with pool.Fori(0, PAIRS_A) as i:
                    pool.wait_ge(sin_ready, l + 1)
                    for b in range(4):
                        pool.wait_ge(acc_free[b], l * SETS + i + 2)
                    for t in range(NT):
                        v = pj[:, t, 0:512].rearrange("p (b n) -> p b n", n=ROT)
                        v4 = pj[:, t, 0:512].rearrange("p (b s n) -> p b s n", s=2, n=ROT)
                        a = R[:, 0, :].rearrange("p (b n) -> p b n", n=ROT)
                        a4 = R[:, 0, :].rearrange("p (b s n) -> p b s n", s=2, n=ROT)
                        b4 = R[:, 1, :].rearrange("p (b s n) -> p b s n", s=2, n=ROT)
                        cosv = cosb[:, t, :].unsqueeze(1)
                        sinv = sinb[:, t, :].unsqueeze(1).to_broadcast([P, 8, ROT])
                        n0 = l * (10 * PAIRS_A) + i * 10 + 5 * t
                        if t:
                            pool.wait_ge(rope_step, n0)
                        pool.tensor_tensor(a, v, cosv.to_broadcast([P, 16, ROT]), ALU.mult)\
                            .then_inc(rope_step, 1)
                        for s in range(2):
                            pool.tensor_tensor(b4[:, :, s, :], v4[:, :, 1 - s, :], sinv, ALU.mult)\
                                .then_inc(rope_step, 1)
                        pool.wait_ge(rope_step, n0 + 3)
                        for s, op in ((0, ALU.subtract), (1, ALU.add)):
                            pool.tensor_tensor(v4[:, :, s, :], a4[:, :, s, :], b4[:, :, s, :], op)\
                                .then_inc(rope_step, 1)

                def spread(i):
                    head, dven, actn, scores, one = attention(2, l, i)
                    pool.wait_ge(cum_ready, l + 1)
                    pool.wait_ge(dve_att, dven(0))
                    h2 = bass.ds(i * 2, 2)
                    pool.tensor_tensor(nlb[:, :, :, :].rearrange("p h t n -> p (h t) n"),
                                       nlf[:, h2, :].rearrange("p h t -> p (h t)").unsqueeze(2)
                                       .to_broadcast([P, 2 * NT, P]),
                                       ones.unsqueeze(1).to_broadcast([P, 2 * NT, P]), ALU.mult)
                    pool.tensor_copy(cumq[:, :, :], cum[:, h2, :]).then_inc(fox_ready, 1)
                with pool.Fori(0, PAIRS_C - 1) as i:
                    spread(i)
                pool.wait_ge(sq_done, l * SQUARES + Q_C)
                rms(1, 1, rh[:, 0:10], ssh[:, 0:10], IW_A, rh_ready)
                spread(PAIRS_C - 1)
                pool.wait_ge(sq_done, l * SQUARES + Q_C + NT)
                rms(2, 2, rh[:, 10:12], ssh[:, 10:12], IW_C, rh_ready)
                pool.wait_ge(sq_done, l * SQUARES + Q_MEM + NT)
                rms(3, 3, rm[:, :], ssm[:, :], IW_D, rm_ready)
                for g in range(8):
                    t, k = g % 2, g // 2 * 4
                    tok = slice(t * P, (t + 1) * P)
                    pool.wait_ge(tp_high, l * GROUPS + (T_MEM + g + 1))
                    pool.tensor_tensor(memTl[:, k:k + 4, tok], R[:, t, :].rearrange("p (k n) -> p k n", k=4),
                                       memTh[:, k:k + 4, tok].bitcast(F32), ALU.subtract)\
                        .then_inc(mem_low, 1)

                rms_y(4, 4, 0)
                rms_x(6, 5, Q_X2)
                rms_y(7, 6, 1)
                rms_x(9, 7, Q_X3)
                rms_y(10, 8, 2)


_INS = ["x", "mem", "positions", "g_mix_pre", "g_mix_post", "w_in", "b_f", "lam_q1", "lam_k1", "lam_q2",
        "lam_k2", "g_diff_sub", "g_sb_out", "g_fox_out", "w_out", "g_x_pre", "g_x_post", "g_mem", "w_cq",
        "w_ckv", "w_co", "g_ffn_pre", "g_ffn_post", "w_gate", "w_up", "w_down"]


def _constants():
    q, k = np.arange(P)[:, None], np.arange(P)[None, :]
    zero = np.zeros((P, P))
    causal = np.where(q >= k, 0.0, NEG)
    strict = np.where(q > k, 0.0, NEG)
    c = np.zeros((P, C_W), np.float32)
    c[:, C_ID:C_ID + P] = np.eye(P)
    c[:, C_CAUSAL:C_CAUSAL + 3 * P] = np.concatenate([causal, zero, causal], 1)
    c[:, C_STRICT:C_STRICT + 3 * P] = np.concatenate([strict, zero, strict], 1)
    c[:, C_TRI:C_TRI + P] = q <= k
    c[:, C_ONES:C_ONES + P] = 1.0
    c[:, C_FREQ:C_FREQ + ROT] = np.float32(ROPE_THETA) ** (-np.arange(ROT, dtype=np.float32) / ROT)
    return c


def kernel(**inputs):
    import concourse.bacc as bacc
    from concourse.bass_utils import run_bass_kernel_spmd

    nc = bacc.Bacc("TRN2", target_bir_lowering=False, num_devices=1, dynamic_dma_scratch_size=1024)
    arrays, args = {}, []
    for name in _INS:
        a = np.ascontiguousarray(inputs[name])
        arrays[f"in_{name}"] = a
        args.append(nc.dram_tensor(f"in_{name}", a.shape, mybir.dt.from_np(a.dtype), kind="ExternalInput").ap())
    arrays["in_consts"] = _constants()
    args.append(nc.dram_tensor("in_consts", (P, C_W), F32, kind="ExternalInput").ap())
    args.append(nc.dram_tensor("out_x", inputs["x"].shape, F32, kind="ExternalOutput").ap())
    trunk(nc, *args)
    r = run_bass_kernel_spmd(nc, [arrays], core_ids=[0])
    return r.results[0]["out_x"]
```

```python
import math
from contextlib import ExitStack

import numpy as np

import concourse.bass as bass
from concourse import mybir

ALU = mybir.AluOpType
ACT = mybir.ActivationFunctionType
F32 = mybir.dt.float32
F32R = mybir.dt.float32r
BF16 = mybir.dt.bfloat16
I32 = mybir.dt.int32
AX_X = mybir.AxisListType.X

P = 128
NT = 2
EPS = 1e-6
NEG = -1e30
ROPE_THETA = 10000.0
N_DIFF, N_SB, N_FOX = 4, 6, 6
HD = 128
ROT = 32
PAIR_W = 3 * 2 * HD
WIDE = 1024
PAIRS_A, PAIRS_B, PAIRS_C = N_DIFF // 2, N_SB // 2, N_FOX // 2
PAIRS = PAIRS_A + PAIRS_B + PAIRS_C

ORDER = (0, 2, 1, 3)
RING = 4

C_ID, C_CAUSAL, C_STRICT, C_TRI, C_ONES, C_FREQ = 0, 128, 512, 896, 1024, 1152
C_W = C_FREQ + ROT


def trunk(nc, x, mem, positions, g_mix_pre, g_mix_post, w_in, b_f, lam_q1, lam_k1, lam_q2, lam_k2,
          g_diff_sub, g_sb_out, g_fox_out, w_out, g_x_pre, g_x_post, g_mem, w_cq, w_ckv, w_co,
          g_ffn_pre, g_ffn_post, w_gate, w_up, w_down, consts, out):
    DEPTH, D = g_mix_pre.shape
    DFF = w_gate.shape[2]
    KT = D // P
    FB = DFF // 512
    CW = w_cq.shape[2]
    NCH = CW // HD
    COK = CW // P
    lam_init = [0.8 - 0.6 * math.exp(-0.3 * n) for n in range(DEPTH)]
    G = 4 * (FB)
    assert D == 2048 and G == DFF // P and FB % 2 == 1 and CW == 512

    S_OUT = PAIRS
    S_MK, S_CQ, S_MV, S_CO = S_OUT + 2, S_OUT + 3, S_OUT + 4, S_OUT + 5
    S_FFN, S_DOWN = S_CO + 2, S_CO + 2 + FB
    SETS = S_DOWN + 2
    K_OUT = PAIRS * KT
    K_MK = K_OUT + 2 * KT
    K_CQ = K_MK + KT // 2
    K_MV = K_CQ + KT // 2
    K_CO = K_MV + KT // 2
    K_FFN = K_CO + 2 * COK
    K_DOWN = K_FFN + FB * KT
    CHUNKS = K_DOWN + 2 * G
    T_X, T_MIX, T_MEM, T_CQ, T_CO, T_FFN, GROUPS = 0, 8, 16, 24, 32, 34, 42
    G_MIX, G_X, G_FFN, G_MEM, G_MERGED, GAINS = 0, KT, 2 * KT, 3 * KT, 4 * KT, 5 * KT
    Q_X, Q_A, Q_B, Q_C, Q_OUT, Q_MEM, Q_OUT2, Q_X2, Q_CO, Q_X3, Q_DOWN, SQUARES = \
        0, 2, 10, 12, 14, 18, 20, 24, 26, 34, 36, 44

    NORMS = 12

    with ExitStack() as ctx:
        def sb(name, shape, dt=F32):
            return ctx.enter_context(nc.sbuf_tensor(name, shape, dt))

        def sem(name):
            return ctx.enter_context(nc.semaphore(name))

        cst = sb("cst", [P, C_W])
        ident = cst[:, C_ID:C_ID + P]
        causal = cst[:, C_CAUSAL:C_CAUSAL + 3 * P]
        strict = cst[:, C_STRICT:C_STRICT + 3 * P]
        tri = cst[:, C_TRI:C_TRI + P]
        ones = cst[:, C_ONES:C_ONES + P]
        freq = cst[:, C_FREQ:C_FREQ + ROT]
        xs = sb("xs", [P, NT, D])
        raw = sb("raw", [P, RING, WIDE])
        wh = sb("wh", [P, RING, WIDE], F32R)
        wl = sb("wl", [P, RING, WIDE], F32R)
        xTh = sb("xTh", [P, KT, NT * P], F32R)
        xTl = sb("xTl", [P, KT, NT * P], F32R)
        pj = sb("pj", [P, NT, PAIR_W])
        mg = sb("mg", [P, NT, D])
        mst = sb("mst", [P, NT, D])
        with ExitStack() as mixer:
            memTh = mixer.enter_context(nc.sbuf_tensor("memTh", [P, KT, NT * P], F32R))
            memTl = mixer.enter_context(nc.sbuf_tensor("memTl", [P, KT, NT * P], F32R))
            kv = mixer.enter_context(nc.sbuf_tensor("kv", [P, NT, 2 * CW], F32))
        hidT = sb("hidT", [P, G, NT * P])
        gbc = sb("gbc", [P, D])
        Z = sb("Z", [P, 2, 512])
        E = sb("E", [P, 2, 512])
        R = sb("R", [P, 2, 512])
        pT = sb("pT", [P, 2, 512])
        qkT = sb("qkT", [P, 2, 512])
        nlb = sb("nlb", [P, 2, NT, P])
        fT = Z[0:N_FOX, 0, 0:NT * P]
        junk = qkT[:, :, :].rearrange("p a n -> p (a n)").bitcast(BF16)
        gT = sb("gT", [P, DEPTH, GAINS])
        grow = sb("grow", [P, DEPTH, P])
        wfr = sb("wfr", [P, DEPTH, KT, N_FOX])
        wfh = sb("wfh", [P, KT, N_FOX], F32R)
        wfl = sb("wfl", [P, KT, N_FOX], F32R)
        bfb = sb("bfb", [P, DEPTH, N_FOX])
        fz = sb("fz", [P, NT, N_FOX])
        fe = sb("fe", [P, NT, N_FOX])
        fs = sb("fs", [P, NT, N_FOX])
        nlf = sb("nlf", [P, N_FOX, NT])
        cum = sb("cum", [P, N_FOX, NT])
        cumq = sb("cumq", [P, 2, NT])
        posi = sb("posi", [P, NT], I32)
        posf = sb("posf", [P, NT])
        trig = sb("trig", [P, 5, NT, ROT])
        cosb = sb("cosb", [P, NT, ROT])
        sinb = sb("sinb", [P, NT, ROT])
        lamr = sb("lamr", [P, 4, DEPTH * 64])
        lamp = sb("lamp", [P, 2, DEPTH * 64])
        lamd = sb("lamd", [P, 2, DEPTH])
        lame = sb("lame", [P, 2, DEPTH])
        lamn = sb("lamn", [P, DEPTH])
        nlam = sb("nlam", [P, DEPTH])
        mhalf = sb("mhalf", [P, 16])
        eps = sb("eps", [P, 16])
        inv_w = sb("inv_w", [P, 14])
        IW_D, IW_A, IW_C = 0, 2, 12
        ssy = sb("ssy", [P, NT, 4])
        ssy2 = sb("ssy2", [P, NT])
        ssx = sb("ssx", [P, NT])
        ssm = sb("ssm", [P, NT])
        ssh = sb("ssh", [P, 12])
        msx = sb("msx", [P, 9, 12])
        rx = sb("rx", [P, NT])
        rm = sb("rm", [P, NT])
        ry = sb("ry", [P, NT])
        rh = sb("rh", [P, 12])
        nmax = sb("nmax", [P, 4, NT])
        rsum = sb("rsum", [P, 4, NT])
        rinv = sb("rinv", [P, 4, NT])

        acc = ctx.enter_context(nc.psum_tensor("acc", [P, 4, 512], F32))
        aux = ctx.enter_context(nc.psum_tensor("aux", [P, 4, 512], F32))

        cst_full = sem("cst_full")
        x_full = [sem(f"x_full{n}") for n in range(4)]
        gains_full = sem("gains_full")
        wf_full = sem("wf_full")
        par_full = sem("par_full")
        raw_full = [sem(f"raw_full{s}") for s in range(RING)]
        wh_ready = sem("wh_ready")
        wl_ready = sem("wl_ready")
        w_free = sem("w_free")
        acc_done = sem("acc_done")
        acc_free = [sem(f"acc_free{b}") for b in range(4)]
        tp_done = sem("tp_done")
        tp_gain = sem("tp_gain")
        tp_high = sem("tp_high")
        xT_ready = sem("xT_ready")
        mem_full = sem("mem_full")
        gbc_full = sem("gbc_full")
        x_upd = [sem(f"x_upd{t}") for t in range(NT)]
        sq_done = sem("sq_done")
        ssy_ready = [sem(f"ssy_ready{t}") for t in range(NT)]
        ms = sem("ms")
        rx_ready = sem("rx_ready")
        rm_ready = sem("rm_ready")
        ry_ready = [sem(f"ry_ready{t}") for t in range(NT)]
        rh_ready = sem("rh_ready")
        mg_ready = sem("mg_ready")
        f_done = sem("f_done")
        f_step = sem("f_step")
        f_act = sem("f_act")
        cum_done = sem("cum_done")
        cum_ready = sem("cum_ready")
        fox_ready = sem("fox_ready")
        rope_step = sem("rope_step")
        rope_dve = sem("rope_dve")
        mem_low = sem("mem_low")
        qkT_done = sem("qkT_done")
        qkT_act = sem("qkT_act")
        qkT_dve = sem("qkT_dve")
        s_done = sem("s_done")
        dve_att = sem("dve_att")
        act_att = sem("act_att")
        pT_done = sem("pT_done")
        pT_act = sem("pT_act")
        pT_dve = sem("pT_dve")
        o_done = sem("o_done")
        o_read = sem("o_read")
        x_act = sem("x_act")
        x_dve = sem("x_dve")
        x_tp = sem("x_tp")
        x_s = sem("x_s")
        x_max = sem("x_max")
        x_exp = sem("x_exp")
        x_inv = sem("x_inv")
        x_pT = sem("x_pT")
        x_pTa = sem("x_pTa")
        x_pTd = sem("x_pTd")
        x_o = sem("x_o")
        x_or = sem("x_or")
        hT_done = sem("hT_done")
        hT_act = sem("hT_act")
        hT_dve = sem("hT_dve")
        st_high = sem("st_high")
        st_ready = sem("st_ready")
        boot = sem("boot")
        boot_pe = sem("boot_pe")
        boot_pool = sem("boot_pool")
        boot_trig = sem("boot_trig")
        sin_ready = sem("sin_ready")
        lam_step = sem("lam_step")
        lam_exp = sem("lam_exp")
        stored = sem("stored")

        TRIG_STEPS = 3 + 2 * 11
        DA, DB, DC = 24, 10, 10
        AA, AB, AC = 8, 8, 4
        DVE_ATT = PAIRS_A * DA + PAIRS_B * DB + PAIRS_C * DC
        ACT_ATT = PAIRS_A * AA + PAIRS_B * AB + PAIRS_C * AC
        MAPS = PAIRS_A * 4 + (PAIRS_B + PAIRS_C) * 2

        w_in_v = [
            w_in[:, :, 0:3 * N_DIFF * HD],
            w_in[:, :, 3 * N_DIFF * HD:3 * (N_DIFF + N_SB) * HD],
            w_in[:, :, 3 * (N_DIFF + N_SB) * HD:3 * (N_DIFF + N_SB + N_FOX) * HD],
        ]
        w_in_v = [v.rearrange("l (k p) (s c) -> l k p s c", p=P, s=3) for v in w_in_v]
        w_f_v = w_in[:, :, 3 * (N_DIFF + N_SB + N_FOX) * HD:].rearrange("l (k p) c -> p l k c", p=P)
        w_out_v = w_out.rearrange("l (k p) n -> l k p n", p=P)
        w_ckv_v = w_ckv.rearrange("l (k j p) n -> l k p j n", j=2, p=P)
        w_cq_v = w_cq.rearrange("l (k j p) n -> l k p j n", j=2, p=P)
        w_co_v = w_co.rearrange("l (k p) n -> l k p n", p=P)
        w_gate_v = w_gate.rearrange("l (k p) n -> l k p n", p=P)
        w_up_v = w_up.rearrange("l (k p) n -> l k p n", p=P)
        w_down_v = w_down.rearrange("l (k p) n -> l k p n", p=P)
        x_v = x.rearrange("b (t p) d -> p (b t) d", p=P)
        mem_v = mem.rearrange("b (t p) d -> p (b t) d", p=P)
        out_v = out.rearrange("b (t p) d -> p (b t) d", p=P)

        block = ctx.enter_context(nc.Block())

        def lows(l, n):
            return l * (GROUPS - 8) + ((n if n < T_MEM else n - 8) + 1)

        def last_chunk(s):
            if s < S_MK:
                return KT * (s + 1) - 1
            if s < S_FFN:
                return (K_CQ, K_MV, K_CO, K_CO + COK, K_FFN)[s - S_MK] - 1
            if s < S_DOWN:
                return K_FFN + (s - S_FFN + 1) * KT - 1
            return K_DOWN + (s - S_DOWN + 1) * G - 1

        def wait_acc(eng, l, sets, s, b):
            if b < 3:
                eng.wait_ge(acc_done, l * (3 * SETS) + sets * 3 + (3 * s + ORDER.index(b) + 1))
            else:
                eng.wait_ge(w_free, l * CHUNKS + sets * KT + (last_chunk(s) + 1 + RING))

        def attention(group, l, i):
            pb = (0, PAIRS_A, PAIRS_A + PAIRS_B)[group]
            dve0 = (0, PAIRS_A * DA, PAIRS_A * DA + PAIRS_B * DB)[group]
            act0 = (0, PAIRS_A * AA, PAIRS_A * AA + PAIRS_B * AB)[group]
            map0 = (0, PAIRS_A * 4, PAIRS_A * 4 + PAIRS_B * 2)[group]
            d, a, m = ((DA, AA, 4), (DB, AB, 2), (DC, AC, 2))[group]

            def head(n):
                return l * (2 * PAIRS) + i * 2 + (2 * pb + n)

            def dve(n):
                return l * DVE_ATT + i * d + (dve0 + n)

            def act(n):
                return l * ACT_ATT + i * a + (act0 + n)

            def scores(n):
                return l * MAPS + i * m + (map0 + n)

            def one(n):
                return l * PAIRS + i + (pb + n)
            return head, dve, act, scores, one

        def rope(eng, t, scratch, step, n0):
            v = pj[:, t, 0:512].rearrange("p (b n) -> p b n", n=ROT)
            v4 = pj[:, t, 0:512].rearrange("p (b s n) -> p b s n", s=2, n=ROT)
            a = scratch[:, 0, :].rearrange("p (b n) -> p b n", n=ROT)
            a4 = scratch[:, 0, :].rearrange("p (b s n) -> p b s n", s=2, n=ROT)
            b4 = scratch[:, 1, :].rearrange("p (b s n) -> p b s n", s=2, n=ROT)
            cosv = cosb[:, t, :].unsqueeze(1).to_broadcast([P, 16, ROT])
            sinv = sinb[:, t, :].unsqueeze(1).to_broadcast([P, 8, ROT])
            eng.tensor_tensor(a, v, cosv, ALU.mult).then_inc(step, 1)
            for s in range(2):
                eng.tensor_tensor(b4[:, :, s, :], v4[:, :, 1 - s, :], sinv, ALU.mult).then_inc(step, 1)
            eng.wait_ge(step, n0 + 3)
            for s, op in ((0, ALU.subtract), (1, ALU.add)):
                eng.tensor_tensor(v4[:, :, s, :], a4[:, :, s, :], b4[:, :, s, :], op).then_inc(step, 1)

        @block.sync
        def _(sp):
            sp.dma_start(cst[:, :], consts).then_inc(cst_full, 16)
            for at, g in ((G_MIX, g_mix_pre), (G_X, g_x_pre), (G_FFN, g_ffn_pre)):
                sp.dma_start(grow[at:at + KT, :, :], g.rearrange("l (k p) -> k l p", p=P))\
                  .then_inc(gains_full, 16)
            sp.dma_start(xs[:, :, 0:512], x_v[:, :, 0:512]).then_inc(x_full[0], 16)

            with sp.Fori(0, DEPTH) as l:
                def chunk(ahead, c, dsts, srcs):
                    sp.wait_ge(wl_ready, l * CHUNKS + ahead + (c + 1))
                    for d, v in zip(dsts, srcs):
                        sp.dma_start(d, v).then_inc(raw_full[c % RING], 32 // len(srcs))

                def slot(c):
                    return raw[:, c % RING, :]

                def pair_chunk(group, base, ahead, col, k):
                    chunk(ahead, base + k, [slot(k)[:, 0:PAIR_W].rearrange("p (s c) -> p s c", s=3)],
                          [w_in_v[group][l, k, :, :, bass.ds(col, 2 * HD)]])

                for k in range(KT):
                    if k == KT // 2:
                        sp.wait_ge(x_upd[1], l * 12 + 4)
                        sp.dma_start(gbc[:, :], g_mix_post[l, :].partition_broadcast(P))\
                          .then_inc(gbc_full, 16)
                    pair_chunk(0, 0, 0, 0, k)
                for group, start, n in ((0, 1, PAIRS_A), (1, 0, PAIRS_B), (2, 0, PAIRS_C)):
                    pb = (0, PAIRS_A, PAIRS_A + PAIRS_B)[group]
                    with sp.Fori(start, n) as i:
                        for k in range(KT):
                            pair_chunk(group, pb * KT, i * KT, i * (2 * HD), k)
                with sp.Fori(0, 2) as s:
                    for k in range(KT):
                        chunk(s * KT, K_OUT + k, [slot(k)], [w_out_v[l, k, :, bass.ds(s * WIDE, WIDE)]])
                for base, w, col in ((K_MK, w_ckv_v, 0), (K_CQ, w_cq_v, 0), (K_MV, w_ckv_v, CW)):
                    for k in range(KT // 2):
                        if base == K_MV and k == 0:
                            sp.wait_ge(x_upd[1], l * 12 + 8)
                            sp.dma_start(gbc[:, :], g_x_post[l, :].partition_broadcast(P))\
                              .then_inc(gbc_full, 16)
                        chunk(0, base + k, [slot(k).rearrange("p (j n) -> p j n", j=2)],
                              [w[l, k, :, :, col:col + CW]])
                for s in range(2):
                    for k in range(COK):
                        chunk(0, K_CO + s * COK + k, [slot(k)], [w_co_v[l, k, :, s * WIDE:(s + 1) * WIDE]])
                with sp.Fori(0, FB) as j:
                    for k in range(KT):
                        chunk(j * KT, K_FFN + k, [slot(k)[:, 0:512], slot(k)[:, 512:1024]],
                              [w_gate_v[l, k, :, bass.ds(j * 512, 512)],
                               w_up_v[l, k, :, bass.ds(j * 512, 512)]])
                sp.wait_ge(x_upd[1], l * 12 + 12)
                sp.dma_start(gbc[:, :], g_ffn_post[l, :].partition_broadcast(P)).then_inc(gbc_full, 16)
                for s in range(2):
                    half = slice(s * WIDE, (s + 1) * WIDE)
                    for k in range(4):
                        chunk(0, K_DOWN + s * G + k, [slot(k)], [w_down_v[l, k, :, half]])
                    with sp.Fori(0, FB // 2) as g:
                        for k in range(8):
                            chunk(g * 8, K_DOWN + s * G + 4 + k, [slot(k)],
                                  [w_down_v[l, g * 8 + (4 + k), :, half]])
            sp.wait_ge(x_upd[0], DEPTH * 12 + 4)
            sp.dma_start(out_v[:, 0, :], xs[:, 0, :]).then_inc(stored, 16)
            for b in range(4):
                sp.wait_ge(x_upd[1], DEPTH * 12 + (b + 1))
                c = slice(b * 512, (b + 1) * 512)
                sp.dma_start(out_v[:, 1, c], xs[:, 1, c]).then_inc(stored, 16)
            sp.wait_ge(stored, 16 * 5)

        N_GAINS, N_PAR = 7, 1 + 1 + 4

        @block.tensor
        def _(pe):
            pe.wait_ge(cst_full, 16)
            pe.wait_ge(gains_full, 16 * N_GAINS)
            for n in range(DEPTH):
                pe.transpose(aux[:, 4 - DEPTH + n, 0:GAINS], grow[0:GAINS, n, :], ident[0:GAINS, 0:GAINS])\
                  .then_inc(boot_pe, 1)

            with pe.Fori(0, DEPTH) as l:
                def stream(ahead, c0, set_ahead, set0, n, width, lhs, hooks=None, start=True,
                           stop=True, subs=1, before=None, early=False, late=False):
                    def products(k, t):
                        slot = (c0 + k) % RING
                        for a in range(2):
                            b = 2 * a + t
                            if start and k == 0:
                                pe.wait_ge(acc_free[b], l * SETS + set_ahead + (set0 + 1))
                            for j in range(subs):
                                hi, lo = lhs(k * subs + j)
                                cols = slice(j * 512 + a * width, j * 512 + (a + 1) * width)
                                tok = slice(t * P, (t + 1) * P)
                                o = acc[:, b, 0:width]
                                pe.matmul(o, hi[:, tok], wh[:, slot, cols],
                                          start=start and k == 0 and j == 0, stop=False)
                                pe.matmul(o, hi[:, tok], wl[:, slot, cols], start=False, stop=False)
                                mm = pe.matmul(o, lo[:, tok], wh[:, slot, cols], start=False,
                                               stop=stop and k == n - 1 and j == subs - 1)
                            if stop and k == n - 1 and b < 3:
                                mm.then_inc(acc_done, 1)
                        if t == 1:
                            mm.then_inc(w_free, 1)

                    def enter(k, t):
                        if hooks and (k, t) in hooks:
                            hooks[(k, t)]()
                        if t == 0:
                            if hooks and k in hooks:
                                hooks[k]()
                            pe.wait_ge(wl_ready, l * CHUNKS + ahead + (c0 + k + 1 + RING))
                        if before:
                            before(k, t)
                    apart = [range(0, RING)] if early else []
                    apart += [range(n - RING, n)] if late else []
                    k = 0
                    while k < n:
                        ks = next((list(a) for a in apart if k in a), [k])
                        for t in range(NT):
                            for k in ks:
                                enter(k, t)
                                products(k, t)
                        k = ks[-1] + 1
                    if hooks and n in hooks:
                        hooks[n]()

                def x_lhs(k):
                    return xTh[:, k, :], xTl[:, k, :]

                def mem_lhs(k):
                    return memTh[:, k, :], memTl[:, k, :]

                def group(n, src, ready=None, back=4):
                    if ready is not None:
                        pe.wait_ge(*ready)
                    if n >= back:
                        pe.wait_ge(tp_gain, l * GROUPS + (n - back + 1))
                    for j in range(4):
                        tr = pe.transpose(aux[:, n % 4, j * P:(j + 1) * P],
                                          src[:, j * P:(j + 1) * P], ident)
                    tr.then_inc(tp_done, 1)

                def cols(g):
                    return g % 2, slice(g // 2 * 512, (g // 2 + 1) * 512)

                def wait_x(k, t, t0, per):
                    if k % (4 // per) == 0:
                        pe.wait_ge(xT_ready, lows(l, t0 + 2 * (k * per // 4) + t))

                def x_groups(t0, lo, hi, n):
                    for g in range(lo, hi):
                        t, c = cols(g)
                        if t0 == T_X and t == 0:
                            pe.wait_ge(x_full[g // 2], 16)
                        group(t0 + g, xs[:, t, c], (x_upd[t], l * 12 + 4 * n + (g // 2 + 1)))

                def att_transpose(group_, i):
                    head, dve, act, scores, one = attention(group_, l, i)
                    if group_ == 0:
                        pe.wait_ge(rope_step, l * (5 * PAIRS_A) + i * 5 + 5)
                        pe.wait_ge(rope_dve, l * (5 * PAIRS_A) + i * 5 + 5)
                    for b in range(4):
                        pe.wait_ge(acc_free[b], l * SETS + i + ((0, PAIRS_A, PAIRS_A + PAIRS_B)[group_] + 2))
                    for h in range(2):
                        for j, (t, at) in enumerate(((0, h), (1, h), (0, 2 + h), (1, 2 + h))):
                            tr = pe.transpose(aux[:, (0, 3)[h], j * P:(j + 1) * P],
                                              pj[:, t, at * HD:(at + 1) * HD], ident)
                        tr.then_inc(qkT_done, 1)

                def att_scores(group_, i, h):
                    head, dve, act, scores, one = attention(group_, l, i)
                    pe.wait_ge((qkT_act, qkT_dve)[h], one(1))
                    if group_ == 0 and h == 1:
                        pe.wait_ge(dve_att, dve(2))
                    if group_ == 2 and h == 0:
                        pe.wait_ge(fox_ready, l * PAIRS_C + i + 1)
                    maps = 2 if group_ == 0 else 1
                    for m in range(maps):
                        rows = slice(64 * m, 64 * m + 64) if group_ == 0 else slice(0, P)
                        s = aux[:, 1 + (m if group_ == 0 else h), :]
                        q, k = qkT[rows, h, 0:256], qkT[rows, h, 256:512]
                        last = group_ != 2
                        mm = pe.matmul(s[:, 0:P], q[:, 0:P], k[:, 0:P], start=True, stop=last)
                        if not last:
                            pe.matmul(s[:, 0:P], nlb[:, h, 0, :], tri, start=False, stop=True)
                        mm = pe.matmul(s[:, P:3 * P], q[:, P:2 * P], k[:, :], start=True, stop=last)
                        if not last:
                            pe.matmul(s[:, P:2 * P], nlb[:, h, 0, :], tri, start=False, stop=False)
                            pe.matmul(s[:, 2 * P:3 * P], nlb[:, h, 0, :], ones, start=False, stop=False)
                            mm = pe.matmul(s[:, 2 * P:3 * P], nlb[:, h, 1, :], tri, start=False, stop=True)
                        mm.then_inc(s_done, 1)

                def att_weights(group_, i, h):
                    head, dve, act, scores, one = attention(group_, l, i)
                    if group_ == 0:
                        pe.wait_ge(dve_att, dve(12 * (h + 1)))
                    else:
                        pe.wait_ge(act_att, act(7 + h if group_ == 1 else 2 * h + 2))
                    src = (R if group_ == 0 else E)[:, h, :]
                    for j in range(3):
                        tr = pe.transpose(aux[:, (0, 2)[h], j * P:(j + 1) * P],
                                          src[:, j * P:(j + 1) * P], ident)
                    tr.then_inc(pT_done, 1)

                def att_values(group_, i, h):
                    head, dve, act, scores, one = attention(group_, l, i)
                    pe.wait_ge((pT_act, pT_dve)[h], one(1))
                    v = [pj[:, t, (4 + h) * HD:(5 + h) * HD] for t in range(NT)]
                    o = aux[:, 3, h * 256:(h + 1) * 256]
                    pe.matmul(o[:, 0:P], pT[:, h, 0:P], v[0], start=True, stop=True)
                    pe.matmul(o[:, P:2 * P], pT[:, h, P:2 * P], v[0], start=True, stop=False)
                    pe.matmul(o[:, P:2 * P], pT[:, h, 2 * P:3 * P], v[1], start=False, stop=True)\
                      .then_inc(o_done, 1)

                def both(f, g_, i):
                    f(g_, i, 0)
                    f(g_, i, 1)

                def att_hooks(g_, i):
                    if g_ == 0:
                        return {4: lambda: att_transpose(0, i), 6: lambda: att_scores(0, i, 0),
                                8: lambda: att_scores(0, i, 1), 10: lambda: att_weights(0, i, 0),
                                11: lambda: att_values(0, i, 0), 12: lambda: att_weights(0, i, 1),
                                13: lambda: att_values(0, i, 1)}
                    return {1: lambda: att_transpose(g_, i), 3: lambda: both(att_scores, g_, i),
                            9: lambda: both(att_weights, g_, i), 11: lambda: both(att_values, g_, i)}

                x_groups(T_X, 0, 1, 0)

                def gate():
                    pe.wait_ge(f_step, l * 6 + 1)
                    o = aux[0:N_FOX, 3, 0:NT * P]
                    for k in range(KT):
                        pe.matmul(o, wfh[:, k, :], xTh[:, k, :], start=k == 0, stop=False)
                        pe.matmul(o, wfl[:, k, :], xTh[:, k, :], start=False, stop=False)
                        mm = pe.matmul(o, wfh[:, k, :], xTl[:, k, :], start=False, stop=k == KT - 1)
                    mm.then_inc(f_done, 1)

                def gate_wait():
                    pe.wait_ge(f_step, l * 6 + 2)

                def gate_transpose():
                    for t in range(NT):
                        tr = pe.transpose(aux[:, 3, t * P:t * P + N_FOX], fT[:, t * P:(t + 1) * P],
                                          ident[0:N_FOX, 0:N_FOX])
                    tr.then_inc(f_done, 1)

                def cumulate():
                    pe.wait_ge(f_step, l * 6 + 6)
                    o = aux[:, 2, :]
                    pe.matmul(o[:, 0:N_FOX], tri, nlf[:, :, 0], start=True, stop=True)
                    pe.matmul(o[:, 8:8 + N_FOX], ones, nlf[:, :, 0], start=True, stop=False)
                    pe.matmul(o[:, 8:8 + N_FOX], tri, nlf[:, :, 1], start=False, stop=True)\
                      .then_inc(cum_done, 1)

                stream(0, 0, 0, 0, KT, 384, x_lhs, {
                    1: lambda: x_groups(T_X, 1, 2, 0), 3: lambda: x_groups(T_X, 2, 3, 0),
                    (1, 1): lambda: x_groups(T_X, 3, 4, 0), (3, 1): lambda: x_groups(T_X, 4, 6, 0),
                    5: lambda: x_groups(T_X, 6, 8, 0), 8: gate, 10: gate_wait, 11: gate_transpose, 14: cumulate,
                }, before=lambda k, t: wait_x(k, t, T_X, 1), early=True)

                for g_, n in ((0, PAIRS_A), (1, PAIRS_B), (2, PAIRS_C - 2)):
                    pb = (0, PAIRS_A, PAIRS_A + PAIRS_B)[g_]
                    with pe.Fori(0, n) as i:
                        stream(i * KT, (pb + 1) * KT, i, pb + 1, KT, 384, x_lhs, att_hooks(g_, i))

                def mix_groups(lo, hi):
                    for g in range(lo, hi):
                        t, c = cols(g)
                        group(T_MIX + g, mg[:, t, c],
                              (mg_ready, l * 5 + (1 if g < 2 else 3 if g < 4 else 5)))

                def mem_groups(lo, hi):
                    for g in range(lo, hi):
                        t, c = cols(g)
                        group(T_MEM + g, mst[:, t, c])
                hooks = att_hooks(2, PAIRS_C - 2)
                hooks[(KT - RING, 1)] = lambda: mix_groups(0, 2)
                stream(0, K_OUT - KT, 0, PAIRS - 1, KT, 384, x_lhs, hooks, late=True)

                mix_groups(2, 4)

                def last_transpose():
                    pe.wait_ge(tp_gain, l * GROUPS + (T_MIX + 4))
                    att_transpose(2, PAIRS_C - 1)
                stream(0, K_OUT, 0, S_OUT, KT, 512, x_lhs, {
                    (1, 1): last_transpose, 4: lambda: both(att_scores, 2, PAIRS_C - 1),
                    5: lambda: both(att_weights, 2, PAIRS_C - 1),
                    6: lambda: both(att_values, 2, PAIRS_C - 1), 8: lambda: mix_groups(4, 8)},
                       before=lambda k, t: wait_x(k, t, T_MIX, 1), early=True, late=True)
                pe.wait_ge(mem_full, 16)
                stream(0, K_OUT + KT, 0, S_OUT + 1, KT, 512, x_lhs,
                       {(n + 1, 1) if n < 3 else n + 1: (lambda g: lambda: mem_groups(g, g + 1))(n)
                        for n in range(8)},
                       early=True, late=True)

                pe.wait_ge(mem_low, l * 8 + 8)
                stream(0, K_MK, 0, S_MK, KT // 2, 256, mem_lhs,
                       {(0, 1): lambda: x_groups(T_CQ, 0, 2, 1),
                        4: lambda: x_groups(T_CQ, 2, 4, 1),
                        6: lambda: x_groups(T_CQ, 4, 6, 1)}, subs=2, early=True)
                stream(0, K_CQ, 0, S_CQ, KT // 2, 256, x_lhs, {1: lambda: x_groups(T_CQ, 6, 8, 1)}, subs=2,
                       before=lambda k, t: wait_x(k, t, T_CQ, 2))

                def x_transpose(p):
                    for b in range(4):
                        pe.wait_ge(acc_free[b], l * SETS + (S_CQ + 2))
                    for h in range(2):
                        at = slice((2 * p + h) * HD, (2 * p + h + 1) * HD)
                        for j, v in enumerate((pj[:, 0, at], pj[:, 1, at], kv[:, 0, at], kv[:, 1, at])):
                            tr = pe.transpose(aux[:, (0, 3)[h], j * P:(j + 1) * P], v, ident)
                        tr.then_inc(x_tp, 1)

                def x_scores(p):
                    for h in range(2):
                        pe.wait_ge((x_act, x_dve)[h], l * 2 + (p + 1))
                        if p:
                            pe.wait_ge(x_exp, l * (2 * NCH) + (2 * h + 2))
                        for t in range(NT):
                            mm = pe.matmul(aux[:, 1 + h, t * 256:(t + 1) * 256],
                                           qkT[:, h, t * P:(t + 1) * P], qkT[:, h, 256:512],
                                           start=True, stop=True)
                        mm.then_inc(x_s, 1)

                def x_weights(p):
                    for h in range(2):
                        pe.wait_ge(x_exp, l * (2 * NCH) + (4 * p + 2 * h + 2))
                        for j in range(4):
                            tr = pe.transpose(aux[:, ((0, 3) if p == 0 else (1, 2))[h], j * P:(j + 1) * P],
                                              (E if p == 0 else Z)[:, h, j * P:(j + 1) * P], ident)
                        tr.then_inc(x_pT, 1)

                def x_values(t):
                    for n in range(NCH):
                        p, h = n // 2, n % 2
                        if t == 0:
                            pe.wait_ge((x_pTa, x_pTd)[h], l * 2 + (p + 1))
                        for m in range(NT):
                            mm = pe.matmul(aux[:, 3 * t, n * HD:(n + 1) * HD],
                                           (pT if p == 0 else R)[:, h, (2 * t + m) * P:(2 * t + m + 1) * P],
                                           kv[:, m, CW + n * HD:CW + (n + 1) * HD],
                                           start=m == 0, stop=m == 1)
                    mm.then_inc(x_o, 1)
                stream(0, K_MV, 0, S_MV, KT // 2, 256, mem_lhs,
                       {1: lambda: x_transpose(0), 2: lambda: x_scores(0), 3: lambda: x_transpose(1),
                        4: lambda: x_scores(1), (4, 1): lambda: x_weights(0), (5, 1): lambda: x_weights(1)},
                       subs=2, late=True)
                for b in range(4):
                    pe.wait_ge(acc_free[b], l * SETS + (S_MV + 2))
                for t in range(NT):
                    x_values(t)
                for t in range(NT):
                    group(T_CO + t, mg[:, t, 0:CW], (x_or, l * 2 + (t + 1)))

                def co_lhs(k):
                    return xTh[:, k, :], xTl[:, k, :]
                for s in range(2):
                    stream(0, K_CO + s * COK, 0, S_CO + s, COK, 512, co_lhs,
                           before=(lambda k, t: wait_x(k, t, T_CO, 1)) if s == 0 else None,
                           hooks={(COK - 1, 1): lambda: x_groups(T_FFN, 0, 1, 2)} if s == 1 else None,
                           early=True)

                def hidden_groups(n):
                    for t in range(NT):
                        pe.wait_ge(acc_free[2 + t], n)
                        for j in range(4):
                            tr = pe.transpose(aux[:, t, j * P:(j + 1) * P],
                                              E[:, t, j * P:(j + 1) * P], ident)
                        tr.then_inc(hT_done, 1)
                stream(0, K_FFN, 0, S_FFN, KT, 512, x_lhs,
                       {3: lambda: x_groups(T_FFN, 1, 3, 2),
                        (1, 1): lambda: x_groups(T_FFN, 3, 4, 2), (3, 1): lambda: x_groups(T_FFN, 4, 6, 2),
                        5: lambda: x_groups(T_FFN, 6, 8, 2)},
                       before=lambda k, t: wait_x(k, t, T_FFN, 1), early=True, late=True)
                with pe.Fori(0, (FB - 1) // 2) as j:
                    for n in range(2):
                        stream(j * (2 * KT), K_FFN + KT + n * KT, j * 2, S_FFN + 1 + n, KT, 512, x_lhs,
                               {3: lambda: hidden_groups(l * SETS + j * 2 + (S_FFN + 2 + n))},
                               late=True)

                def stage_lhs(slot):
                    return lambda k: (xTh[:, 4 * slot + k % 4, :], xTl[:, 4 * slot + k % 4, :])
                for s in range(2):
                    base, g0 = K_DOWN + s * G, s * FB
                    pe.wait_ge(st_ready, l * (2 * FB) + g0 + 1)
                    stream(0, base, 0, S_DOWN + s, 4, 512, stage_lhs(2),
                           {(0, 1): lambda: hidden_groups(l * SETS + (S_DOWN + 1))}
                           if s == 0 else None, stop=False, early=True)

                    def two(ahead, g, c, stop):
                        for n in range(2):
                            pe.wait_ge(st_ready, l * (2 * FB) + g + (g0 + n + 1))
                            stream(ahead, c + 4 * n, 0, S_DOWN + s, 4, 512, stage_lhs(1 - n),
                                   start=False, stop=stop and n == 1, late=stop and n == 1)
                    with pe.Fori(0, FB // 2 - 1) as g:
                        two(g * 8, g * 2 + 1, base + 4, False)
                    two(0, FB - 2, base + G - 8, True)

        @block.scalar
        def _(act):
            def par(dst, src, full):
                act.dma_start(dst, src).then_inc(full, 16)
            par(grow[G_MERGED:G_MERGED + N_DIFF, :, :], g_diff_sub.partition_broadcast(N_DIFF), gains_full)
            for at, g in ((G_MEM, g_mem), (G_MERGED + N_DIFF, g_sb_out), (G_MERGED + N_DIFF + N_SB, g_fox_out)):
                k = g.shape[1] // P
                par(grow[at:at + k, :, :], g.rearrange("l (k p) -> k l p", p=P), gains_full)
            with nc.allow_non_contiguous_dma(reason="the forget gate's weights, once"):
                for n in range(DEPTH):
                    par(wfr[:, n, :, :], w_f_v[:, n, :, :], wf_full)

            with act.Fori(0, DEPTH) as l:
                def split(ahead, c, width=WIDE):
                    s = c % RING
                    act.wait_ge(raw_full[s], l * (CHUNKS // RING * 32)
                                + ahead * (32 // RING)
                                + 32 * (c // RING + 1))
                    act.wait_ge(w_free, l * CHUNKS + ahead + (c + 1))
                    act.activation(wh[:, s, 0:width], raw[:, s, 0:width], ACT.Copy).then_inc(wh_ready, 1)

                def splits(ahead, c0, n, width=WIDE, hooks=None):
                    for k in range(n):
                        if hooks and k in hooks:
                            hooks[k]()
                        split(ahead, c0 + k, width)
                    if hooks and n in hooks:
                        hooks[n]()

                def square(n, src, total, wait=None):
                    if wait is not None:
                        act.wait_ge(*wait)
                    if n:
                        act.wait_ge(sq_done, l * SQUARES + n)
                    width = src.shape[-1]
                    act.activation(junk[:, 0:width], src, ACT.Square, accum_out=total).then_inc(sq_done, 1)

                def highs(t0, lo, hi, dst=None):
                    for g in range(lo, hi):
                        t, k = g % 2, g // 2 * 4
                        act.wait_ge(tp_gain, l * GROUPS + (t0 + g + 1))
                        act.activation((xTh if dst is None else dst)[:, k:k + 4, t * P:(t + 1) * P],
                                       R[:, g % 2, :].rearrange("p (k n) -> p k n", k=4), ACT.Copy)\
                           .then_inc(tp_high, 1)

                def drain_set(set_ahead, s, scale, dst, width):
                    for b in (0, 2):
                        wait_acc(act, l, set_ahead, s, b)
                        act.activation(dst(b // 2), acc[:, b, 0:width], ACT.Copy, scale=scale[:, 0:1])\
                           .then_inc(acc_free[b], 1)

                def drain_pair(i, pb):
                    act.wait_ge(rx_ready, l * 3 + 1)
                    drain_set(i, pb, rx, lambda a: pj[:, 0, a * 384:(a + 1) * 384], 384)

                def y_squares(s, q, tiles=(0, 1)):
                    half = (s - S_OUT if s < S_MK else s - S_CO if s < S_FFN else s - S_DOWN)
                    for n, b in enumerate(ORDER):
                        if b % 2 not in tiles:
                            continue
                        wait_acc(act, l, 0, s, b)
                        at = 2 * half + b // 2
                        square(q + n, acc[:, b, :], ssy[:, b % 2, at:at + 1])

                def att_qk(g_, i):
                    head, dve, actn, scores, one = attention(g_, l, i)
                    scale = 64 ** -0.5 if g_ == 0 else HD ** -0.5
                    act.wait_ge(qkT_done, head(1))
                    act.activation(qkT[:, 0, 0:256], aux[:, 0, 0:256], ACT.Copy, scale=scale)
                    act.activation(qkT[:, 0, 256:512], aux[:, 0, 256:512], ACT.Copy).then_inc(qkT_act, 1)

                def att_exps_a(i, h):
                    head, dve, actn, scores, one = attention(0, l, i)
                    if h == 1:
                        act.wait_ge(dve_att, dve(12))
                    for m in range(2):
                        act.wait_ge(dve_att, dve(12 * h + 4 + 2 * m))
                        for t, c in enumerate((slice(0, P), slice(P, 3 * P))):
                            act.activation(E[:, m, c], Z[:, m, c], ACT.Exp,
                                           bias=nmax[:, 2 * h + m, t:t + 1],
                                           accum_out=rsum[:, 2 * h + m, t:t + 1]).then_inc(act_att, 1)

                def att_exps_c(i):
                    head, dve, actn, scores, one = attention(2, l, i)
                    for h in range(2):
                        act.wait_ge(dve_att, dve(6 + 2 * h))
                        for t, c in enumerate((slice(0, P), slice(P, 3 * P))):
                            act.activation(E[:, h, c], Z[:, h, c], ACT.Exp, bias=nmax[:, h, t:t + 1],
                                           accum_out=rsum[:, h, t:t + 1]).then_inc(act_att, 1)

                def att_log(i):
                    head, dve, actn, scores, one = attention(1, l, i)
                    steps = ((ACT.Abs, Z, 1.0, 0.0), (ACT.Exp, E, -1.0, 0.0), (ACT.Ln, E, 1.0, 1.0))
                    for n, (f, src, scale, bias) in enumerate(steps):
                        for h in range(2):
                            if n == 0:
                                act.wait_ge(dve_att, dve(h + 1))
                            else:
                                act.wait_ge(act_att, actn(2 * n - 2 + h + 1))
                            act.activation(E[:, h, 0:3 * P], src[:, h, 0:3 * P], f, bias=bias, scale=scale)\
                               .then_inc(act_att, 1)

                def att_exps_b(i):
                    head, dve, actn, scores, one = attention(1, l, i)
                    for h in range(2):
                        act.wait_ge(dve_att, dve(9 + h))
                        act.activation(E[:, h, 0:3 * P], Z[:, h, 0:3 * P], ACT.Exp).then_inc(act_att, 1)

                def att_pT(g_, i):
                    head, dve, actn, scores, one = attention(g_, l, i)
                    act.wait_ge(pT_done, head(1))
                    act.activation(pT[:, 0, 0:3 * P], aux[:, 0, 0:3 * P], ACT.Copy).then_inc(pT_act, 1)

                def att_hooks(g_, i, pb):
                    hooks = {3: lambda: drain_pair(i, pb)}
                    if g_ == 0:
                        hooks.update({7: lambda: att_qk(0, i), 10: lambda: att_exps_a(i, 0),
                                      12: lambda: att_exps_a(i, 1), 13: lambda: att_pT(0, i)})
                    elif g_ == 1:
                        hooks.update({4: lambda: att_qk(1, i), 7: lambda: att_log(i),
                                      10: lambda: att_exps_b(i), 12: lambda: att_pT(1, i)})
                    else:
                        hooks.update({4: lambda: att_qk(2, i), 7: lambda: att_exps_c(i),
                                      12: lambda: att_pT(2, i)})
                    return hooks

                def gate_log():
                    act.wait_ge(f_step, l * 6 + 4)
                    act.activation(fe[:, :, :], fz[:, :, :], ACT.Abs).then_inc(f_act, 1)
                    act.wait_ge(f_act, l * 4 + 2)
                    act.activation(fe[:, :, :], fe[:, :, :], ACT.Exp, scale=-1.0).then_inc(f_act, 1)
                    act.wait_ge(f_act, l * 4 + 3)
                    act.activation(fe[:, :, :], fe[:, :, :], ACT.Ln, bias=1.0).then_inc(f_act, 1)

                def mem_squares():
                    for t in range(NT):
                        square(Q_MEM + t, mst[:, t, :], ssm[:, t:t + 1], (mem_full, 16))

                def sines():
                    act.wait_ge(boot_trig, TRIG_STEPS)
                    act.activation(sinb[:, :, :], trig[:, 2, :, :], ACT.Sin)
                    act.activation(cosb[:, :, :], trig[:, 3, :, :], ACT.Sin).then_inc(sin_ready, 1)
                    act.wait_ge(lam_step, l * 5 + 3)
                    act.activation(lame[:, :, :], lamd[:, :, :], ACT.Exp).then_inc(lam_exp, 1)

                def gate_weights():
                    act.wait_ge(wf_full, 16 * DEPTH)
                    act.activation(wfh[:, :, :], wfr[:, bass.ds(l, 1), :, :].rearrange("p a k c -> p (a k) c"),
                                   ACT.Copy).then_inc(f_act, 1)
                highs(T_X, 0, 1)
                splits(0, 0, 3, PAIR_W)
                highs(T_X, 1, 2)
                splits(0, 3, 1, PAIR_W)
                highs(T_X, 2, 4)
                splits(0, RING, KT - RING, PAIR_W, {
                    1: lambda: highs(T_X, 4, 6), 3: lambda: highs(T_X, 6, 8), 4: gate_weights,
                    5: lambda: [square(Q_X + t, xs[:, t, :], ssx[:, t:t + 1]) for t in range(NT)],
                    6: sines, 9: gate_log})

                for g_, n in ((0, PAIRS_A), (1, PAIRS_B), (2, PAIRS_C - 2)):
                    pb = (0, PAIRS_A, PAIRS_A + PAIRS_B)[g_]
                    with act.Fori(0, n) as i:
                        splits(i * KT, (pb + 1) * KT, KT, PAIR_W, att_hooks(g_, i, pb))

                def head_squares():
                    act.wait_ge(o_read, l * (2 * PAIRS) + 2 * (PAIRS_A + PAIRS_B))
                    for t in range(NT):
                        for h in range(N_DIFF):
                            n = t * N_DIFF + h
                            square(Q_A + n, mg[:, t, h * HD:(h + 1) * HD], ssh[:, n:n + 1])
                    for t in range(NT):
                        square(Q_B + t, mg[:, t, 4 * HD:10 * HD], ssh[:, 8 + t:9 + t])

                def fox_squares():
                    act.wait_ge(o_read, (l + 1) * (2 * PAIRS))
                    for t in range(NT):
                        square(Q_C + t, mg[:, t, 10 * HD:D], ssh[:, 10 + t:11 + t])
                hooks = att_hooks(2, PAIRS_C - 2, 0)
                hooks[3] = lambda: drain_pair(0, PAIRS - 2)
                hooks[9] = head_squares
                splits(0, K_OUT - KT, KT, PAIR_W, hooks)

                def mix_first():
                    wait_acc(act, l, 0, PAIRS - 1, 2)
                    highs(T_MIX, 0, 1)
                    drain_pair(0, PAIRS - 1)

                def mix_highs():
                    wait_acc(act, l, 0, PAIRS - 1, 3)
                    highs(T_MIX, 1, 2)
                splits(0, K_OUT, KT, WIDE, {
                    0: mix_first, 3: mix_highs, 4: lambda: highs(T_MIX, 2, 4),
                    5: lambda: att_qk(2, PAIRS_C - 1), 6: lambda: att_exps_c(PAIRS_C - 1),
                    8: lambda: att_pT(2, PAIRS_C - 1), 10: fox_squares,
                    11: lambda: highs(T_MIX, 4, 6), 12: lambda: highs(T_MIX, 6, 8)})
                splits(0, K_OUT + KT, KT, WIDE, {
                    0: lambda: y_squares(S_OUT, Q_OUT, (0,)), 3: lambda: y_squares(S_OUT, Q_OUT, (1,)),
                    13: mem_squares,
                    **{5 + n: (lambda g: lambda: highs(T_MEM, g, g + 1, memTh))(n) for n in range(8)}})

                def x_squares(q, n):
                    act.wait_ge(x_upd[1], l * 12 + n)
                    for t in range(NT):
                        square(q + t, xs[:, t, :], ssx[:, t:t + 1])
                splits(0, K_MK, KT // 2, WIDE, {
                    0: lambda: y_squares(S_OUT + 1, Q_OUT2, (0,)),
                    3: lambda: y_squares(S_OUT + 1, Q_OUT2, (1,)), 4: lambda: highs(T_CQ, 0, 2),
                    6: lambda: highs(T_CQ, 2, 4), 8: lambda: highs(T_CQ, 4, 6)})

                def drain_keys():
                    act.wait_ge(rm_ready, l + 1)
                    drain_set(0, S_MK, rm, lambda a: kv[:, 0, a * 256:(a + 1) * 256], 256)

                def drain_queries():
                    act.wait_ge(rx_ready, l * 3 + 2)
                    drain_set(0, S_CQ, rx, lambda a: pj[:, 0, a * 256:(a + 1) * 256], 256)

                def drain_values():
                    drain_set(0, S_MV, rm, lambda a: kv[:, 0, CW + a * 256:CW + (a + 1) * 256], 256)

                def x_qk(p):
                    act.wait_ge(x_tp, l * NCH + (2 * p + 1))
                    act.activation(qkT[:, 0, 0:256], aux[:, 0, 0:256], ACT.Copy, scale=HD ** -0.5)
                    act.activation(qkT[:, 0, 256:512], aux[:, 0, 256:512], ACT.Copy).then_inc(x_act, 1)

                def x_exps(p):
                    for h in range(2):
                        act.wait_ge(x_max, l * NCH + (2 * p + h + 1))
                        for t in range(NT):
                            act.activation((E if p == 0 else Z)[:, h, t * 256:(t + 1) * 256],
                                           aux[:, 1 + h, t * 256:(t + 1) * 256], ACT.Exp,
                                           bias=nmax[:, 2 * p + h, t:t + 1],
                                           accum_out=rsum[:, 2 * p + h, t:t + 1]).then_inc(x_exp, 1)

                def x_pTs(p):
                    act.wait_ge(x_pT, l * NCH + (2 * p + 1))
                    act.activation((pT if p == 0 else R)[:, 0, :], aux[:, 0 if p == 0 else 1, :], ACT.Copy)\
                       .then_inc(x_pTa, 1)
                splits(0, K_CQ, KT // 2, WIDE, {3: drain_keys, 4: lambda: highs(T_CQ, 6, 8),
                                                5: lambda: x_squares(Q_X2, 8)})
                splits(0, K_MV, KT // 2, WIDE, {
                    3: drain_queries, 4: lambda: x_qk(0), 5: lambda: x_exps(0), 6: lambda: x_qk(1),
                    7: lambda: x_exps(1), 8: lambda: x_pTs(0)})
                drain_values()
                splits(0, K_CO, 1)
                x_pTs(1)
                splits(0, K_CO + 1, 3)
                for t in range(NT):
                    act.wait_ge(tp_gain, l * GROUPS + (T_CO + t + 1))
                    act.activation(xTh[:, 0:4, t * P:(t + 1) * P],
                                   R[:, t, :].rearrange("p (k n) -> p k n", k=4), ACT.Copy)\
                       .then_inc(tp_high, 1)
                y_squares(S_CO, Q_CO, (0,))
                splits(0, K_CO + 4, 3)
                y_squares(S_CO, Q_CO, (1,))
                splits(0, K_CO + 7, 1)
                y_squares(S_CO + 1, Q_CO + 4, (0,))
                splits(0, K_FFN, 2)
                highs(T_FFN, 0, 1)
                y_squares(S_CO + 1, Q_CO + 4, (1,))
                splits(0, K_FFN + 2, 2)
                highs(T_FFN, 1, 4)
                splits(0, K_FFN + RING, KT - RING, WIDE, {
                    1: lambda: highs(T_FFN, 4, 6), 3: lambda: highs(T_FFN, 6, 8),
                    6: lambda: x_squares(Q_X3, 12)})

                def silu(set_ahead, s, t):
                    act.wait_ge(rx_ready, l * 3 + 3)
                    wait_acc(act, l, set_ahead, s, t)
                    act.activation(Z[:, t, :], acc[:, t, :], ACT.Silu, scale=rx[:, t:t + 1])\
                       .then_inc(acc_free[t], 1)

                def hidden(ahead, j):
                    act.wait_ge(hT_done, l * (2 * FB) + ahead * 2 + 2 * j + 1)
                    act.activation(hidT[:, bass.ds(ahead * 4 + 4 * j, 4), 0:P],
                                   aux[:, 0, :].rearrange("p (k n) -> p k n", k=4), ACT.Copy)\
                       .then_inc(hT_act, 1)
                with act.Fori(0, FB - 1) as j:
                    splits(j * KT, K_FFN + KT, KT, WIDE,
                           {0: lambda: silu(j, S_FFN, 0), 3: lambda: silu(j, S_FFN, 1),
                            7: lambda: hidden(j, 0)})

                def stage(ahead, s, g, slot):
                    act.wait_ge(w_free, l * CHUNKS + ahead * 4 + (K_DOWN + s * G + 4 * g))
                    act.activation(xTh[:, 4 * slot:4 * slot + 4, :],
                                   hidT[:, bass.ds(ahead * 4 + 4 * g, 4), :], ACT.Copy).then_inc(st_high, 1)
                for s in range(2):
                    base = K_DOWN + s * G
                    if s == 0:
                        act.wait_ge(hT_dve, l * FB + (FB - 1))
                    if s == 0:
                        silu(0, S_FFN + FB - 1, 0)
                    else:
                        y_squares(S_DOWN, Q_DOWN, (0,))
                    stage(0, s, 0, 2)
                    splits(0, base, 3)
                    if s == 0:
                        silu(0, S_FFN + FB - 1, 1)
                    else:
                        y_squares(S_DOWN, Q_DOWN, (1,))
                    splits(0, base + 3, 1)
                    if s == 0:
                        stage(0, s, 1, 1)
                        splits(0, base + 4, 3)
                        hidden(0, FB - 1)
                        splits(0, base + 7, 1)
                        stage(0, s, 2, 0)
                        splits(0, base + 8, 4)
                        act.wait_ge(hT_dve, l * FB + FB)
                        act.wait_ge(hT_act, l * FB + FB)
                    lo = 3 if s == 0 else 1
                    with act.Fori(0, (FB - lo) // 2) as g:
                        stage(g * 2, s, lo, 1)
                        splits(g * 8, base + 4 * lo, 4)
                        stage(g * 2, s, lo + 1, 0)
                        splits(g * 8, base + 4 * lo + 4, 4)
                y_squares(S_DOWN + 1, Q_DOWN + 4)

        @block.vector
        def _(dve):
            dve.memset(fs[:, 0, 1:2], 0.0).then_inc(x_upd[0], 4)
            dve.memset(mhalf[:, :], -0.5).then_inc(wl_ready, RING)
            dve.memset(fs[:, 0, 0:1], 0.0).then_inc(w_free, RING)
            for b in range(4):
                dve.memset(fe[:, 0, b:b + 1], 0.0).then_inc(acc_free[b], 1)
            for n in range(DEPTH):
                dve.wait_ge(boot_pe, n + 1)
                dve.tensor_copy(gT[:, n, :], aux[:, 4 - DEPTH + n, 0:GAINS]).then_inc(boot, 1)
            dve.wait_ge(boot, DEPTH)
            for n in range(DEPTH):
                v = gT[:, n, G_MERGED:G_MERGED + N_DIFF]
                dve.tensor_scalar(v, v, 1.0 - lam_init[n], None, ALU.mult).then_inc(boot, 1)
            dve.wait_ge(boot, 2 * DEPTH)

            with dve.Fori(0, DEPTH) as l:
                def splits(ahead, c0, n, width=WIDE, hooks=None):
                    for k in range(n):
                        if hooks and k in hooks:
                            hooks[k]()
                        s = (c0 + k) % RING
                        dve.wait_ge(wh_ready, l * CHUNKS + ahead + (c0 + k + 1))
                        dve.tensor_tensor(wl[:, s, 0:width], raw[:, s, 0:width],
                                          wh[:, s, 0:width].bitcast(F32), ALU.subtract)\
                           .then_inc(wl_ready, 1)
                    if hooks and n in hooks:
                        hooks[n]()

                def gain(n, t, k, goff, reused=False):
                    dve.wait_ge(tp_done, l * GROUPS + (n + 1))
                    src = aux[:, n % 4, :]
                    dst = R[:, t, :]
                    if reused:
                        dve.wait_ge(xT_ready, lows(l, n - 2))
                    if goff is None:
                        dve.tensor_copy(dst, src).then_inc(tp_gain, 1)
                    else:
                        g = gT[:, bass.ds(l, 1), goff + k:goff + k + 4].rearrange("p a k -> p (a k)")
                        dve.tensor_tensor(dst.rearrange("p (k n) -> p k n", k=4),
                                          src.rearrange("p (k n) -> p k n", k=4),
                                          g.unsqueeze(2).to_broadcast([P, 4, P]), ALU.mult)\
                           .then_inc(tp_gain, 1)

                def low(n, t, k):
                    dve.wait_ge(tp_high, l * GROUPS + (n + 1))
                    tok = slice(t * P, (t + 1) * P)
                    dve.tensor_tensor(xTl[:, k:k + 4, tok], R[:, t, :].rearrange("p (k n) -> p k n", k=4),
                                      xTh[:, k:k + 4, tok].bitcast(F32), ALU.subtract)\
                       .then_inc(xT_ready, 1)

                def groups(t0, lo, hi, goff):
                    for g in range(lo, hi):
                        gain(t0 + g, g % 2, g // 2 * 4, goff, g > 1)
                        if g > lo:
                            low(t0 + g - 1, (g - 1) % 2, (g - 1) // 2 * 4)
                    low(t0 + hi - 1, (hi - 1) % 2, (hi - 1) // 2 * 4)

                def update(n, t, *blocks):
                    dve.wait_ge(ry_ready[t], l * 3 + (n + t))
                    for b in blocks:
                        if n == 0:
                            dve.wait_ge(x_full[b], 16)
                        c = slice(b * 512, (b + 1) * 512)
                        dve.scalar_tensor_tensor(xs[:, t, c], mg[:, t, c], ry[:, t:t + 1], xs[:, t, c],
                                                 ALU.mult, ALU.add).then_inc(x_upd[t], 1)

                def drain_set(set_ahead, s, scale, dst, width):
                    for b in (1, 3):
                        wait_acc(dve, l, set_ahead, s, b)
                        dve.tensor_scalar(dst(b // 2), acc[:, b, 0:width], scale[:, 1:2], None, ALU.mult)\
                           .then_inc(acc_free[b], 1)

                def drain_pair(i, pb):
                    dve.wait_ge(rx_ready, l * 3 + 1)
                    drain_set(i, pb, rx, lambda a: pj[:, 1, a * 384:(a + 1) * 384], 384)

                def drain_y(half, q, n, tiles=(0, 1)):
                    dve.wait_ge(gbc_full, l * 48 + 16 * (n + 1))
                    for at, b in enumerate(ORDER):
                        if b % 2 not in tiles:
                            continue
                        dve.wait_ge(sq_done, l * SQUARES + (q + at + 1))
                        c = slice((2 * half + b // 2) * 512, (2 * half + b // 2 + 1) * 512)
                        dve.tensor_tensor(mg[:, b % 2, c], acc[:, b, :], gbc[:, c], ALU.mult)\
                           .then_inc(acc_free[b], 1)

                def sum_y(t):
                    dve.tensor_reduce(ssy2[:, t:t + 1], ssy[:, t, :], AX_X, ALU.add).then_inc(ssy_ready[t], 1)

                def turn(t0, goff, n, c0, width):
                    if n:
                        splits(0, c0 + 2, 1, width)
                        update(n, 0, 1)
                        update(n, 1, 0)
                        splits(0, c0 + 3, 1, width)
                        gain(t0 + 1, 1, 0, goff)
                    else:
                        gain(t0, 0, 0, goff)
                        low(t0, 0, 0)
                        splits(0, c0, 1, width)
                        update(n, 1, 0)
                        splits(0, c0 + 1, 2, width)
                        gain(t0 + 1, 1, 0, goff)
                        splits(0, c0 + 3, 1, width)
                    low(t0 + 1, 1, 0)
                    update(n, 1, 1)
                    groups(t0, 2, 4, goff)
                    if n:
                        update(n, 0, 2)
                    update(n, 1, 2)

                def turn_end(t0, goff, n):
                    groups(t0, 4, 6, goff)
                    if n:
                        update(n, 0, 3)
                    update(n, 1, 3)

                def att_qk(g_, i):
                    head, dven, actn, scores, one = attention(g_, l, i)
                    scale = 64 ** -0.5 if g_ == 0 else HD ** -0.5
                    dve.wait_ge(qkT_done, head(2))
                    dve.tensor_scalar(qkT[:, 1, 0:256], aux[:, 3, 0:256], scale, None, ALU.mult)
                    dve.tensor_copy(qkT[:, 1, 256:512], aux[:, 3, 256:512]).then_inc(qkT_dve, 1)

                def neg_max(m, src):
                    dve.tensor_reduce(nmax[:, m, 0:1], src[:, 0:P], AX_X, ALU.max, negate=True)\
                       .then_inc(dve_att, 1)
                    dve.tensor_reduce(nmax[:, m, 1:2], src[:, P:3 * P], AX_X, ALU.max, negate=True)\
                       .then_inc(dve_att, 1)

                def att_max_a(i, h):
                    head, dven, actn, scores, one = attention(0, l, i)
                    for m in range(2):
                        dve.wait_ge(s_done, scores(2 * h + m + 1))
                        dve.tensor_tensor(Z[:, m, 0:3 * P], aux[:, 1 + m, 0:3 * P], causal, ALU.add)\
                           .then_inc(dve_att, 1)
                    for m in range(2):
                        dve.wait_ge(dve_att, dven(12 * h + m + 1))
                        neg_max(2 * h + m, Z[:, m, :])

                def att_mix_a(i, h):
                    head, dven, actn, scores, one = attention(0, l, i)
                    dve.wait_ge(act_att, actn(4 * h + 4))
                    dve.reciprocal(rinv[:, 2 * h:2 * h + 2, :], rsum[:, 2 * h:2 * h + 2, :])\
                       .then_inc(dve_att, 1)
                    dve.wait_ge(dve_att, dven(12 * h + 7))
                    dve.tensor_scalar(rinv[:, 2 * h + 1, :], rinv[:, 2 * h + 1, :], nlam[:, bass.ds(l, 1)],
                                      None, ALU.mult).then_inc(dve_att, 1)
                    parts = (slice(0, P), slice(P, 3 * P))
                    for t, c in enumerate(parts):
                        dve.tensor_scalar(R[:, h, c], E[:, 0, c], rinv[:, 2 * h, t:t + 1], None, ALU.mult)\
                           .then_inc(dve_att, 1)
                    dve.wait_ge(dve_att, dven(12 * h + 10))
                    for t, c in enumerate(parts):
                        dve.scalar_tensor_tensor(R[:, h, c], E[:, 1, c], rinv[:, 2 * h + 1, t:t + 1],
                                                 R[:, h, c], ALU.mult, ALU.add).then_inc(dve_att, 1)

                def att_mask_b(i):
                    head, dven, actn, scores, one = attention(1, l, i)
                    for h in range(2):
                        dve.wait_ge(s_done, scores(h + 1))
                        dve.tensor_tensor(Z[:, h, 0:3 * P], aux[:, 1 + h, 0:3 * P], strict, ALU.add)\
                           .then_inc(dve_att, 1)

                def att_sums_b(i):
                    head, dven, actn, scores, one = attention(1, l, i)
                    for h in range(2):
                        dve.wait_ge(act_att, actn(5 + h))
                        dve.scalar_tensor_tensor(E[:, h, 0:3 * P], Z[:, h, 0:3 * P], 0.0, E[:, h, 0:3 * P],
                                                 ALU.max, ALU.add).then_inc(dve_att, 1)
                    for h in range(2):
                        dve.wait_ge(dve_att, dven(3 + h))
                        for lo, hi in ((0, P), (P, 3 * P)):
                            back = E[:, h, lo:hi][:, ::-1]
                            dve.tensor_tensor_scan(R[:, h, lo:hi][:, ::-1], back, back, 0.0,
                                                   ALU.add, ALU.max).then_inc(dve_att, 1)
                    for h in range(2):
                        dve.wait_ge(dve_att, dven(6 + 2 * h))
                        dve.tensor_tensor(Z[:, h, 0:3 * P], Z[:, h, 0:3 * P], R[:, h, 0:3 * P],
                                          ALU.subtract).then_inc(dve_att, 1)

                def att_max_c(i):
                    head, dven, actn, scores, one = attention(2, l, i)
                    for h in range(2):
                        dve.wait_ge(s_done, scores(h + 1))
                        for t, c in enumerate((slice(0, P), slice(P, 3 * P))):
                            dve.scalar_tensor_tensor(Z[:, h, c], aux[:, 1 + h, c], cumq[:, h, t:t + 1],
                                                     causal[:, c], ALU.add, ALU.add).then_inc(dve_att, 1)
                    for h in range(2):
                        dve.wait_ge(dve_att, dven(2 * h + 2))
                        neg_max(h, Z[:, h, :])

                def att_inv_c(i):
                    head, dven, actn, scores, one = attention(2, l, i)
                    for h in range(2):
                        dve.wait_ge(act_att, actn(2 * h + 2))
                        dve.reciprocal(rinv[:, h, :], rsum[:, h, :]).then_inc(dve_att, 1)

                def att_pT(g_, i):
                    head, dven, actn, scores, one = attention(g_, l, i)
                    dve.wait_ge(pT_done, head(2))
                    dve.tensor_copy(pT[:, 1, 0:3 * P], aux[:, 2, 0:3 * P]).then_inc(pT_dve, 1)

                def att_out(g_, i):
                    head, dven, actn, scores, one = attention(g_, l, i)
                    col = (0, N_DIFF * HD, (N_DIFF + N_SB) * HD)[g_]
                    if g_ == 2:
                        dve.wait_ge(dve_att, dven(10))
                    dve.wait_ge(o_done, head(2))
                    for h in range(2):
                        at = bass.ds(i * (2 * HD) + (col + h * HD), HD)
                        o = aux[:, 3, h * 256:(h + 1) * 256].rearrange("p (t n) -> p t n", t=NT)
                        if g_ < 2:
                            dve.tensor_copy(mg[:, :, at], o).then_inc(o_read, 1)
                        else:
                            dve.tensor_tensor(mg[:, :, at], o, rinv[:, h, :].unsqueeze(2)
                                              .to_broadcast([P, NT, HD]), ALU.mult).then_inc(o_read, 1)

                def drain_rotate(i):
                    drain_pair(i, 0)
                    for b in (1, 3):
                        dve.wait_ge(acc_free[b], l * SETS + i + 2)
                    rope(dve, 1, E, rope_dve, l * (5 * PAIRS_A) + i * 5)

                def att_hooks(g_, i, pb):
                    hooks = {3: lambda: drain_pair(i, pb)}
                    if g_ == 0:
                        hooks.update({3: lambda: drain_rotate(i),
                                      7: lambda: att_qk(0, i), 9: lambda: att_max_a(i, 0),
                                      10: lambda: att_mix_a(i, 0), 11: lambda: att_max_a(i, 1),
                                      13: lambda: att_mix_a(i, 1), 15: lambda: att_pT(0, i),
                                      16: lambda: att_out(0, i)})
                    elif g_ == 1:
                        hooks.update({4: lambda: att_qk(1, i), 6: lambda: att_mask_b(i),
                                      9: lambda: att_sums_b(i), 12: lambda: att_pT(1, i),
                                      14: lambda: att_out(1, i)})
                    else:
                        hooks.update({4: lambda: att_qk(2, i), 6: lambda: att_max_c(i),
                                      9: lambda: att_inv_c(i), 12: lambda: att_pT(2, i),
                                      14: lambda: att_out(2, i)})
                    return hooks

                def gate_logits():
                    dve.wait_ge(f_done, l * 2 + 2)
                    dve.wait_ge(rx_ready, l * 3 + 1)
                    for t in range(NT):
                        dve.scalar_tensor_tensor(
                            fz[:, t, :], aux[:, 3, t * P:t * P + N_FOX], rx[:, t:t + 1],
                            bfb[:, bass.ds(l, 1), :].rearrange("p a c -> p (a c)"),
                            ALU.mult, ALU.add).then_inc(f_step, 1)
                    dve.wait_ge(f_step, l * 6 + 4)
                    dve.tensor_scalar(fs[:, :, :], fz[:, :, :], -1.0, 0.0, ALU.mult, ALU.max)\
                       .then_inc(f_step, 1)

                def gate_sum():
                    dve.wait_ge(f_step, l * 6 + 5)
                    dve.wait_ge(f_act, l * 4 + 4)
                    dve.tensor_tensor(nlf[:, :, :].rearrange("p c t -> p t c"), fs[:, :, :], fe[:, :, :],
                                      ALU.add).then_inc(f_step, 1)

                def gate_cum():
                    dve.wait_ge(cum_done, l + 1)
                    for t in range(NT):
                        m = dve.tensor_scalar(cum[:, :, t], aux[:, 2, t * 8:t * 8 + N_FOX], -1.0, None,
                                              ALU.mult)
                    m.then_inc(cum_ready, 1)

                def lambdas():
                    dve.wait_ge(par_full, 16 * N_PAR)
                    for n in range(2):
                        dve.tensor_tensor(lamp[:, n, :], lamr[:, 2 * n, :], lamr[:, 2 * n + 1, :], ALU.mult)\
                           .then_inc(lam_step, 1)
                    dve.wait_ge(lam_step, l * 5 + 2)
                    dve.tensor_reduce(lamd[:, :, :], lamp[:, :, :].rearrange("p n (l d) -> p (n l) d", l=DEPTH),
                                      AX_X, ALU.add).then_inc(lam_step, 1)

                def lambdas_end():
                    dve.wait_ge(lam_exp, l + 1)
                    dve.tensor_tensor(lamn[:, :], lame[:, 1, :], lame[:, 0, :], ALU.subtract)\
                       .then_inc(lam_step, 1)
                    dve.wait_ge(lam_step, l * 5 + 4)
                    for n in range(DEPTH):
                        m = dve.tensor_scalar(nlam[:, n:n + 1], lamn[:, n:n + 1], -lam_init[n], None,
                                              ALU.add)
                    m.then_inc(lam_step, 1)

                def gate_low():
                    dve.wait_ge(f_act, l * 4 + 1)
                    dve.tensor_tensor(wfl[:, :, :],
                                      wfr[:, bass.ds(l, 1), :, :].rearrange("p a k c -> p (a k) c"),
                                      wfh[:, :, :].bitcast(F32), ALU.subtract).then_inc(f_step, 1)

                def gate_out():
                    dve.wait_ge(f_done, l * 2 + 1)
                    dve.tensor_copy(fT, aux[0:N_FOX, 3, 0:NT * P]).then_inc(f_step, 1)
                turn(T_X, G_MIX, 0, 0, PAIR_W)
                splits(0, RING, KT - RING, PAIR_W, {
                    1: lambda: turn_end(T_X, G_MIX, 0), 3: lambda: groups(T_X, 6, 8, G_MIX),
                    4: gate_low, 5: lambdas, 6: lambdas_end, 7: gate_out, 8: gate_logits, 9: gate_sum,
                    12: gate_cum})

                for g_, n in ((0, PAIRS_A), (1, PAIRS_B), (2, PAIRS_C - 2)):
                    pb = (0, PAIRS_A, PAIRS_A + PAIRS_B)[g_]
                    with dve.Fori(0, n) as i:
                        splits(i * KT, (pb + 1) * KT, KT, PAIR_W, att_hooks(g_, i, pb))

                def norm_ab():
                    dve.wait_ge(rh_ready, l * 2 + 1)
                    for t in range(NT):
                        v = mg[:, t, 0:N_DIFF * HD].rearrange("p (h n) -> p h n", n=HD)
                        r = rh[:, t * N_DIFF:(t + 1) * N_DIFF].unsqueeze(2).to_broadcast([P, N_DIFF, HD])
                        m = dve.tensor_tensor(v, v, r, ALU.mult)
                    m.then_inc(mg_ready, 1)
                    for t in range(NT):
                        v = mg[:, t, 4 * HD:10 * HD]
                        dve.tensor_scalar(v, v, rh[:, 8 + t:9 + t], None, ALU.mult).then_inc(mg_ready, 1)

                def norm_c():
                    dve.wait_ge(rh_ready, l * 2 + 2)
                    for t in range(NT):
                        v = mg[:, t, 10 * HD:D]
                        dve.tensor_scalar(v, v, rh[:, 10 + t:11 + t], None, ALU.mult).then_inc(mg_ready, 1)
                hooks = att_hooks(2, PAIRS_C - 2, 0)
                hooks[3] = lambda: drain_pair(0, PAIRS - 2)
                hooks[15] = norm_ab
                splits(0, K_OUT - KT, KT, PAIR_W, hooks)

                def mix_first():
                    groups(T_MIX, 0, 1, G_MERGED)
                    gain(T_MIX + 1, 1, 0, G_MERGED)

                def mix_next():
                    low(T_MIX + 1, 1, 0)
                    drain_pair(0, PAIRS - 1)

                def mem_gain(g):
                    if g > 1:
                        dve.wait_ge(mem_low, l * 8 + g - 1)
                    gain(T_MEM + g, g % 2, g // 2 * 4, G_MEM)
                last = PAIRS_C - 1
                splits(0, K_OUT, KT, WIDE, {
                    0: mix_first, 3: mix_next, 4: lambda: groups(T_MIX, 2, 4, G_MERGED),
                    5: lambda: (att_qk(2, last), att_max_c(last)), 7: lambda: att_inv_c(last),
                    8: lambda: att_pT(2, last), 9: lambda: att_out(2, last), 10: norm_c,
                    11: lambda: groups(T_MIX, 4, 8, G_MERGED)})
                splits(0, K_OUT + KT, KT, WIDE, {
                    0: lambda: drain_y(0, Q_OUT, 0, (0,)), 3: lambda: drain_y(0, Q_OUT, 0, (1,)),
                    **{4 + n: (lambda g: lambda: mem_gain(g))(n) for n in range(8)}})

                def drain_keys():
                    dve.wait_ge(rm_ready, l + 1)
                    drain_set(0, S_MK, rm, lambda a: kv[:, 1, a * 256:(a + 1) * 256], 256)

                def drain_queries():
                    dve.wait_ge(rx_ready, l * 3 + 2)
                    drain_set(0, S_CQ, rx, lambda a: pj[:, 1, a * 256:(a + 1) * 256], 256)

                def drain_values():
                    drain_set(0, S_MV, rm, lambda a: kv[:, 1, CW + a * 256:CW + (a + 1) * 256], 256)

                def x_qk(p):
                    dve.wait_ge(x_tp, l * NCH + (2 * p + 2))
                    dve.tensor_scalar(qkT[:, 1, 0:256], aux[:, 3, 0:256], HD ** -0.5, None, ALU.mult)
                    dve.tensor_copy(qkT[:, 1, 256:512], aux[:, 3, 256:512]).then_inc(x_dve, 1)

                def x_maxs(p):
                    for h in range(2):
                        dve.wait_ge(x_s, l * NCH + (2 * p + h + 1))
                        dve.tensor_reduce(nmax[:, 2 * p + h, :],
                                          aux[:, 1 + h, :].rearrange("p (t n) -> p t n", t=NT),
                                          AX_X, ALU.max, negate=True).then_inc(x_max, 1)

                def x_pTs(p):
                    dve.wait_ge(x_pT, l * NCH + (2 * p + 2))
                    dve.tensor_copy((pT if p == 0 else R)[:, 1, :], aux[:, 3 if p == 0 else 2, :])\
                       .then_inc(x_pTd, 1)

                def x_inverse():
                    dve.wait_ge(x_exp, l * (2 * NCH) + 2 * NCH)
                    dve.reciprocal(rinv[:, :, :], rsum[:, :, :]).then_inc(x_inv, 1)

                def keys_y(t):
                    drain_y(1, Q_OUT2, 0, (t,))
                    sum_y(t)

                def x2_groups(*which):
                    for g in which:
                        if g == 0:
                            update(1, 0, 0)
                            update(1, 1, 0)
                        groups(T_CQ, g, g + 2, G_X)
                        if g < 6:
                            update(1, 0, g // 2 + 1)
                            update(1, 1, g // 2 + 1)
                splits(0, K_MK, KT // 2, WIDE, {
                    0: lambda: keys_y(0), 3: lambda: keys_y(1), 4: lambda: x2_groups(0),
                    6: lambda: x2_groups(2), 8: lambda: x2_groups(4)})
                splits(0, K_CQ, KT // 2, WIDE, {2: drain_keys, 4: lambda: x2_groups(6)})
                splits(0, K_MV, KT // 2, WIDE, {
                    3: drain_queries, 4: lambda: x_qk(0), 5: lambda: x_maxs(0), 6: lambda: x_qk(1),
                    7: lambda: x_maxs(1), 8: lambda: x_pTs(0)})
                splits(0, K_CO, 1)
                x_pTs(1)
                drain_values()
                x_inverse()
                splits(0, K_CO + 1, 1)
                dve.wait_ge(x_inv, l + 1)
                for t in range(NT):
                    dve.wait_ge(x_o, l * 2 + (t + 1))
                    dve.tensor_tensor(mg[:, t, 0:CW].rearrange("p (h n) -> p h n", h=NCH),
                                      aux[:, 3 * t, :].rearrange("p (h n) -> p h n", h=NCH),
                                      rinv[:, :, t:t + 1].to_broadcast([P, NCH, HD]), ALU.mult)\
                       .then_inc(x_or, 1)
                    if t == 0:
                        splits(0, K_CO + 2, 1)
                for t in range(NT):
                    gain(T_CO + t, t, 0, None)
                low(T_CO, 0, 0)
                splits(0, K_CO + 3, 1)
                low(T_CO + 1, 1, 0)
                drain_y(0, Q_CO, 1, (0,))
                splits(0, K_CO + 4, 3)
                drain_y(0, Q_CO, 1, (1,))
                splits(0, K_CO + 7, 1)
                drain_y(1, Q_CO + 4, 1, (0,))
                sum_y(0)
                update(2, 0, 0)
                splits(0, K_FFN, 1)
                gain(T_FFN, 0, 0, G_FFN)
                low(T_FFN, 0, 0)
                splits(0, K_FFN + 1, 1)
                drain_y(1, Q_CO + 4, 1, (1,))
                sum_y(1)
                turn(T_FFN, G_FFN, 2, K_FFN, WIDE)
                splits(0, K_FFN + RING, KT - RING, WIDE, {
                    1: lambda: turn_end(T_FFN, G_FFN, 2), 3: lambda: groups(T_FFN, 6, 8, G_FFN)})

                def product(set_ahead, s, t):
                    dve.wait_ge(rx_ready, l * 3 + 3)
                    wait_acc(dve, l, set_ahead, s, 2 + t)
                    dve.wait_ge(acc_free[t], l * SETS + set_ahead + (s + 2))
                    dve.scalar_tensor_tensor(E[:, t, :], acc[:, 2 + t, :], rx[:, t:t + 1], Z[:, t, :],
                                             ALU.mult, ALU.mult).then_inc(acc_free[2 + t], 1)

                def hidden(ahead, j):
                    dve.wait_ge(hT_done, l * (2 * FB) + ahead * 2 + 2 * j + 2)
                    dve.tensor_copy(hidT[:, bass.ds(ahead * 4 + 4 * j, 4), P:2 * P],
                                    aux[:, 1, :].rearrange("p (k n) -> p k n", k=4)).then_inc(hT_dve, 1)
                with dve.Fori(0, FB - 1) as j:
                    splits(j * KT, K_FFN + KT, KT, WIDE,
                           {0: lambda: product(j, S_FFN, 0), 3: lambda: product(j, S_FFN, 1),
                            7: lambda: hidden(j, 0)})

                def stage(ahead, s, g, slot):
                    dve.wait_ge(st_high, l * (2 * FB) + ahead + (s * FB + g + 1))
                    dve.tensor_tensor(xTl[:, 4 * slot:4 * slot + 4, :],
                                      hidT[:, bass.ds(ahead * 4 + 4 * g, 4), :],
                                      xTh[:, 4 * slot:4 * slot + 4, :].bitcast(F32), ALU.subtract)\
                       .then_inc(st_ready, 1)
                for s in range(2):
                    base = K_DOWN + s * G
                    if s == 0:
                        product(0, S_FFN + FB - 1, 0)
                    else:
                        drain_y(0, Q_DOWN, 2, (0,))
                    stage(0, s, 0, 2)
                    splits(0, base, 3)
                    if s == 0:
                        product(0, S_FFN + FB - 1, 1)
                    else:
                        drain_y(0, Q_DOWN, 2, (1,))
                    splits(0, base + 3, 1)
                    if s == 0:
                        stage(0, s, 1, 1)
                        splits(0, base + 4, 3)
                        hidden(0, FB - 1)
                        splits(0, base + 7, 1)
                        stage(0, s, 2, 0)
                        splits(0, base + 8, 4)
                    lo = 3 if s == 0 else 1
                    with dve.Fori(0, (FB - lo) // 2) as g:
                        stage(g * 2, s, lo, 1)
                        splits(g * 8, base + 4 * lo, 4)
                        stage(g * 2, s, lo + 1, 0)
                        splits(g * 8, base + 4 * lo + 4, 4)
                drain_y(1, Q_DOWN + 4, 2, (0,))
                sum_y(0)
                update(3, 0, 0, 1, 2, 3)
                drain_y(1, Q_DOWN + 4, 2, (1,))
                sum_y(1)
            dve.wait_ge(ry_ready[1], DEPTH * 3 + 1)
            for b in range(4):
                c = slice(b * 512, (b + 1) * 512)
                dve.scalar_tensor_tensor(xs[:, 1, c], mg[:, 1, c], ry[:, 1:2], xs[:, 1, c],
                                         ALU.mult, ALU.add).then_inc(x_upd[1], 1)

        @block.gpsimd
        def _(pool):
            pool.memset(eps[:, :], EPS).then_inc(boot_pool, 1)
            pool.memset(inv_w[:, IW_D:IW_A], 1.0 / D).then_inc(boot_pool, 1)
            pool.memset(inv_w[:, IW_A:IW_A + NT * N_DIFF], 1.0 / HD).then_inc(boot_pool, 1)
            pool.memset(inv_w[:, IW_A + NT * N_DIFF:IW_C], 1.0 / (N_SB * HD)).then_inc(boot_pool, 1)
            pool.memset(inv_w[:, IW_C:IW_C + NT], 1.0 / (N_FOX * HD)).then_inc(boot_pool, 1)
            pool.memset(mg[:, 1, :], 0.0).then_inc(boot_pool, 1)
            pool.wait_ge(boot_pool, 6)
            pool.memset(ry[:, 1:2], 0.0).then_inc(ry_ready[1], 1)
            def load(dst, src, full):
                pool.dma_start(dst, src).then_inc(full, 16)
            with nc.allow_non_contiguous_dma(reason="small parameters, once"):
                load(posi[:, :], positions.rearrange("b (t p) -> p (b t)", p=P), par_full)
                load(bfb[:, :, :], b_f.partition_broadcast(P), par_full)
                for n, v in enumerate((lam_q1, lam_k1, lam_q2, lam_k2)):
                    load(lamr[:, n, :], v.rearrange("l d -> (l d)").partition_broadcast(P), par_full)
            for n in range(1, 4):
                load(xs[:, :, n * 512:(n + 1) * 512], x_v[:, :, n * 512:(n + 1) * 512], x_full[n])
            load(mst[:, :, :], mem_v, mem_full)
            pool.wait_ge(wl_ready, RING)
            pool.wait_ge(cst_full, 16)
            pool.wait_ge(par_full, 16 * N_PAR)
            two_pi = 2.0 * math.pi
            c1 = 6.28125
            c2 = float(np.float32(two_pi - c1))
            c3 = two_pi - c1 - c2
            big = 12582912.0
            angle, u, w = trig[:, 0, :, :], trig[:, 1, :, :], trig[:, 4, :, :]
            pool.tensor_copy(posf[:, :], posi[:, :]).then_inc(boot_trig, 1)
            pool.wait_ge(boot_trig, 1)
            for t in range(NT):
                pool.tensor_scalar(trig[:, 0, t, :], freq, posf[:, t:t + 1], None, ALU.mult)\
                    .then_inc(boot_trig, 1)
            for which, shift in ((2, 0.0), (3, 0.25)):
                r = trig[:, which, :, :]
                n0 = 3 + 11 * (which - 2)
                pool.wait_ge(boot_trig, n0)
                pool.tensor_scalar(u, angle, 1.0 / two_pi, shift, ALU.mult, ALU.add).then_inc(boot_trig, 1)
                pool.wait_ge(boot_trig, n0 + 1)
                pool.tensor_scalar(u, u, big, None, ALU.add).then_inc(boot_trig, 1)
                pool.wait_ge(boot_trig, n0 + 2)
                pool.tensor_scalar(u, u, -big, None, ALU.add).then_inc(boot_trig, 1)
                for n, part in enumerate((c1, c2, c3)):
                    pool.wait_ge(boot_trig, n0 + 3 + 2 * n)
                    pool.tensor_scalar(w, u, -part, None, ALU.mult).then_inc(boot_trig, 1)
                    pool.wait_ge(boot_trig, n0 + 4 + 2 * n)
                    pool.tensor_tensor(r, r if n else angle, w, ALU.add).then_inc(boot_trig, 1)
                pool.wait_ge(boot_trig, n0 + 9)
                pool.tensor_scalar(r, r, two_pi * shift, None, ALU.add).then_inc(boot_trig, 1)
                pool.wait_ge(boot_trig, n0 + 10)
                pool.tensor_scalar(r, r, 3.1415925, -3.1415925, ALU.min, ALU.max).then_inc(boot_trig, 1)

            with pool.Fori(0, DEPTH) as l:
                def rms(n, row, dst, src, at, done, col=0):
                    w = src.shape[-1]
                    m = msx[:, row, col:col + w]
                    pool.tensor_tensor(m, src, inv_w[:, at:at + w], ALU.mult).then_inc(ms, 1)
                    pool.wait_ge(ms, l * (2 * NORMS) + 2 * n + 1)
                    pool.tensor_tensor(m, m, eps[:, 0:w], ALU.add).then_inc(ms, 1)
                    pool.wait_ge(ms, l * (2 * NORMS) + 2 * n + 2)
                    pool.tensor_tensor(dst, m, mhalf[:, 0:w], ALU.pow).then_inc(done, 1)

                def rms_x(n, row, q):
                    pool.wait_ge(sq_done, l * SQUARES + q + NT)
                    rms(n, row, rx[:, :], ssx[:, :], IW_D, rx_ready)

                def rms_y(n, row, k):
                    for t in range(NT):
                        pool.wait_ge(ssy_ready[t], l * 3 + k + 1)
                        rms(n + t, row, ry[:, t:t + 1], ssy2[:, t:t + 1], IW_D, ry_ready[t], t)
                rms_x(0, 0, Q_X)
                with pool.Fori(0, PAIRS_A) as i:
                    pool.wait_ge(sin_ready, l + 1)
                    for b in (0, 2):
                        pool.wait_ge(acc_free[b], l * SETS + i + 2)
                    rope(pool, 0, R, rope_step, l * (5 * PAIRS_A) + i * 5)

                def spread(i):
                    head, dven, actn, scores, one = attention(2, l, i)
                    pool.wait_ge(cum_ready, l + 1)
                    pool.wait_ge(dve_att, dven(0))
                    h2 = bass.ds(i * 2, 2)
                    pool.tensor_tensor(nlb[:, :, :, :].rearrange("p h t n -> p (h t) n"),
                                       nlf[:, h2, :].rearrange("p h t -> p (h t)").unsqueeze(2)
                                       .to_broadcast([P, 2 * NT, P]),
                                       ones.unsqueeze(1).to_broadcast([P, 2 * NT, P]), ALU.mult)
                    pool.tensor_copy(cumq[:, :, :], cum[:, h2, :]).then_inc(fox_ready, 1)
                with pool.Fori(0, PAIRS_C - 1) as i:
                    spread(i)
                pool.wait_ge(sq_done, l * SQUARES + Q_C)
                rms(1, 1, rh[:, 0:10], ssh[:, 0:10], IW_A, rh_ready)
                spread(PAIRS_C - 1)
                pool.wait_ge(sq_done, l * SQUARES + Q_C + NT)
                rms(2, 2, rh[:, 10:12], ssh[:, 10:12], IW_C, rh_ready)
                for g in range(8):
                    t, k = g % 2, g // 2 * 4
                    tok = slice(t * P, (t + 1) * P)
                    pool.wait_ge(tp_high, l * GROUPS + (T_MEM + g + 1))
                    pool.tensor_tensor(memTl[:, k:k + 4, tok], R[:, t, :].rearrange("p (k n) -> p k n", k=4),
                                       memTh[:, k:k + 4, tok].bitcast(F32), ALU.subtract)\
                        .then_inc(mem_low, 1)
                pool.wait_ge(sq_done, l * SQUARES + Q_MEM + NT)
                rms(3, 3, rm[:, :], ssm[:, :], IW_D, rm_ready)
                rms_y(4, 4, 0)
                rms_x(6, 5, Q_X2)
                rms_y(7, 6, 1)
                rms_x(9, 7, Q_X3)
                rms_y(10, 8, 2)


_INS = ["x", "mem", "positions", "g_mix_pre", "g_mix_post", "w_in", "b_f", "lam_q1", "lam_k1", "lam_q2",
        "lam_k2", "g_diff_sub", "g_sb_out", "g_fox_out", "w_out", "g_x_pre", "g_x_post", "g_mem", "w_cq",
        "w_ckv", "w_co", "g_ffn_pre", "g_ffn_post", "w_gate", "w_up", "w_down"]


def _constants():
    q, k = np.arange(P)[:, None], np.arange(P)[None, :]
    zero = np.zeros((P, P))
    causal = np.where(q >= k, 0.0, NEG)
    strict = np.where(q > k, 0.0, NEG)
    c = np.zeros((P, C_W), np.float32)
    c[:, C_ID:C_ID + P] = np.eye(P)
    c[:, C_CAUSAL:C_CAUSAL + 3 * P] = np.concatenate([causal, zero, causal], 1)
    c[:, C_STRICT:C_STRICT + 3 * P] = np.concatenate([strict, zero, strict], 1)
    c[:, C_TRI:C_TRI + P] = q <= k
    c[:, C_ONES:C_ONES + P] = 1.0
    c[:, C_FREQ:C_FREQ + ROT] = np.float32(ROPE_THETA) ** (-np.arange(ROT, dtype=np.float32) / ROT)
    return c


def kernel(**inputs):
    import concourse.bacc as bacc
    from concourse.bass_utils import run_bass_kernel_spmd

    nc = bacc.Bacc("TRN2", target_bir_lowering=False, num_devices=1, dynamic_dma_scratch_size=1024)
    arrays, args = {}, []
    for name in _INS:
        a = np.ascontiguousarray(inputs[name])
        arrays[f"in_{name}"] = a
        args.append(nc.dram_tensor(f"in_{name}", a.shape, mybir.dt.from_np(a.dtype), kind="ExternalInput").ap())
    arrays["in_consts"] = _constants()
    args.append(nc.dram_tensor("in_consts", (P, C_W), F32, kind="ExternalInput").ap())
    args.append(nc.dram_tensor("out_x", inputs["x"].shape, F32, kind="ExternalOutput").ap())
    trunk(nc, *args)
    r = run_bass_kernel_spmd(nc, [arrays], core_ids=[0])
    return r.results[0]["out_x"]
```
